# Optimizing a Trainium2 kernel written in Bass

```python
import math
import jax
import jax.numpy as jnp
from jax import lax
import numpy as np
import jax, jax.numpy as jnp

D_MODEL = 1024
BATCH = 1
SEQ = 1024
DEPTH = 1

D_MIX = D_MODEL
HEAD_DIM = 64
D_HYENA = D_MIX // 2
D_FOURIER = D_MIX - D_HYENA
N_HYENA_HEADS = D_HYENA // HEAD_DIM
N_FOURIER_GROUPS = D_FOURIER // HEAD_DIM
N_MIX_HEADS = N_HYENA_HEADS + N_FOURIER_GROUPS
D_IN_PROJ = 3 * D_HYENA + D_FOURIER
SHORT_CONV = 3
FILTER_EMB = 33
FILTER_BANDS = (FILTER_EMB - 1) // 2
FILTER_ORDER = 64
N_INNER_MLPS = 2
DECAY_FAST_PCT = 0.3
DECAY_SLOW_PCT = 1.5
DECAY_TARGET = 1e-2
N_GROUPS = 4
EXPERTS_PER_GROUP = 8
N_EXPERTS = N_GROUPS * EXPERTS_PER_GROUP
TOP_K = 2
D_EXPERT = D_MODEL // 2
MOE_BLOCK = 128
EPS = 1e-6


def rmsnorm(x, g):
    xf = x.astype(jnp.float32)
    y = xf * lax.rsqrt(jnp.mean(xf * xf, axis=-1, keepdims=True) + EPS)
    return (y * g.astype(jnp.float32)).astype(x.dtype)

def short_conv_centred(u, w, b):
    L = u.shape[1]
    half = SHORT_CONV // 2
    up = jnp.pad(u, ((0, 0), (half, half), (0, 0)))
    y = b
    for k in range(SHORT_CONV):
        y = y + up[:, k:k + L] * w[k]
    return y

def hyena_filters(L, f_w_in, f_b_in, f_w_mid, f_b_mid, f_freq, f_w_out):
    t = jnp.linspace(0.0, 1.0, L, dtype=jnp.float32)[:, None]
    w = (2.0 * math.pi / L) * jnp.arange(L, dtype=jnp.float32)[:, None]
    f = jnp.linspace(1e-4, FILTER_BANDS - 1, FILTER_BANDS, dtype=jnp.float32)[None, :]
    z = jnp.concatenate([t, jnp.cos(f * w), -jnp.sin(f * w)], axis=-1)
    h = jnp.sin(f_freq[0] * (z @ f_w_in + f_b_in))
    for i in range(N_INNER_MLPS):
        h = jnp.sin(f_freq[i + 1] * (h @ f_w_mid[i] + f_b_mid[i]))
    h = (h @ f_w_out).astype(jnp.float32).reshape(L, 2, D_HYENA)
    max_decay = math.log(DECAY_TARGET) / DECAY_FAST_PCT
    min_decay = math.log(DECAY_TARGET) / DECAY_SLOW_PCT
    deltas = jnp.abs(jnp.linspace(min_decay, max_decay, D_HYENA, dtype=jnp.float32))
    decay = jnp.exp(-t * deltas)
    h = h * decay[:, None, :]
    return h[:, 0], h[:, 1]

def bidirectional_long_conv(u, h_fwd, h_bwd):
    L = u.shape[1]
    k = jnp.concatenate([h_fwd, jnp.zeros_like(h_fwd[:1]), h_bwd[:0:-1]], axis=0)
    k = k / jnp.sum(jnp.abs(k), axis=0, keepdims=True)
    k_f = jnp.fft.rfft(k, n=2 * L, axis=0)
    u_f = jnp.fft.rfft(u, n=2 * L, axis=1)
    return jnp.fft.irfft(u_f * k_f[None], n=2 * L, axis=1)[:, :L]

def hyena_mixer(u, conv_w, conv_b, f_w_in, f_b_in, f_w_mid, f_b_mid, f_freq, f_w_out, f_bias):
    uc = short_conv_centred(u, conv_w, conv_b).astype(jnp.float32)
    x0, x1, v = jnp.split(uc, 3, axis=-1)
    h_fwd, h_bwd = hyena_filters(u.shape[1], f_w_in, f_b_in, f_w_mid, f_b_mid, f_freq, f_w_out)
    z = x1 * v
    z = bidirectional_long_conv(z, h_fwd, h_bwd) + z * f_bias.astype(jnp.float32)
    return x0 * z

def fourier_mixer(u):
    B, L, _ = u.shape
    ug = u.astype(jnp.float32).reshape(B, L, N_FOURIER_GROUPS, HEAD_DIM)
    y = jnp.fft.fftn(ug, axes=(1, 3), norm='ortho').real
    return y.reshape(B, L, D_FOURIER)

def head_rmsnorm(y, g):
    B, L, _ = y.shape
    yh = y.reshape(B, L, N_MIX_HEADS, HEAD_DIM)
    yh = yh * lax.rsqrt(jnp.mean(yh * yh, axis=-1, keepdims=True) + EPS)
    return yh.reshape(B, L, D_MIX) * g.astype(jnp.float32)

def mixer_sublayer(x, norm_g, w_in, conv_w, conv_b, f_w_in, f_b_in, f_w_mid, f_b_mid, f_freq, f_w_out,
                   f_bias, mix_g, w_out):
    h = rmsnorm(x, norm_g)
    proj = h @ w_in
    y_hyena = hyena_mixer(proj[..., :3 * D_HYENA], conv_w, conv_b, f_w_in, f_b_in, f_w_mid, f_b_mid,
                          f_freq, f_w_out, f_bias)
    y_fourier = fourier_mixer(proj[..., 3 * D_HYENA:])
    y = head_rmsnorm(jnp.concatenate([y_hyena, y_fourier], axis=-1), mix_g).astype(x.dtype)
    return x + y @ w_out

def hierarchical_moe(h, w_group, b_group, w_router, b_router, w_gate, w_up, w_down):
    B, L, D = h.shape
    T = B * L
    tok = h.reshape(T, D)
    g_logits = (tok @ w_group).astype(jnp.float32) + b_group.astype(jnp.float32)
    g_sel = jnp.argmax(g_logits, axis=-1)
    p_group = jnp.take_along_axis(jax.nn.softmax(g_logits, axis=-1), g_sel[:, None], axis=-1)[:, 0]
    e_logits = jnp.einsum('td,gde->tge', tok, w_router).astype(jnp.float32) + b_router.astype(jnp.float32)
    e_logits = jnp.take_along_axis(e_logits, g_sel[:, None, None], axis=1)[:, 0]
    top_l, top_i = lax.top_k(e_logits, TOP_K)
    weight = p_group[:, None] * jax.nn.softmax(top_l, axis=-1)
    expert = (g_sel[:, None] * EXPERTS_PER_GROUP + top_i).astype(jnp.int32)

    P = T * TOP_K
    flat_e = expert.reshape(P)
    flat_t = jnp.repeat(jnp.arange(T, dtype=jnp.int32), TOP_K)
    flat_w = weight.reshape(P)
    order = jnp.argsort(flat_e)
    se = flat_e[order]
    counts = jnp.bincount(flat_e, length=N_EXPERTS).astype(jnp.int32)
    starts = jnp.cumsum(counts) - counts
    padded = ((counts + MOE_BLOCK - 1) // MOE_BLOCK) * MOE_BLOCK
    pad_ends = jnp.cumsum(padded)
    pad_starts = pad_ends - padded
    dest = pad_starts[se] + (jnp.arange(P, dtype=jnp.int32) - starts[se])
    n_blocks = -(-P // MOE_BLOCK) + N_EXPERTS
    n_rows = n_blocks * MOE_BLOCK
    row_tok = jnp.zeros((n_rows,), jnp.int32).at[dest].set(flat_t[order])
    row_w = jnp.zeros((n_rows,), jnp.float32).at[dest].set(flat_w[order])
    block_start = jnp.arange(n_blocks, dtype=jnp.int32) * MOE_BLOCK
    block_e = jnp.minimum(jnp.searchsorted(pad_ends, block_start, side='right'), N_EXPERTS - 1)

    def expert_block(args):
        e, rows_tok, rows_w = args
        xb = tok[rows_tok]
        a = xb @ w_gate[e]
        u = xb @ w_up[e]
        y = (jax.nn.silu(a) * u) @ w_down[e]
        return (y * rows_w[:, None].astype(y.dtype)).astype(tok.dtype)

    ys = lax.map(expert_block, (block_e, row_tok.reshape(n_blocks, MOE_BLOCK), row_w.reshape(n_blocks, MOE_BLOCK)))
    out = jnp.zeros((T, D), tok.dtype).at[row_tok].add(ys.reshape(n_rows, D))
    return out.reshape(B, L, D)

def first_inputs(seed: int = 0) -> dict:
    key = jax.random.key(seed)
    ks = jax.random.split(key, 24)
    f32 = jnp.float32
    n = lambda k, shape, s: (jax.random.normal(k, shape, f32) * s)
    return {
        'x': n(ks[0], (BATCH, SEQ, D_MODEL), 1.0),
        'norm1_g': 1.0 + n(ks[1], (DEPTH, D_MODEL), 0.02),
        'w_in': n(ks[2], (DEPTH, D_MODEL, D_IN_PROJ), D_MODEL ** -0.5),
        'conv_w': n(ks[3], (DEPTH, SHORT_CONV, 3 * D_HYENA), SHORT_CONV ** -0.5),
        'conv_b': n(ks[4], (DEPTH, 3 * D_HYENA), 0.02),
        'f_w_in': n(ks[5], (DEPTH, FILTER_EMB, FILTER_ORDER), FILTER_EMB ** -0.5),
        'f_b_in': n(ks[6], (DEPTH, FILTER_ORDER), 0.1),
        'f_w_mid': n(ks[7], (DEPTH, N_INNER_MLPS, FILTER_ORDER, FILTER_ORDER), FILTER_ORDER ** -0.5),
        'f_b_mid': n(ks[8], (DEPTH, N_INNER_MLPS, FILTER_ORDER), 0.1),
        'f_freq': 1.0 + n(ks[9], (DEPTH, N_INNER_MLPS + 1, FILTER_ORDER), 0.1),
        'f_w_out': n(ks[10], (DEPTH, FILTER_ORDER, 2 * D_HYENA), FILTER_ORDER ** -0.5),
        'f_bias': n(ks[11], (DEPTH, D_HYENA), 1.0),
        'mix_g': 1.0 + n(ks[12], (DEPTH, D_MIX), 0.02),
        'w_out': n(ks[13], (DEPTH, D_MIX, D_MODEL), D_MIX ** -0.5),
        'norm2_g': 1.0 + n(ks[14], (DEPTH, D_MODEL), 0.02),
        'w_group': n(ks[15], (DEPTH, D_MODEL, N_GROUPS), D_MODEL ** -0.5),
        'b_group': n(ks[16], (DEPTH, N_GROUPS), 0.01),
        'w_router': n(ks[17], (DEPTH, N_GROUPS, D_MODEL, EXPERTS_PER_GROUP), D_MODEL ** -0.5),
        'b_router': n(ks[18], (DEPTH, N_GROUPS, EXPERTS_PER_GROUP), 0.01),
        'w_gate': n(ks[19], (DEPTH, N_EXPERTS, D_MODEL, D_EXPERT), D_MODEL ** -0.5),
        'w_up': n(ks[20], (DEPTH, N_EXPERTS, D_MODEL, D_EXPERT), D_MODEL ** -0.5),
        'w_down': n(ks[21], (DEPTH, N_EXPERTS, D_EXPERT, D_MODEL), D_EXPERT ** -0.5),
        'final_g': 1.0 + n(ks[22], (D_MODEL,), 0.02),
    }

def first_block(x, norm1_g, w_in, conv_w, conv_b, f_w_in, f_b_in, f_w_mid, f_b_mid, f_freq, f_w_out, f_bias,
              mix_g, w_out, norm2_g, w_group, b_group, w_router, b_router, w_gate, w_up, w_down, final_g):
    for i in range(DEPTH):
        x = mixer_sublayer(x, norm1_g[i], w_in[i], conv_w[i], conv_b[i], f_w_in[i], f_b_in[i], f_w_mid[i],
                           f_b_mid[i], f_freq[i], f_w_out[i], f_bias[i], mix_g[i], w_out[i])
        x = x + hierarchical_moe(rmsnorm(x, norm2_g[i]), w_group[i], b_group[i], w_router[i], b_router[i],
                                 w_gate[i], w_up[i], w_down[i])
    return rmsnorm(x, final_g)


CHUNK = 64
BAND_CHUNKS = 9
ATTN_HEADS = 8
ATTN_WIDTH = ATTN_HEADS * HEAD_DIM
POOL_WINDOWS = (2, 4, 8, 16)
POOL_GROUPS = len(POOL_WINDOWS)
POOL_WIDTH = D_MODEL // 2
POOL_GROUP_DIM = POOL_WIDTH // POOL_GROUPS
MAX_REL_DIST = 256
N_REL = 2 * MAX_REL_DIST + 1
D_FF = 2816
CONV_WIDTH = 3
N_BRANCH = 2
IN_WIDTH = 3 * ATTN_WIDTH + POOL_WIDTH + N_BRANCH * D_MODEL


def rms_norm(x, g):
    xf = x.astype(jnp.float32)
    y = xf * lax.rsqrt(jnp.mean(xf * xf, axis=-1, keepdims=True) + EPS)
    return (y * g.astype(jnp.float32)).astype(x.dtype)

def chunk_band_attention(q, k, v, rel_bias):
    b, s, h, dh = q.shape
    n_chunks = s // CHUNK
    band = BAND_CHUNKS * CHUNK
    lead = (BAND_CHUNKS - 1) * CHUNK
    pad = ((0, 0), (lead, 0), (0, 0), (0, 0))
    k_pad = jnp.pad(k, pad)
    v_pad = jnp.pad(v, pad)
    dist = jnp.arange(CHUNK)[:, None] + lead - jnp.arange(band)[None, :]
    idx = jnp.clip(dist, -MAX_REL_DIST, MAX_REL_DIST) + MAX_REL_DIST
    bias = rel_bias.astype(jnp.float32)[:, idx]
    scale = HEAD_DIM ** -0.5
    key_offsets = jnp.arange(band)

    def one_chunk(c):
        start = c * CHUNK
        q_c = lax.dynamic_slice_in_dim(q, start, CHUNK, axis=1)
        k_c = lax.dynamic_slice_in_dim(k_pad, start, band, axis=1)
        v_c = lax.dynamic_slice_in_dim(v_pad, start, band, axis=1)
        sc = jnp.einsum('bqhd,bkhd->bhqk', q_c, k_c,
                        preferred_element_type=jnp.float32) * scale + bias
        valid = (start - lead + key_offsets) >= 0
        sc = jnp.where(valid[None, None, None, :], sc, -1e30)
        p = jax.nn.softmax(sc, axis=-1).astype(v.dtype)
        return jnp.einsum('bhqk,bkhd->bqhd', p, v_c)

    out = lax.map(one_chunk, jnp.arange(n_chunks))
    return jnp.moveaxis(out, 0, 1).reshape(b, s, h * dh)

def multiscale_pool(u, w_group, scale):
    b, s, c = u.shape
    uf = u.astype(jnp.float32)
    max_w = max(POOL_WINDOWS)
    cs = jnp.pad(jnp.cumsum(uf, axis=1), ((0, 0), (max_w, 0), (0, 0)))
    t = jnp.arange(s)
    outs = []
    for g, w in enumerate(POOL_WINDOWS):
        sl = slice(g * POOL_GROUP_DIM, (g + 1) * POOL_GROUP_DIM)
        win = cs[:, max_w:, sl] - cs[:, max_w - w:max_w - w + s, sl]
        cnt = jnp.minimum(t + 1, w).astype(jnp.float32)[None, :, None]
        outs.append(win / cnt - uf[:, :, sl])
    pooled = jnp.stack(outs, axis=2).astype(u.dtype)
    mixed = jnp.einsum('bsgc,gcd->bsgd', pooled, w_group).reshape(b, s, c)
    return mixed * scale

def conv_gated_ffn(x, w_up, conv_w, conv_b, w_down):
    hu = x @ w_up
    s = hu.shape[1]
    hp = jnp.pad(hu, ((0, 0), (CONV_WIDTH - 1, 0), (0, 0)))
    hc = conv_b + conv_w[CONV_WIDTH - 1] * hu
    for i in range(CONV_WIDTH - 1):
        hc = hc + conv_w[i] * hp[:, i:i + s]
    val, gate = jnp.split(hc, 2, axis=-1)
    return (jax.nn.gelu(gate, approximate=True) * val) @ w_down

def second_inputs(seed: int = 0) -> dict:
    key = jax.random.key(seed)
    ks = jax.random.split(key, 20)
    f32 = jnp.float32

    def nrm(k, shape, s):
        return jax.random.normal(k, shape, f32) * s

    return {
        "x": jax.random.normal(ks[0], (BATCH, SEQ, D_MODEL), f32),
        "norm_mix_pre": 1.0 + nrm(ks[1], (DEPTH, D_MODEL), 0.05),
        "w_in": nrm(ks[2], (DEPTH, D_MODEL, IN_WIDTH), D_MODEL ** -0.5),
        "b_gate": nrm(ks[3], (DEPTH, N_BRANCH * D_MODEL), 0.01),
        "rel_bias": nrm(ks[4], (DEPTH, ATTN_HEADS, N_REL), 0.1),
        "w_attn_out": nrm(ks[5], (DEPTH, ATTN_WIDTH, D_MODEL), ATTN_WIDTH ** -0.5),
        "w_pool_group": nrm(ks[6], (DEPTH, POOL_GROUPS, POOL_GROUP_DIM, POOL_GROUP_DIM), POOL_GROUP_DIM ** -0.5),
        "pool_scale": 1.0 + nrm(ks[7], (DEPTH, POOL_WIDTH), 0.1),
        "w_pool_out": nrm(ks[8], (DEPTH, POOL_WIDTH, D_MODEL), POOL_WIDTH ** -0.5),
        "w_o": nrm(ks[9], (DEPTH, D_MODEL, D_MODEL), D_MODEL ** -0.5),
        "norm_mix_post": 1.0 + nrm(ks[10], (DEPTH, D_MODEL), 0.05),
        "norm_ffn_pre": 1.0 + nrm(ks[11], (DEPTH, D_MODEL), 0.05),
        "w_up": nrm(ks[12], (DEPTH, D_MODEL, 2 * D_FF), D_MODEL ** -0.5),
        "conv_w": nrm(ks[13], (DEPTH, CONV_WIDTH, 2 * D_FF), CONV_WIDTH ** -0.5),
        "conv_b": nrm(ks[14], (DEPTH, 2 * D_FF), 0.01),
        "w_down": nrm(ks[15], (DEPTH, D_FF, D_MODEL), D_FF ** -0.5),
        "norm_ffn_post": 1.0 + nrm(ks[16], (DEPTH, D_MODEL), 0.05),
    }

def second_block(x, norm_mix_pre, w_in, b_gate, rel_bias, w_attn_out, w_pool_group, pool_scale,
              w_pool_out, w_o, norm_mix_post, norm_ffn_pre, w_up, conv_w, conv_b, w_down,
              norm_ffn_post):
    b, s, _ = x.shape
    splits = [ATTN_WIDTH, 2 * ATTN_WIDTH, 3 * ATTN_WIDTH, 3 * ATTN_WIDTH + POOL_WIDTH]
    for l in range(DEPTH):
        h = rms_norm(x, norm_mix_pre[l])
        proj = h @ w_in[l]
        q, k, v, u, gates = jnp.split(proj, splits, axis=-1)
        q = q.reshape(b, s, ATTN_HEADS, HEAD_DIM)
        k = k.reshape(b, s, ATTN_HEADS, HEAD_DIM)
        v = v.reshape(b, s, ATTN_HEADS, HEAD_DIM)
        y_a = chunk_band_attention(q, k, v, rel_bias[l]) @ w_attn_out[l]
        y_b = multiscale_pool(u, w_pool_group[l], pool_scale[l]) @ w_pool_out[l]
        g_a, g_b = jnp.split(jax.nn.sigmoid(gates + b_gate[l]), N_BRANCH, axis=-1)
        mix = (g_a * y_a + g_b * y_b) @ w_o[l]
        x = x + rms_norm(mix, norm_mix_post[l])
        f = conv_gated_ffn(rms_norm(x, norm_ffn_pre[l]), w_up[l], conv_w[l], conv_b[l], w_down[l])
        x = x + rms_norm(f, norm_ffn_post[l])
    return x


def setup_inputs(seed=0):
    out = dict(first_inputs(seed))
    for name, value in second_inputs(seed + 1).items():
        if name != "x":
            out[name + "_2"] = value
    return out


def reference(
    x, norm1_g, w_in, conv_w, conv_b, f_w_in, f_b_in, f_w_mid, f_b_mid, f_freq, f_w_out, f_bias,
    mix_g, w_out, norm2_g, w_group, b_group, w_router, b_router, w_gate, w_up, w_down, final_g,
    norm_mix_pre_2, w_in_2, b_gate_2, rel_bias_2, w_attn_out_2, w_pool_group_2, pool_scale_2,
    w_pool_out_2, w_o_2, norm_mix_post_2, norm_ffn_pre_2, w_up_2, conv_w_2, conv_b_2, w_down_2,
    norm_ffn_post_2,
):
    x = first_block(
        x, norm1_g, w_in, conv_w, conv_b, f_w_in, f_b_in, f_w_mid, f_b_mid, f_freq, f_w_out,
        f_bias, mix_g, w_out, norm2_g, w_group, b_group, w_router, b_router, w_gate, w_up,
        w_down, final_g,
    )
    return second_block(
        x, norm_mix_pre_2, w_in_2, b_gate_2, rel_bias_2, w_attn_out_2, w_pool_group_2,
        pool_scale_2, w_pool_out_2, w_o_2, norm_mix_post_2, norm_ffn_pre_2, w_up_2, conv_w_2,
        conv_b_2, w_down_2, norm_ffn_post_2,
    )


_drawn_inputs = setup_inputs


def setup_inputs(seed=0):
    import zlib

    import numpy as np

    out = dict(_drawn_inputs(seed))
    spreads = {}
    factors = {'f_b_in': 3.695,
     'f_freq': 3.945,
     'b_group': 5.377,
     'b_router': 4.203,
     'b_gate_2': 8.0,
     'rel_bias_2': 6.346,
     'conv_b_2': 6.838}
    for name, (base, spread) in spreads.items():
        noise = np.random.default_rng([zlib.crc32(name.encode()), seed]).standard_normal(out[name].shape)
        drawn = base * np.exp(spread * noise) if base else spread * noise
        out[name] = jnp.asarray(drawn.astype(out[name].dtype))
    for name, factor in factors.items():
        out[name] = (out[name] * factor).astype(out[name].dtype)
    return out
```

```python
from contextlib import ExitStack, contextmanager

import numpy as np

import concourse.bass as bass
from concourse import mybir

ALU = mybir.AluOpType
ACT = mybir.ActivationFunctionType
AX_X = mybir.AxisListType.X
F32 = mybir.dt.float32
I32 = mybir.dt.int32

P = 128
SEQ = 1024
D = 1024
TT = SEQ // P
KT = D // P
BANK = 512
EPS = 1e-6

D_HYENA = 512
HT = D_HYENA // P
HEAD = 64
F_EMB = 33
F_BANDS = (F_EMB - 1) // 2
F_ORDER = 64
HALF = SEQ // 2
JT = HALF // P
TWO_PI = 2.0 * np.pi

GROUPS = 4
PER_GROUP = 8
EXPERTS = GROUPS * PER_GROUP
D_EXPERT = 512
CAP = 96
OVER = 2 * SEQ // (CAP + 1)
FULL_BLOCKS = (SEQ + CAP - 1) // CAP
BLOCKS = EXPERTS + OVER
ROWS = BLOCKS * CAP

HEADS = 8
ATT = HEADS * HEAD
CHUNK = 64
BAND = 9 * CHUNK
KEYS = BAND + CHUNK
KEY_TILES = KEYS // P
REL = 256
EXT = P + KEYS - 1
WINDOWS = (2, 4, 8, 16)
D_FF = 2816
FT = D_FF // P
NEG = -1e30
ROUND = 1.5 * 2.0 ** 23
TWO_PI_HIGH = 6.28125
TWO_PI_LOW = TWO_PI - TWO_PI_HIGH
PI_BELOW = 3.1415925

COLS = {}
_at = 0
for _name, _n in (("norm1_g", KT), ("conv_w", 3 * 3 * HT), ("conv_b", 3 * HT), ("f_bias", HT), ("mix_g", KT),
                  ("norm_mix_pre_2", KT), ("b_gate_2", 2 * KT), ("pool_scale_2", HT), ("norm_ffn_pre_2", KT),
                  ("conv_w_2", 3 * 2 * FT), ("conv_b_2", 2 * FT), ("f_b", 3), ("f_freq", 3)):
    COLS[_name] = (_at, _n)
    _at += _n
N_COLS = _at


def col(params, name, i, rows=P):
    at, n = COLS[name]
    assert 0 <= i < n
    return params[0:rows, at + i:at + i + 1]


class Steps:

    def __init__(self, sem):
        self.sem = sem
        self.n = 0

    def end(self, instruction):
        self.n += 1
        instruction.then_inc(self.sem, 1)

    def wait(self, engine):
        engine.wait_ge(self.sem, self.n)


def filter_spectrum(nc, m, A):
    with ExitStack() as mem:
        def sb(name, shape, dt=F32):
            return mem.enter_context(nc.sbuf_tensor(name, shape, dt))

        sem = m.sem
        pos = sb("pos", [F_EMB, SEQ])
        f_w_in = sb("f_w_in", [F_EMB, F_ORDER])
        f_w_mid = sb("f_w_mid", [F_ORDER, 2, F_ORDER])
        f_w_out = sb("f_w_out", [F_ORDER, 2 * D_HYENA])
        arg = sb("arg", [F_ORDER, SEQ])
        turns = sb("turns", [F_ORDER, SEQ])
        hid = sb("hid", [F_ORDER, 2, SEQ])
        decay = sb("decay", [P, 2 * JT, D_HYENA])
        lag_sum = sb("lag_sum", [P, 2, JT, D_HYENA])
        lag_dif = sb("lag_dif", [P, 2, JT, D_HYENA])
        taps = sb("taps", [P, 2, 2, D_HYENA])
        sizes = sb("sizes", [P, 2, 2, D_HYENA])
        size = sb("size", [P, D_HYENA])
        table = sb("filter_table", [P, 4, HALF])
        even_part = sb("even_part", [P, JT, BANK])
        ps = mem.enter_context(nc.psum_tensor("filter_ps", [P, 8, BANK], F32))

        w_in = sem("filter_weights_in")
        decay_in = sem("decay_in")
        tab_in = [sem(f"filter_table_in{i}") for i in range(4)]
        tab_used = sem("filter_table_used")
        mlp_mm = sem("mlp_mm")
        mlp_arg = sem("mlp_arg")
        mlp_act = sem("mlp_act")
        taps_mm = sem("taps_mm")
        taps_read = sem("taps_read")
        taps_set = sem("taps_set")
        lags_done = sem("lags_done")
        abs_done = sem("abs_done")
        size_step = sem("size_step")
        norm_mm = sem("norm_mm")
        norm_done = sem("norm_done")
        even_kept = sem("even_kept")
        spec_done = sem("spec_done")
        steps = Steps(sem("filter_steps"))
        block = mem.enter_context(nc.Block())

        @block.sync
        def _(sp):
            sp.dma_start(pos[:], A["positions"]).then_inc(w_in, 16)
            sp.dma_start(f_w_in[:], A["f_w_in"][0]).then_inc(w_in, 16)
            sp.dma_start(f_w_mid[:], A["f_w_mid"][0].rearrange("l k n -> k l n")).then_inc(w_in, 16)
            sp.dma_start(m.params[:], A["params"]).then_inc(w_in, 16)
            sp.dma_start(f_w_out[:], A["f_w_out"][0]).then_inc(w_in, 16)
            sp.dma_start(decay[:], A["decay"].rearrange("(n p) c -> p n c", p=P)).then_inc(decay_in, 16)
            for n in range(4 * JT):
                if n >= 4:
                    sp.wait_ge(tab_used, n - 3)
                sp.dma_start(table[:, n % 4, :], A["half_tables"][n // JT, (n % JT) * P:(n % JT + 1) * P, :]) \
                    .then_inc(tab_in[n % 4], 16)
                if n == 3:
                    for t in range(TT):
                        sp.dma_start(m.res[:, t, :], A["x"][0, t * P:(t + 1) * P, :]).then_inc(m.x_in, 16)

        @block.gpsimd
        def _(pool):
            nc.gpsimd.memset(m.ident[:], 0.0).then_inc(m.consts_set, 1)
            nc.gpsimd.memset(m.ones[:], 1.0).then_inc(m.consts_set, 1)
            pool.wait_ge(m.consts_set, 2)
            nc.gpsimd.affine_select(out=m.ident[:], in_=m.ident[:], compare_op=ALU.not_equal, fill=1.0, base=0,
                                    pattern=[[-1, P]], channel_multiplier=1).then_inc(m.consts_set, 1)
            nc.gpsimd.memset(size[:], 0.0).then_inc(size_step, 1)
            for n in range(2 * JT):
                pool.wait_ge(abs_done, n + 1)
                for way in range(2):
                    pool.wait_ge(size_step, 2 * n + way + 1)
                    nc.gpsimd.tensor_tensor(size[:], size[:], sizes[:, n % 2, way, :], ALU.add).then_inc(size_step, 1)

        @block.tensor
        def _(pe):
            pe.wait_ge(w_in, 80)
            for layer in range(3):
                if layer:
                    pe.wait_ge(mlp_act, layer)
                for n in range(2):
                    if layer == 0:
                        w, data = f_w_in[:], pos[:, n * BANK:(n + 1) * BANK]
                    else:
                        w, data = f_w_mid[:, layer - 1, :], hid[:, (layer - 1) % 2, n * BANK:(n + 1) * BANK]
                    last = nc.tensor.matmul(ps[0:F_ORDER, n, :], w, data, start=True, stop=True)
                last.then_inc(mlp_mm, 1)
            pe.wait_ge(mlp_act, 3)
            for n in range(2 * JT):
                par, a = n // JT, n % JT
                if n >= 2:
                    pe.wait_ge(taps_read, n - 1)
                for way in range(2):
                    last = nc.tensor.matmul(ps[:, 2 + 2 * (n % 2) + way, :],
                                            hid[:, 0, 2 * P * a + par:2 * P * (a + 1):2],
                                            f_w_out[:, way * BANK:(way + 1) * BANK], start=True, stop=True)
                last.then_inc(taps_mm, 1)
            pe.wait_ge(size_step, 2 * 2 * JT + 1)
            pe.wait_ge(m.consts_set, 3)
            for c in range(HT):
                last = nc.tensor.matmul(ps[:, 6, c:c + 1], size[:, c * P:(c + 1) * P], m.ones[:, 0:1],
                                        start=True, stop=True)
            last.then_inc(norm_mm, 1)
            pe.wait_ge(lags_done, 2 * JT)
            pe.wait_ge(norm_done, 1)
            for g in range(4):
                if g >= 2:
                    pe.wait_ge(spec_done if g % 2 else even_kept, 1)
                data = lag_sum if g < 2 else lag_dif
                for a in range(JT):
                    n = g * JT + a
                    pe.wait_ge(tab_in[n % 4], 16 * (n // 4 + 1))
                    for f in range(JT):
                        last = nc.tensor.matmul(ps[:, 4 * (g % 2) + f, :], table[:, n % 4, f * P:(f + 1) * P],
                                                data[:, g % 2, a, :], start=(a == 0), stop=(a == JT - 1))
                    last.then_inc(tab_used, 1)

        @block.scalar
        def _(act):
            for layer in range(3):
                act.wait_ge(mlp_arg, layer + 1)
                nc.scalar.activation(hid[:, layer % 2, :], arg[:], ACT.Sin).then_inc(mlp_act, 1)
            for n in range(2 * JT):
                act.wait_ge(taps_set, n + 1)
                if n >= 2:
                    act.wait_ge(size_step, 2 * (n - 1) + 1)
                nc.scalar.activation(sizes[:, n % 2, :, :], taps[:, n % 2, :, :], ACT.Abs).then_inc(abs_done, 1)
            for g in (0, 2):
                act.wait_ge(tab_used, (g + 1) * JT)
                if g:
                    act.wait_ge(spec_done, 1)
                nc.scalar.activation(even_part[:], ps[:, 0:4, :], ACT.Copy).then_inc(even_kept, 1)

        @block.vector
        def _(dve):
            nc.vector.memset(m.eps[:], EPS).then_inc(m.eps_set, 1)
            for layer in range(3):
                dve.wait_ge(mlp_mm, layer + 1)
                if layer == 0:
                    dve.wait_ge(w_in, 80)
                else:
                    dve.wait_ge(mlp_act, layer)
                steps.end(nc.vector.tensor_scalar(arg[:].rearrange("p (n c) -> p n c", n=2), ps[0:F_ORDER, 0:2, :],
                                                  col(m.params, "f_b", layer, F_ORDER),
                                                  col(m.params, "f_freq", layer, F_ORDER), ALU.add, ALU.mult))
                steps.wait(dve)
                steps.end(nc.vector.tensor_scalar(turns[:], arg[:], 1.0 / TWO_PI, ROUND, ALU.mult, ALU.add))
                steps.wait(dve)
                steps.end(nc.vector.tensor_scalar(turns[:], turns[:], -ROUND, None, ALU.add))
                for part in (TWO_PI_HIGH, TWO_PI_LOW):
                    steps.wait(dve)
                    steps.end(nc.vector.scalar_tensor_tensor(out=arg[:], in0=turns[:], scalar=-part, in1=arg[:],
                                                             op0=ALU.mult, op1=ALU.add))
                steps.wait(dve)
                nc.vector.tensor_scalar(arg[:], arg[:], PI_BELOW, -PI_BELOW, ALU.min, ALU.max).then_inc(mlp_arg, 1)
            dve.wait_ge(decay_in, 16)
            for n in range(2 * JT):
                par, a = n // JT, n % JT
                dve.wait_ge(taps_mm, n + 1)
                if n >= 2:
                    dve.wait_ge(abs_done, n - 1)
                for way in range(2):
                    last = nc.vector.tensor_tensor(taps[:, n % 2, way, :], ps[:, 2 + 2 * (n % 2) + way, :],
                                                   decay[:, n, :], ALU.mult)
                last.then_inc(taps_read, 1)
                dve.wait_ge(taps_read, n + 1)
                if n == 0:
                    steps.end(nc.vector.memset(taps[0:1, 0, 1, :], 0.0))
                    steps.wait(dve)
                nc.vector.tensor_tensor(lag_sum[:, par, a, :], taps[:, n % 2, 0, :], taps[:, n % 2, 1, :], ALU.add).then_inc(taps_set, 1)
                nc.vector.tensor_tensor(lag_dif[:, par, a, :], taps[:, n % 2, 0, :], taps[:, n % 2, 1, :],
                                        ALU.subtract).then_inc(lags_done, 1)
            dve.wait_ge(norm_mm, 1)
            nc.vector.reciprocal(m.inv_size[:], ps[:, 6, 0:HT]).then_inc(norm_done, 1)
            for trig in range(2):
                dve.wait_ge(even_kept, trig + 1)
                dve.wait_ge(tab_used, (2 * trig + 2) * JT)
                nc.vector.tensor_tensor(m.K[:, trig, 0, :, :], even_part[:], ps[:, 4:8, :], ALU.add)
                nc.vector.tensor_tensor(m.K[:, trig, 1, :, :], even_part[:], ps[:, 4:8, :], ALU.subtract) \
                    .then_inc(spec_done, 1)


def norm_to_T(nc, m, name, hT, gamma=None, gamma_row=None, rows_out=None, x_ready=None):
    with ExitStack() as mem:
        def sb(part, shape, dt=F32):
            return mem.enter_context(nc.sbuf_tensor(f"{name}_{part}", shape, dt))

        def sem(part):
            return m.sem(f"{name}_{part}")

        squares = sb("squares", [P, D])
        sums = sb("sums", [P, TT])
        rms = sb("rms", [P, TT])
        rstd = sb("rstd", [P, TT])
        scaled = sb("scaled", [P, 2, D])
        ps = mem.enter_context(nc.psum_tensor(f"{name}_ps", [P, 4, 4, P], F32))
        summed = sem("summed")
        rms_done = sem("rms_done")
        rstd_done = sem("rstd_done")
        scaled_done = sem("scaled_done")
        turned = sem("turned")
        out_done = sem("out_done")
        if gamma_row is not None:
            g_row = sb("gamma_row", [P, D])
            g_in = sem("gamma_in")
            stored = [sem(f"stored{i}") for i in range(2)]
        block = mem.enter_context(nc.Block())

        @block.scalar
        def _(act):
            act.wait_ge(m.eps_set, 1)
            for t in range(TT):
                if x_ready is not None:
                    act.wait_ge(x_ready, 16 * TT)
                if t:
                    act.wait_ge(summed, t)
                nc.scalar.activation(squares[:], m.res[:, t, :], ACT.Square, accum_out=sums[:, t:t + 1]) \
                    .then_inc(summed, 1)
                act.wait_ge(summed, t + 1)
                nc.scalar.activation(rms[:, t:t + 1], sums[:, t:t + 1], ACT.Sqrt, bias=m.eps[:], scale=1.0 / D) \
                    .then_inc(rms_done, 1)
                if gamma is None and t:
                    act.wait_ge(turned, t)
                    for half in range(2):
                        last = nc.scalar.activation(hT[:, 4 * half:4 * half + 4, (t - 1) * P:t * P],
                                                    ps[:, 2 * ((t - 1) % 2) + half, :, :], ACT.Copy)
                    last.then_inc(out_done, 1)
            if gamma is None:
                act.wait_ge(turned, TT)
                for half in range(2):
                    last = nc.scalar.activation(hT[:, 4 * half:4 * half + 4, (TT - 1) * P:TT * P],
                                                ps[:, 2 * ((TT - 1) % 2) + half, :, :], ACT.Copy)
                last.then_inc(out_done, 1)

        @block.gpsimd
        def _(pool):
            if gamma is not None:
                for t in range(TT):
                    pool.wait_ge(rstd_done, t + 1)
                    if t >= 2:
                        pool.wait_ge(turned, t - 1)
                    nc.gpsimd.tensor_scalar(scaled[:, t % 2, :], m.res[:, t, :], rstd[:, t:t + 1], None, ALU.mult) \
                        .then_inc(scaled_done, 1)

        @block.vector
        def _(dve):
            def turn_out(t):
                dve.wait_ge(turned, t + 1)
                for half in range(2):
                    at, _ = COLS[gamma]
                    scale = m.params[:, at + 4 * half:at + 4 * half + 4].unsqueeze(2).to_broadcast([P, 4, P])
                    last = nc.vector.tensor_tensor(hT[:, 4 * half:4 * half + 4, t * P:(t + 1) * P],
                                                   ps[:, 2 * (t % 2) + half, :, :], scale, ALU.mult)
                last.then_inc(out_done, 1)

            for t in range(TT):
                dve.wait_ge(rms_done, t + 1)
                nc.vector.reciprocal(rstd[:, t:t + 1], rms[:, t:t + 1]).then_inc(rstd_done, 1)
                if gamma is not None:
                    if t:
                        turn_out(t - 1)
                else:
                    dve.wait_ge(rstd_done, t + 1)
                    if t == 0:
                        dve.wait_ge(g_in, 16)
                    if t >= 2:
                        dve.wait_ge(turned, t - 1)
                        dve.wait_ge(stored[t % 2], 16 * (t // 2))
                    nc.vector.scalar_tensor_tensor(out=scaled[:, t % 2, :], in0=m.res[:, t, :],
                                                   scalar=rstd[:, t:t + 1], in1=g_row[:], op0=ALU.mult,
                                                   op1=ALU.mult).then_inc(scaled_done, 1)
            if gamma is not None:
                turn_out(TT - 1)

        @block.tensor
        def _(pe):
            for t in range(TT):
                pe.wait_ge(scaled_done, t + 1)
                if t >= 2:
                    pe.wait_ge(out_done, t - 1)
                for k in range(KT):
                    last = nc.tensor.transpose(ps[:, 2 * (t % 2) + k // 4, k % 4, :],
                                               scaled[:, t % 2, k * P:(k + 1) * P], m.ident[:])
                last.then_inc(turned, 1)

        @block.sync
        def _(sp):
            if gamma_row is not None:
                sp.dma_start(g_row[:], gamma_row.to_broadcast([P, D])).then_inc(g_in, 16)
                for t in range(TT):
                    sp.wait_ge(scaled_done, t + 1)
                    sp.dma_start(rows_out[t * P:(t + 1) * P, :], scaled[:, t % 2, :]).then_inc(stored[t % 2], 16)
                for s in range(2):
                    sp.wait_ge(stored[s], 16 * TT // 2)


def project_first(nc, m, A, hT):
    with ExitStack() as mem:
        sem = m.sem
        SLOTS = 4
        w = mem.enter_context(nc.sbuf_tensor("proj_w", [P, SLOTS, KT, P], F32))
        x1 = mem.enter_context(nc.sbuf_tensor("x1", [P, HT, SEQ], F32))
        conv = mem.enter_context(nc.sbuf_tensor("conv", [P, 2, SEQ], F32))
        zero = mem.enter_context(nc.sbuf_tensor("zero_rows", [CAP, D], F32))
        zero_set = sem("zero_set")
        rows_blank = sem("rows_blank")
        ps = mem.enter_context(nc.psum_tensor("proj_ps", [P, 4, 2, BANK], F32))
        w_in = [sem(f"proj_w_in{i}") for i in range(SLOTS)]
        proj_mm = sem("proj_mm")
        centre = sem("proj_centre")
        proj_out = sem("proj_out")
        steps = Steps(sem("proj_steps"))
        block = mem.enter_context(nc.Block())
        COUNT = 4 * HT

        @block.sync
        def _(sp):
            weights = A["w_in"][0].rearrange("(k p) n -> p k n", p=P)
            for s in range(SLOTS):
                sp.dma_start(w[:, s, :, :], weights[:, :, s * P:(s + 1) * P]).then_inc(w_in[s], 16)
            with sp.Fori(1, COUNT // SLOTS) as r:
                for s in range(SLOTS):
                    sp.wait_ge(proj_mm, (r - 1) * SLOTS + s + 1)
                    sp.dma_start(w[:, s, :, :], weights[:, :, bass.ds((r * SLOTS + s) * P, P)]).then_inc(w_in[s], 16)

        @block.gpsimd
        def _(pool):
            nc.gpsimd.memset(zero[:], 0.0).then_inc(zero_set, 1)
            pool.wait_ge(zero_set, 1)
            for b in range(EXPERTS, BLOCKS):
                pool.dma_start(m.y_dram[b * CAP:(b + 1) * CAP, :], zero[:]).then_inc(rows_blank, 16)
            pool.wait_ge(rows_blank, 16 * OVER)

        @block.tensor
        def _(pe):
            def channel_tile(s, arrived, free):
                pe.wait_ge(w_in[s], arrived)
                if free is not None:
                    pe.wait_ge(proj_out, free)
                for half in range(2):
                    for k in range(KT):
                        last = nc.tensor.matmul(ps[:, s, half, :], w[:, s, k, :],
                                                hT[:, k, half * BANK:(half + 1) * BANK],
                                                start=(k == 0), stop=(k == KT - 1))
                last.then_inc(proj_mm, 1)

            for s in range(SLOTS):
                channel_tile(s, 16, None)
            with pe.Fori(1, COUNT // SLOTS) as r:
                for s in range(SLOTS):
                    channel_tile(s, (r + 1) * 16, (r - 1) * SLOTS + s + 1)

        @block.scalar
        def _(act):
            for c in range(3 * HT):
                act.wait_ge(proj_mm, c + 1)
                into = (m.mixT[:, c % HT, :], x1[:, c % HT, :], conv[:, c % 2, :])[c // HT]
                if c >= 2 * HT + 2:
                    act.wait_ge(proj_out, c - 1)
                nc.scalar.activation(into.rearrange("p (h c) -> p h c", h=2), ps[:, c % 4, :, :], ACT.Identity,
                                     bias=col(m.params, "conv_b", c),
                                     scale=col(m.params, "conv_w", 3 * HT + c)).then_inc(centre, 1)

        @block.vector
        def _(dve):
            for c in range(4 * HT):
                dve.wait_ge(proj_mm, c + 1)
                raw = ps[:, c % 4, :, :].rearrange("p h c -> p (h c)")
                if c >= 3 * HT:
                    nc.vector.tensor_copy(m.mixT[:, c - 2 * HT, :], raw).then_inc(proj_out, 1)
                    continue
                into = (m.mixT[:, c % HT, :], x1[:, c % HT, :], conv[:, c % 2, :])[c // HT]
                dve.wait_ge(centre, c + 1)
                steps.end(nc.vector.scalar_tensor_tensor(out=into[:, 1:SEQ], in0=raw[:, 0:SEQ - 1],
                                                         scalar=col(m.params, "conv_w", c), in1=into[:, 1:SEQ],
                                                         op0=ALU.mult, op1=ALU.add))
                steps.wait(dve)
                last = nc.vector.scalar_tensor_tensor(out=into[:, 0:SEQ - 1], in0=raw[:, 1:SEQ],
                                                      scalar=col(m.params, "conv_w", 2 * 3 * HT + c),
                                                      in1=into[:, 0:SEQ - 1], op0=ALU.mult, op1=ALU.add)
                if c >= 2 * HT:
                    steps.end(last)
                    steps.wait(dve)
                    last = nc.vector.tensor_tensor(m.zT[:, c % HT, :], x1[:, c % HT, :], conv[:, c % 2, :], ALU.mult)
                last.then_inc(proj_out, 1)


def transform_mixes(nc, m, A):
    with ExitStack() as mem:
        def sb(name, shape, dt=F32):
            return mem.enter_context(nc.sbuf_tensor(name, shape, dt))

        sem = m.sem
        SLOTS = 4
        pair = sb("pair", [P, 2 * P])
        znat = sb("znat", [P, 2 * JT, D_HYENA])
        U = sb("U", [P, 2, 2, JT, BANK])
        even_part = sb("u_even_part", [P, JT, BANK])
        chan = sb("chan", [P, JT, HT, 2 * P])
        table = sb("mix_table", [P, SLOTS, HALF])
        ps = mem.enter_context(nc.psum_tensor("mix_ps", [P, 8, BANK], F32))

        pair_in = sem("pair_in")
        tab_in = [sem(f"mix_table_in{i}") for i in range(SLOTS)]
        tab_used = sem("mix_table_used")
        z_turned = sem("z_turned")
        z_kept = sem("z_kept")
        even_kept = sem("u_even_kept")
        u_done = sem("u_done")
        chan_mm = sem("chan_mm")
        chan_kept = sem("chan_kept")
        g_done = sem("g_done")
        four_even = sem("four_even")
        four_done = sem("four_done")
        bias_done = sem("bias_done")
        back_read = sem("back_read")
        steps = Steps(sem("mix_steps"))
        FWD, DFT, BACK = 0, 4 * JT, 8 * JT
        N_TILES = 12 * JT
        block = mem.enter_context(nc.Block())

        def table_tile(n):
            if n < DFT:
                return A["half_tables"][n // JT, (n % JT) * P:(n % JT + 1) * P, :]
            if n < BACK:
                par, a, trig = (n - DFT) // (2 * JT), (n - DFT) // 2 % JT, n % 2
                return A["dft_tables"][2 * par + trig, a * P:(a + 1) * P, :]
            par, trig, f = (n - BACK) // (2 * JT), (n - BACK) // JT % 2, n % JT
            return A["back_tables"][par, trig, f * P:(f + 1) * P, :]

        @block.sync
        def _(sp):
            sp.dma_start(pair[:], A["pair_table"].rearrange("p t c -> p (t c)")).then_inc(pair_in, 16)
            for n in range(N_TILES):
                if n >= SLOTS:
                    sp.wait_ge(tab_used, n - SLOTS + 1)
                sp.dma_start(table[:, n % SLOTS, :], table_tile(n)).then_inc(tab_in[n % SLOTS], 16)

        @block.tensor
        def _(pe):
            def arrived(n):
                pe.wait_ge(tab_in[n % SLOTS], 16 * (n // SLOTS + 1))

            def channel_transform(par):
                for a in range(JT):
                    n = par * JT + a
                    if a >= 2:
                        pe.wait_ge(chan_kept, n - 1)
                    for c in range(HT):
                        last = nc.tensor.matmul(ps[:, 4 * par + 2 * (a % 2) + c // 2, (c % 2) * 2 * P:(c % 2 + 1) * 2 * P],
                                                m.mixT[:, HT + c, 2 * P * a + par:2 * P * (a + 1):2], pair[:],
                                                start=True, stop=True)
                    last.then_inc(chan_mm, 1)

            for n in range(2 * JT):
                par, a = n // JT, n % JT
                if n >= 4:
                    pe.wait_ge(z_kept, n - 3)
                for c in range(HT):
                    last = nc.tensor.transpose(ps[:, n % 4, c * P:(c + 1) * P],
                                               m.zT[:, c, 2 * P * a + par:2 * P * (a + 1):2], m.ident[:])
                last.then_inc(z_turned, 1)
            for g in range(4):
                if g < 2:
                    pe.wait_ge(z_kept, 2 * JT)
                else:
                    pe.wait_ge(u_done if g % 2 else even_kept, 1)
                for a in range(JT):
                    n = FWD + g * JT + a
                    arrived(n)
                    for f in range(JT):
                        last = nc.tensor.matmul(ps[:, 4 * (g % 2) + f, :], table[:, n % SLOTS, f * P:(f + 1) * P],
                                                znat[:, (g % 2) * JT + a, :], start=(a == 0), stop=(a == JT - 1))
                    last.then_inc(tab_used, 1)
            pe.wait_ge(pair_in, 16)
            for par in range(2):
                pe.wait_ge(u_done if par else even_kept, 2)
                channel_transform(par)
                pe.wait_ge(chan_kept, (par + 1) * JT)
                for a in range(JT):
                    for trig in range(2):
                        n = DFT + (par * JT + a) * 2 + trig
                        arrived(n)
                        for c in range(HT):
                            last = nc.tensor.matmul(ps[:, 4 * par + c, :], chan[:, a, c, trig * P:(trig + 1) * P],
                                                    table[:, n % SLOTS, :], start=(a == 0 and trig == 0),
                                                    stop=(a == JT - 1 and trig == 1))
                        last.then_inc(tab_used, 1)
            for par in range(2):
                pe.wait_ge(four_done if par else four_even, 1)
                for k in range(2 * JT):
                    trig, f = k // JT, k % JT
                    if par == 0 and trig == 0:
                        pe.wait_ge(g_done, f + 1)
                    n = BACK + par * 2 * JT + k
                    arrived(n)
                    for c in range(HT):
                        last = nc.tensor.matmul(ps[:, 4 * par + c, :], U[:, trig, par, f, c * P:(c + 1) * P],
                                                table[:, n % SLOTS, :], start=(k == 0), stop=(k == 2 * JT - 1))
                    last.then_inc(tab_used, 1)

        @block.scalar
        def _(act):
            for n in range(2 * JT):
                act.wait_ge(z_turned, n + 1)
                nc.scalar.activation(znat[:, n, :], ps[:, n % 4, :], ACT.Copy).then_inc(z_kept, 1)
            for trig in range(2):
                act.wait_ge(tab_used, FWD + (2 * trig + 1) * JT)
                if trig:
                    act.wait_ge(u_done, 1)
                nc.scalar.activation(even_part[:], ps[:, 0:4, :], ACT.Copy).then_inc(even_kept, 1)
            for par in range(2):
                for a in range(JT):
                    n = par * JT + a
                    act.wait_ge(chan_mm, n + 1)
                    if par:
                        act.wait_ge(tab_used, DFT + 2 * (a + 1))
                    b = 4 * par + 2 * (a % 2)
                    nc.scalar.activation(chan[:, a, :, :].rearrange("p (b c) n -> p b (c n)", b=2), ps[:, b:b + 2, :],
                                         ACT.Copy).then_inc(chan_kept, 1)
                if par == 0:
                    act.wait_ge(tab_used, DFT + 2 * JT)
                    act.wait_ge(u_done, 2)
                    nc.scalar.activation(even_part[:], ps[:, 0:4, :], ACT.Copy).then_inc(four_even, 1)

        @block.gpsimd
        def _(pool):
            pool.wait_ge(z_turned, 2 * JT)
            for c in range(HT):
                nc.gpsimd.tensor_scalar(m.zT[:, c, :], m.zT[:, c, :], col(m.params, "f_bias", c), None, ALU.mult) \
                    .then_inc(bias_done, 1)

        @block.vector
        def _(dve):
            for trig in range(2):
                dve.wait_ge(even_kept, trig + 1)
                dve.wait_ge(tab_used, FWD + (2 * trig + 2) * JT)
                nc.vector.tensor_tensor(U[:, trig, 0, :, :], even_part[:], ps[:, 4:8, :], ALU.add)
                nc.vector.tensor_tensor(U[:, trig, 1, :, :], even_part[:], ps[:, 4:8, :], ALU.subtract) \
                    .then_inc(u_done, 1)
            dve.wait_ge(u_done, 2)
            for f in range(JT):
                if f:
                    dve.wait_ge(g_done, f)
                for pm in range(2):
                    for i, (a, b) in enumerate(((0, 0), (1, 1), (0, 1), (1, 0))):
                        last = nc.vector.tensor_tensor(znat[:, 4 * pm + i, :], U[:, a, pm, f, :], m.K[:, b, pm, f, :],
                                                       ALU.mult)
                steps.end(last)
                steps.wait(dve)
                for pm in range(2):
                    for i, op in ((0, ALU.subtract), (2, ALU.add)):
                        last = nc.vector.tensor_tensor(znat[:, 4 * pm + i, :], znat[:, 4 * pm + i, :],
                                                       znat[:, 4 * pm + i + 1, :], op)
                steps.end(last)
                steps.wait(dve)
                for trig in range(2):
                    for par, op in ((0, ALU.add), (1, ALU.subtract)):
                        last = nc.vector.tensor_tensor(U[:, trig, par, f, :], znat[:, 2 * trig, :],
                                                       znat[:, 4 + 2 * trig, :], op)
                last.then_inc(g_done, 1)
            dve.wait_ge(four_even, 1)
            dve.wait_ge(tab_used, DFT + 4 * JT)
            nc.vector.tensor_tensor(m.mixT[:, HT:2 * HT, 0:HALF], even_part[:], ps[:, 4:8, :], ALU.add)
            nc.vector.tensor_tensor(m.mixT[:, HT:2 * HT, HALF:SEQ], even_part[:], ps[:, 4:8, :], ALU.subtract) \
                .then_inc(four_done, 1)
            dve.wait_ge(bias_done, HT)
            for par in range(2):
                dve.wait_ge(tab_used, BACK + (par + 1) * 2 * JT)
                for c in range(HT):
                    steps.end(nc.vector.scalar_tensor_tensor(
                        out=m.zT[:, c, par:SEQ:2], in0=ps[:, 4 * par + c, :], scalar=m.inv_size[:, c:c + 1],
                        in1=m.zT[:, c, par:SEQ:2], op0=ALU.mult, op1=ALU.add))
                    steps.wait(dve)
                    nc.vector.tensor_tensor(m.mixT[:, c, par:SEQ:2], m.mixT[:, c, par:SEQ:2], m.zT[:, c, par:SEQ:2],
                                            ALU.mult)


def head_norm_project(nc, m, A):
    with ExitStack() as mem:
        def sb(name, shape, dt=F32):
            return mem.enter_context(nc.sbuf_tensor(name, shape, dt))

        sem = m.sem
        heads = sb("heads", [P, P])
        w = sb("w_out_sb", [P, KT, D])
        sq = sb("head_squares", [P, 2, SEQ])
        rms = sb("head_rms", [P, 2, SEQ])
        ps = mem.enter_context(nc.psum_tensor("head_ps", [P, 4, 2, BANK], F32))
        heads_in = sem("heads_in")
        w_in = sem("w_out_in")
        squared = sem("head_squared")
        mean_mm = sem("head_mean_mm")
        rms_done = sem("head_rms_done")
        normed = sem("head_normed")
        out_mm = sem("w_out_mm")
        added = sem("w_out_added")
        steps = Steps(sem("head_steps"))
        block = mem.enter_context(nc.Block())

        @block.sync
        def _(sp):
            sp.dma_start(heads[:], A["head_table"]).then_inc(heads_in, 16)
            for k in range(KT):
                sp.dma_start(w[:, k, :], A["w_out"][0, k * P:(k + 1) * P, :]).then_inc(w_in, 16)

        @block.gpsimd
        def _(pool):
            for c in range(KT):
                if c >= 2:
                    pool.wait_ge(mean_mm, c - 1)
                nc.gpsimd.tensor_tensor(sq[:, c % 2, :], m.mixT[:, c, :], m.mixT[:, c, :], ALU.mult) \
                    .then_inc(squared, 1)

        @block.tensor
        def _(pe):
            pe.wait_ge(heads_in, 16)
            for c in range(KT):
                pe.wait_ge(squared, c + 1)
                if c >= 4:
                    pe.wait_ge(rms_done, c - 3)
                for half in range(2):
                    last = nc.tensor.matmul(ps[:, c % 4, half, :], heads[:], sq[:, c % 2, half * BANK:(half + 1) * BANK],
                                            start=True, stop=True)
                last.then_inc(mean_mm, 1)
            pe.wait_ge(w_in, 16 * KT)
            pe.wait_ge(rms_done, KT)
            pe.wait_ge(normed, KT)
            for t in range(TT):
                if t >= 4:
                    pe.wait_ge(added, t - 3)
                for half in range(2):
                    for k in range(KT):
                        last = nc.tensor.matmul(ps[:, t % 4, half, :], m.mixT[:, k, t * P:(t + 1) * P],
                                                w[:, k, half * BANK:(half + 1) * BANK],
                                                start=(k == 0), stop=(k == KT - 1))
                last.then_inc(out_mm, 1)

        @block.scalar
        def _(act):
            for c in range(KT):
                act.wait_ge(mean_mm, c + 1)
                if c >= 2:
                    act.wait_ge(normed, c - 1)
                nc.scalar.activation(rms[:, c % 2, :].rearrange("p (h c) -> p h c", h=2), ps[:, c % 4, :, :], ACT.Sqrt,
                                     bias=m.eps[:]).then_inc(rms_done, 1)

        @block.vector
        def _(dve):
            for c in range(KT):
                dve.wait_ge(rms_done, c + 1)
                steps.end(nc.vector.reciprocal(rms[:, c % 2, :], rms[:, c % 2, :]))
                steps.wait(dve)
                nc.vector.scalar_tensor_tensor(out=m.mixT[:, c, :], in0=m.mixT[:, c, :],
                                               scalar=col(m.params, "mix_g", c), in1=rms[:, c % 2, :],
                                               op0=ALU.mult, op1=ALU.mult).then_inc(normed, 1)
            for t in range(TT):
                dve.wait_ge(out_mm, t + 1)
                nc.vector.tensor_tensor(m.res[:, t, :], m.res[:, t, :],
                                        ps[:, t % 4, :, :].rearrange("p h c -> p (h c)"), ALU.add) \
                    .then_inc(added, 1)


def first_mixer(nc, m, A):
    with nc.sbuf_tensor("K", [P, 2, 2, JT, BANK], F32) as m.K:
        filter_spectrum(nc, m, A)
        with nc.sbuf_tensor("mixT", [P, KT, SEQ], F32) as m.mixT, nc.sbuf_tensor("zT", [P, HT, SEQ], F32) as m.zT:
            with nc.sbuf_tensor("hT1", [P, KT, SEQ], F32) as hT:
                norm_to_T(nc, m, "norm1", hT, gamma="norm1_g", x_ready=m.x_in)
                project_first(nc, m, A, hT)
            transform_mixes(nc, m, A)
            head_norm_project(nc, m, A)


def route(nc, m, A, hT):
    with ExitStack() as mem:
        def sb(name, shape, dt=F32):
            return mem.enter_context(nc.sbuf_tensor(name, shape, dt))

        sem = m.sem
        NL = GROUPS + EXPERTS
        w = sb("router_w", [P, KT, NL])
        b = sb("router_b", [P, NL])
        before = sb("before", [P, P])
        idx = sb("index_row", [P, 2, EXPERTS])
        limits = sb("limits", [P, FULL_BLOCKS - 1])
        logits = sb("logits", [P, TT, NL])
        gmax = sb("gmax", [P, TT])
        gdiff = sb("gdiff", [P, TT, GROUPS])
        gexp = sb("gexp", [P, TT, GROUPS])
        gmask = sb("gmask", [P, TT, GROUPS])
        pg = sb("pg", [P, TT])
        part = sb("part", [P, 2, TT, PER_GROUP])
        sel = sb("sel", [P, TT, PER_GROUP])
        cand = sb("cand", [P, TT, PER_GROUP])
        first = sb("first", [P, TT])
        hot = sb("hot", [P, 2, TT, PER_GROUP])
        top = sb("top", [P, 2, TT])
        diff = sb("diff", [P, TT])
        ratio = sb("ratio", [P, TT])
        M = sb("M", [P, 2, TT, EXPERTS])
        both = sb("both", [P, TT, EXPERTS])
        earlier = sb("earlier", [P, TT + 1, EXPERTS])
        rank = sb("rank", [P, TT + 1, EXPERTS])
        over = sb("over", [P, EXPERTS, FULL_BLOCKS - 1])
        n_over = sb("n_over", [P, EXPERTS])
        incl = sb("incl", [P, EXPERTS])
        excl = sb("excl", [P, EXPERTS])
        prod = sb("prod", [P, TT, EXPERTS])
        r_of = sb("r_of", [P, 2, TT])
        e_of = sb("e_of", [P, 2, TT])
        s_of = sb("s_of", [P, 2, TT])
        steps_in = sb("steps_in", [P, 2, TT, FULL_BLOCKS - 1])
        full = sb("full", [P, 2, TT])
        blk = sb("blk", [P, 2, TT])
        posf = sb("posf", [P, 2, TT])
        pos = sb("pos_i", [P, 2, TT], I32)
        tokens = sb("token_ids", [P, TT], I32)
        blank = sb("blank", [CAP, BLOCKS], I32)
        ends = sb("ends", [1, OVER, EXPERTS])
        over_f = sb("over_f", [1, OVER + 1])
        ps = mem.enter_context(nc.psum_tensor("route_ps", [P, 2, BANK], F32))

        w_in = sem("router_in")
        logit_mm = sem("logit_mm")
        gdiff_done = sem("gdiff_done")
        gexp_done = sem("gexp_done")
        diff_done = sem("diff_done")
        ratio_done = sem("ratio_done")
        pairs_done = sem("pairs_done")
        rank_mm = sem("rank_mm")
        pos_done = sem("pos_done")
        ids_set = sem("ids_set")
        blanked = sem("blanked")
        listed = sem("listed")
        steps = Steps(sem("route_steps"))
        block = mem.enter_context(nc.Block())

        @block.sync
        def _(sp):
            sp.dma_start(w[:], A["w_router"].rearrange("(k p) n -> p k n", p=P)).then_inc(w_in, 16)
            sp.dma_start(b[:], A["b_router"].to_broadcast([P, NL])).then_inc(w_in, 16)
            sp.dma_start(before[:], A["before"]).then_inc(w_in, 16)
            sp.dma_start(idx[:], A["index_rows"].to_broadcast([P, 2, EXPERTS])).then_inc(w_in, 16)
            sp.dma_start(limits[:], A["limits"].to_broadcast([P, FULL_BLOCKS - 1])).then_inc(w_in, 16)

        @block.gpsimd
        def _(pool):
            nc.gpsimd.iota(tokens[:], pattern=[[P, TT]], base=0, channel_multiplier=1).then_inc(ids_set, 1)
            nc.gpsimd.memset(blank[:], 0).then_inc(ids_set, 1)
            pool.wait_ge(ids_set, 2)
            pool.dma_start(m.row_list.rearrange("(p b) o -> p (b o)", p=CAP), blank[:]).then_inc(blanked, 16)
            pool.wait_ge(blanked, 16)
            pool.wait_ge(pos_done, 1)
            for slot in range(2):
                for t in range(TT):
                    pool.indirect_dma_start(m.row_list, bass.IndirectOffsetOnAxis(ap=pos[:, slot, t:t + 1], axis=0),
                                            tokens[:, t:t + 1], None).then_inc(listed, 16)
            pool.wait_ge(listed, 16 * 2 * TT)

        @block.tensor
        def _(pe):
            pe.wait_ge(w_in, 80)
            for t in range(TT):
                for k in range(KT):
                    last = nc.tensor.matmul(ps[:, 0, t * NL:(t + 1) * NL], hT[:, k, t * P:(t + 1) * P], w[:, k, :],
                                            start=(k == 0), stop=(k == KT - 1))
            last.then_inc(logit_mm, 1)
            pe.wait_ge(pairs_done, 1)
            for t in range(TT + 1):
                out = ps[:, 1, t * EXPERTS:(t + 1) * EXPERTS]
                if t < TT:
                    nc.tensor.matmul(out, before[:], both[:, t, :], start=True, stop=False)
                last = nc.tensor.matmul(out, m.ones[:], earlier[:, t, :], start=(t == TT), stop=True)
            last.then_inc(rank_mm, 1)

        @block.scalar
        def _(act):
            act.wait_ge(gdiff_done, 1)
            nc.scalar.activation(gexp[:], gdiff[:], ACT.Exp).then_inc(gexp_done, 1)
            act.wait_ge(diff_done, 1)
            nc.scalar.activation(ratio[:], diff[:], ACT.Exp).then_inc(ratio_done, 1)

        @block.vector
        def _(dve):
            def step(instruction):
                steps.end(instruction)
                steps.wait(dve)

            def wide(a, n):
                return a.unsqueeze(2).to_broadcast([P, TT, n])

            def over_tiles(a, n):
                return a.unsqueeze(1).to_broadcast([P, TT, n])

            def first_of(mask_out, values, largest, n):
                c = cand[:, :, 0:n]
                step(nc.vector.tensor_tensor(c, values, wide(largest, n), ALU.is_equal))
                step(nc.vector.tensor_tensor(c, c, over_tiles(idx[:, 0, 0:n], n), ALU.mult))
                step(nc.vector.tensor_reduce(first[:], c, AX_X, ALU.min))
                step(nc.vector.tensor_tensor(mask_out, over_tiles(idx[:, 0, 0:n], n), wide(first[:], n), ALU.is_equal))

            dve.wait_ge(w_in, 80)
            dve.wait_ge(logit_mm, 1)
            step(nc.vector.tensor_tensor(logits[:], ps[:, 0, 0:TT * NL].rearrange("p (t n) -> p t n", t=TT),
                                         over_tiles(b[:], NL), ALU.add))
            group = logits[:, :, 0:GROUPS]
            step(nc.vector.tensor_reduce(gmax[:], group, AX_X, ALU.max))
            nc.vector.tensor_tensor(gdiff[:], group, wide(gmax[:], GROUPS), ALU.subtract).then_inc(gdiff_done, 1)
            first_of(gmask[:], group, gmax[:], GROUPS)
            dve.wait_ge(gexp_done, 1)
            step(nc.vector.tensor_reduce(pg[:], gexp[:], AX_X, ALU.add))
            step(nc.vector.reciprocal(pg[:], pg[:]))
            for g in range(GROUPS):
                of_g = logits[:, :, GROUPS + g * PER_GROUP:GROUPS + (g + 1) * PER_GROUP]
                mask = gmask[:, :, g:g + 1].to_broadcast([P, TT, PER_GROUP])
                if g == 0:
                    step(nc.vector.tensor_tensor(sel[:], of_g, mask, ALU.mult))
                else:
                    step(nc.vector.tensor_tensor(part[:, 0], of_g, mask, ALU.mult))
                    step(nc.vector.tensor_tensor(sel[:], sel[:], part[:, 0], ALU.add))
            for slot in range(2):
                step(nc.vector.tensor_reduce(top[:, slot, :], sel[:], AX_X, ALU.max))
                first_of(hot[:, slot], sel[:], top[:, slot, :], PER_GROUP)
                if slot == 0:
                    step(nc.vector.scalar_tensor_tensor(out=sel[:], in0=hot[:, 0], scalar=NEG, in1=sel[:],
                                                        op0=ALU.mult, op1=ALU.add))
            nc.vector.tensor_tensor(diff[:], top[:, 1, :], top[:, 0, :], ALU.subtract).then_inc(diff_done, 1)
            for slot in range(2):
                for g in range(GROUPS):
                    last = nc.vector.tensor_tensor(M[:, slot, :, g * PER_GROUP:(g + 1) * PER_GROUP], hot[:, slot],
                                                   gmask[:, :, g:g + 1].to_broadcast([P, TT, PER_GROUP]), ALU.mult)
            step(last)
            step(nc.vector.tensor_tensor(both[:], M[:, 0], M[:, 1], ALU.add))
            step(nc.vector.memset(earlier[:, 0, :], 0.0))
            for t in range(TT):
                last = nc.vector.tensor_tensor(earlier[:, t + 1, :], earlier[:, t, :], both[:, t, :], ALU.add)
                if t < TT - 1:
                    step(last)
            last.then_inc(pairs_done, 1)
            dve.wait_ge(ratio_done, 1)
            step(nc.vector.tensor_scalar(diff[:], ratio[:], 1.0, None, ALU.add))
            step(nc.vector.reciprocal(diff[:], diff[:]))
            step(nc.vector.tensor_tensor(m.pair_w[:, 0, :], diff[:], pg[:], ALU.mult))
            step(nc.vector.tensor_tensor(m.pair_w[:, 1, :], m.pair_w[:, 0, :], ratio[:], ALU.mult))
            dve.wait_ge(rank_mm, 1)
            step(nc.vector.tensor_copy(rank[:], ps[:, 1, 0:(TT + 1) * EXPERTS].rearrange("p (t e) -> p t e", t=TT + 1)))
            n_lim = FULL_BLOCKS - 1
            step(nc.vector.tensor_tensor(over[:], rank[:, TT, :].unsqueeze(2).to_broadcast([P, EXPERTS, n_lim]),
                                         limits[:].unsqueeze(1).to_broadcast([P, EXPERTS, n_lim]), ALU.is_gt))
            step(nc.vector.tensor_reduce(n_over[:], over[:], AX_X, ALU.add))
            step(nc.vector.tensor_tensor_scan(incl[:], m.ones[:, 0:EXPERTS], n_over[:], 0.0, ALU.mult, ALU.add))
            step(nc.vector.tensor_tensor(excl[:], incl[:], n_over[:], ALU.subtract))
            for slot in range(2):
                for out, table in ((r_of, rank[:, 0:TT, :]), (e_of, over_tiles(idx[:, 1, :], EXPERTS)),
                                   (s_of, over_tiles(excl[:], EXPERTS))):
                    step(nc.vector.tensor_tensor(prod[:], M[:, slot], table, ALU.mult))
                    step(nc.vector.tensor_reduce(out[:, slot, :], prod[:], AX_X, ALU.add))
            for slot in range(2):
                step(nc.vector.tensor_tensor(steps_in[:, slot], wide(r_of[:, slot, :], n_lim), over_tiles(limits[:], n_lim),
                                             ALU.is_ge))
                step(nc.vector.tensor_reduce(full[:, slot, :], steps_in[:, slot], AX_X, ALU.add))
            step(nc.vector.tensor_tensor(blk[:], s_of[:], full[:], ALU.add))
            step(nc.vector.tensor_tensor(blk[:], blk[:], e_of[:], ALU.subtract))
            step(nc.vector.tensor_scalar(blk[:], blk[:], float(EXPERTS - 1), None, ALU.add))
            step(nc.vector.scalar_tensor_tensor(out=blk[:], in0=full[:], scalar=1.0, in1=blk[:], op0=ALU.min,
                                                op1=ALU.mult))
            step(nc.vector.tensor_tensor(blk[:], blk[:], e_of[:], ALU.add))
            step(nc.vector.scalar_tensor_tensor(out=r_of[:], in0=full[:], scalar=-float(CAP), in1=r_of[:],
                                                op0=ALU.mult, op1=ALU.add))
            step(nc.vector.scalar_tensor_tensor(out=posf[:], in0=r_of[:], scalar=float(BLOCKS), in1=blk[:],
                                                op0=ALU.mult, op1=ALU.add))
            nc.vector.tensor_copy(pos[:], posf[:]).then_inc(pos_done, 1)
            step(nc.vector.scalar_tensor_tensor(out=blk[:], in0=blk[:], scalar=float(CAP), in1=r_of[:],
                                                op0=ALU.mult, op1=ALU.add))
            step(nc.vector.tensor_copy(m.pair_row[:], blk[:]))
            step(nc.vector.tensor_tensor(ends[:], incl[0:1, :].unsqueeze(1).to_broadcast([1, OVER, EXPERTS]),
                                         idx[0:1, 1, 0:OVER].unsqueeze(2).to_broadcast([1, OVER, EXPERTS]), ALU.is_le))
            step(nc.vector.tensor_reduce(over_f[:, 0:OVER], ends[:], AX_X, ALU.add))
            step(nc.vector.tensor_scalar(over_f[:, 0:OVER], over_f[:, 0:OVER], float(EXPERTS - 1), None, ALU.min))
            step(nc.vector.tensor_copy(over_f[:, OVER:OVER + 1], incl[0:1, EXPERTS - 1:EXPERTS]))
            step(nc.vector.tensor_copy(m.over_table[:], over_f[:]))


def experts(nc, m, A):
    with ExitStack() as mem:
        def sb(name, shape, dt=F32):
            return mem.enter_context(nc.sbuf_tensor(name, shape, dt))

        sem = m.sem
        S = 2
        FE = D_EXPERT // P
        w_g = sb("w_gate_sb", [P, S, KT, D_EXPERT])
        w_u = sb("w_up_sb", [P, S, KT, D_EXPERT])
        w_d = sb("w_down_sb", [P, S, FE, D])
        idx_all = sb("row_ids", [CAP, BLOCKS], I32)
        idx = sb("block_ids", [CAP, S], I32)
        rows = sb("rows", [CAP, S, D])
        xT = sb("xT", [P, S, KT, CAP])
        act_out = sb("gate_act", [P, S, FE, CAP])
        hidT = sb("hidT", [P, S, FE, CAP])
        y = sb("y_rows", [CAP, S, D])
        ps_x = mem.enter_context(nc.psum_tensor("x_ps", [P, KT, P], F32))
        ps_h = mem.enter_context(nc.psum_tensor("h_ps", [P, S, 2, FE, P], F32))
        ps_y = mem.enter_context(nc.psum_tensor("y_ps", [P, 2, BANK], F32))

        ids_in = sem("row_ids_in")
        g_in = [sem(f"w_gate_in{s}") for s in range(S)]
        u_in = [sem(f"w_up_in{s}") for s in range(S)]
        d_in = [sem(f"w_down_in{s}") for s in range(S)]
        idx_set = [sem(f"block_ids_set{s}") for s in range(S)]
        rows_in = [sem(f"rows_in{s}") for s in range(S)]
        turned = [sem(f"rows_turned{s}") for s in range(S)]
        xT_done = [sem(f"xT_done{s}") for s in range(S)]
        gate_mm = [sem(f"gate_mm{s}") for s in range(S)]
        up_mm = [sem(f"up_mm{s}") for s in range(S)]
        act_done = [sem(f"gate_act_done{s}") for s in range(S)]
        hid_done = [sem(f"hid_done{s}") for s in range(S)]
        down_mm = [sem(f"down_mm{s}") for s in range(S)]
        y_left = [sem(f"y_left{s}") for s in range(S)]
        y_right = [sem(f"y_right{s}") for s in range(S)]
        y_out = [sem(f"y_stored{s}") for s in range(S)]
        block = mem.enter_context(nc.Block())
        waited_sp = sem("waited_sp")
        waited_pool = sem("waited_pool")
        PAIRS = EXPERTS // S


        def over_blocks(engine, body):
            count = engine.value_load(m.over_table[0:1, OVER:OVER + 1], min_val=0, max_val=OVER)
            with engine.Fori(0, OVER) as j:
                with engine.If(j < count):
                    body(j)
            return count

        @block.sync
        def _(sp):
            def load(s, e, use, first=False):
                for (w, name, arrived, read) in ((w_g, "w_gate", g_in, gate_mm), (w_u, "w_up", u_in, up_mm),
                                                 (w_d, "w_down", d_in, down_mm)):
                    if not first:
                        sp.wait_ge(read[s], use)
                    sp.dma_start(w[:, s, :, :], A[name][0, bass.ds(e, 1)].rearrange("o (k p) n -> p (o k) n", p=P)) \
                        .then_inc(arrived[s], 16)

            def store(s, b, use):
                sp.wait_ge(y_left[s], use + 1)
                sp.wait_ge(y_right[s], use + 1)
                sp.dma_start(m.y_dram[bass.ds(b * CAP, CAP), :], y[:, s, :]).then_inc(y_out[s], 16)

            sp.dma_start(idx_all[:], m.row_list.rearrange("(p b) o -> p (b o)", p=CAP)).then_inc(ids_in, 16)
            for s in range(S):
                load(s, s, 0, first=True)
            with sp.Fori(0, PAIRS - 1) as i:
                for s in range(S):
                    load(s, i * S + (S + s), i + 1)
                    store(s, i * S + s, i)
            for s in range(S):
                store(s, EXPERTS - S + s, PAIRS - 1)

            def over(j):
                e = sp.value_load(m.over_table[0:1, bass.ds(j, 1)], min_val=0, max_val=EXPERTS - 1)
                load(0, e, j + PAIRS)
                store(0, j + EXPERTS, j + PAIRS)

            count = over_blocks(sp, over)
            sp.wait_ge(y_out[0], (count + PAIRS) * 16)
            sp.sem_inc(waited_sp, 1)
            sp.wait_ge(y_out[1], PAIRS * 16)

        @block.gpsimd
        def _(pool):
            def gather(s, b, use, first=False):
                if not first:
                    pool.wait_ge(turned[s], use)
                nc.gpsimd.tensor_copy(idx[:, s:s + 1], idx_all[:, bass.ds(b, 1)]).then_inc(idx_set[s], 1)
                pool.wait_ge(idx_set[s], use + 1)
                pool.sem_inc(waited_pool, 1)
                pool.indirect_dma_start(rows[:, s, :], None, m.hn_dram,
                                        bass.IndirectOffsetOnAxis(ap=idx[:, s:s + 1], axis=0)).then_inc(rows_in[s], 16)

            pool.wait_ge(ids_in, 16)
            for s in range(S):
                gather(s, s, 0, first=True)
            with pool.Fori(1, PAIRS) as i:
                for s in range(S):
                    gather(s, i * S + s, i)
            over_blocks(pool, lambda j: gather(0, j + EXPERTS, j + PAIRS))

        @block.tensor
        def _(pe):
            def turn(s, use, before=None):
                pe.wait_ge(rows_in[s], (use + 1) * 16)
                if before is not None:
                    pe.wait_ge(xT_done[before[0]], before[1] + 1)
                for k in range(KT):
                    last = nc.tensor.transpose(ps_x[:, k, 0:CAP], rows[:, s, k * P:(k + 1) * P], m.ident[0:CAP, 0:CAP])
                last.then_inc(turned[s], 1)

            def gate_up(s, use):
                pe.wait_ge(xT_done[s], use + 1)
                for i, (w, arrived, done) in enumerate(((w_g, g_in, gate_mm), (w_u, u_in, up_mm))):
                    pe.wait_ge(arrived[s], (use + 1) * 16)
                    for f in range(FE):
                        for k in range(KT):
                            last = nc.tensor.matmul(ps_h[:, s, i, f, 0:CAP], w[:, s, k, f * P:(f + 1) * P],
                                                    xT[:, s, k, :], start=(k == 0), stop=(k == KT - 1))
                    last.then_inc(done[s], 1)

            def down(s, use, before=None):
                pe.wait_ge(hid_done[s], use + 1)
                pe.wait_ge(d_in[s], (use + 1) * 16)
                if before is not None:
                    pe.wait_ge(y_left[before[0]], before[1] + 1)
                    pe.wait_ge(y_right[before[0]], before[1] + 1)
                for half in range(2):
                    for f in range(FE):
                        last = nc.tensor.matmul(ps_y[0:CAP, half, :], hidT[:, s, f, :],
                                                w_d[:, s, f, half * BANK:(half + 1) * BANK],
                                                start=(f == 0), stop=(f == FE - 1))
                last.then_inc(down_mm[s], 1)

            turn(0, 0)
            gate_up(0, 0)
            turn(1, 0, before=(0, 0))
            down(0, 0)
            with pe.Fori(0, PAIRS - 1) as i:
                gate_up(1, i)
                turn(0, i + 1, before=(1, i))
                down(1, i, before=(0, i))
                gate_up(0, i + 1)
                turn(1, i + 1, before=(0, i + 1))
                down(0, i + 1, before=(1, i))
            gate_up(1, PAIRS - 1)
            down(1, PAIRS - 1, before=(0, PAIRS - 1))

            def over(j):
                turn(0, j + PAIRS)
                gate_up(0, j + PAIRS)
                down(0, j + PAIRS, before=(0, j + (PAIRS - 1)))

            pe.wait_ge(y_left[1], PAIRS)
            pe.wait_ge(y_right[1], PAIRS)
            over_blocks(pe, over)

        @block.scalar
        def _(act):
            def gate(s, use, first=False):
                act.wait_ge(gate_mm[s], use + 1)
                if not first:
                    act.wait_ge(hid_done[s], use)
                nc.scalar.activation(act_out[:, s, :, :], ps_h[:, s, 0, :, 0:CAP], ACT.Silu).then_inc(act_done[s], 1)

            def left(s, use, first=False):
                act.wait_ge(down_mm[s], use + 1)
                if not first:
                    act.wait_ge(y_out[s], use * 16)
                nc.scalar.activation(y[:, s, 0:BANK], ps_y[0:CAP, 0, :], ACT.Copy).then_inc(y_left[s], 1)

            for s in range(S):
                gate(s, 0, first=True)
                left(s, 0, first=True)
            with act.Fori(1, PAIRS) as i:
                for s in range(S):
                    gate(s, i)
                    left(s, i)

            def over(j):
                gate(0, j + PAIRS)
                left(0, j + PAIRS)

            over_blocks(act, over)

        @block.vector
        def _(dve):
            def x_out(s, use, first=False):
                dve.wait_ge(turned[s], use + 1)
                if not first:
                    dve.wait_ge(up_mm[s], use)
                nc.vector.tensor_copy(xT[:, s, :, :], ps_x[:, :, 0:CAP]).then_inc(xT_done[s], 1)

            def hidden(s, use, first=False):
                dve.wait_ge(up_mm[s], use + 1)
                dve.wait_ge(act_done[s], use + 1)
                if not first:
                    dve.wait_ge(down_mm[s], use)
                nc.vector.tensor_tensor(hidT[:, s, :, :], act_out[:, s, :, :], ps_h[:, s, 1, :, 0:CAP], ALU.mult) \
                    .then_inc(hid_done[s], 1)

            def right(s, use, first=False):
                dve.wait_ge(down_mm[s], use + 1)
                if not first:
                    dve.wait_ge(y_out[s], use * 16)
                nc.vector.tensor_copy(y[:, s, BANK:D], ps_y[0:CAP, 1, :]).then_inc(y_right[s], 1)

            def pair(i, first=False):
                hidden(0, i, first)
                x_out(1, i, first)
                right(0, i, first)
                hidden(1, i, first)
                if not (isinstance(i, int) and i == PAIRS - 1):
                    x_out(0, i + 1)
                right(1, i, first)

            x_out(0, 0, first=True)
            pair(0, first=True)
            with dve.Fori(1, PAIRS - 1) as i:
                pair(i)
            pair(PAIRS - 1)

            def over(j):
                x_out(0, j + PAIRS)
                hidden(0, j + PAIRS)
                right(0, j + PAIRS)

            over_blocks(dve, over)


def combine(nc, m, A):
    with ExitStack() as mem:
        def sb(name, shape, dt=F32):
            return mem.enter_context(nc.sbuf_tensor(name, shape, dt))

        sem = m.sem
        BUF = 3
        y = sb("y_pairs", [P, BUF, 2, D])
        g_row = sb("final_gamma", [P, D])
        squares = sb("final_squares", [P, D])
        sums = sb("final_sums", [P, TT])
        rms = sb("final_rms", [P, TT])
        rstd = sb("final_rstd", [P, TT])
        y_in = [sem(f"y_in{i}") for i in range(BUF)]
        g_in = sem("final_gamma_in")
        summed = sem("combined")
        squared = sem("final_squared")
        rms_done = sem("final_rms_done")
        steps = Steps(sem("combine_steps"))
        block = mem.enter_context(nc.Block())

        @block.sync
        def _(sp):
            sp.dma_start(g_row[:], A["final_g"].to_broadcast([P, D])).then_inc(g_in, 16)

        @block.gpsimd
        def _(pool):
            for t in range(TT):
                if t >= BUF:
                    pool.wait_ge(summed, t - BUF + 1)
                for slot in range(2):
                    pool.indirect_dma_start(y[:, t % BUF, slot, :], None, m.y_dram,
                                            bass.IndirectOffsetOnAxis(ap=m.pair_row[:, slot, t:t + 1], axis=0)) \
                        .then_inc(y_in[t % BUF], 16)

        @block.scalar
        def _(act):
            for t in range(TT):
                act.wait_ge(summed, t + 1)
                if t:
                    act.wait_ge(squared, t)
                nc.scalar.activation(squares[:], m.res[:, t, :], ACT.Square, accum_out=sums[:, t:t + 1]) \
                    .then_inc(squared, 1)
                act.wait_ge(squared, t + 1)
                nc.scalar.activation(rms[:, t:t + 1], sums[:, t:t + 1], ACT.Sqrt, bias=m.eps[:], scale=1.0 / D) \
                    .then_inc(rms_done, 1)

        @block.vector
        def _(dve):
            def normalise(t):
                dve.wait_ge(rms_done, t + 1)
                steps.end(nc.vector.reciprocal(rstd[:, t:t + 1], rms[:, t:t + 1]))
                steps.wait(dve)
                nc.vector.scalar_tensor_tensor(out=m.res[:, t, :], in0=m.res[:, t, :], scalar=rstd[:, t:t + 1],
                                               in1=g_row[:], op0=ALU.mult, op1=ALU.mult)

            dve.wait_ge(g_in, 16)
            for t in range(TT):
                dve.wait_ge(y_in[t % BUF], 32 * (t // BUF + 1))
                for slot in range(2):
                    last = nc.vector.scalar_tensor_tensor(out=m.res[:, t, :], in0=y[:, t % BUF, slot, :],
                                                          scalar=m.pair_w[:, slot, t:t + 1], in1=m.res[:, t, :],
                                                          op0=ALU.mult, op1=ALU.add)
                    if slot == 0:
                        steps.end(last)
                        steps.wait(dve)
                last.then_inc(summed, 1)
                if t:
                    normalise(t - 1)
            normalise(TT - 1)


def mixture(nc, m, A):
    with ExitStack() as mem:
        m.pair_w = mem.enter_context(nc.sbuf_tensor("pair_w", [P, 2, TT], F32))
        m.pair_row = mem.enter_context(nc.sbuf_tensor("pair_row", [P, 2, TT], I32))
        m.over_table = mem.enter_context(nc.sbuf_tensor("over_table", [1, OVER + 1], I32))
        m.hn_dram = nc.dram_tensor("normed_rows", (SEQ, D), F32).ap()
        m.row_list = nc.dram_tensor("row_list", (CAP * BLOCKS, 1), I32).ap()
        with nc.sbuf_tensor("hT2", [P, KT, SEQ], F32) as hT:
            norm_to_T(nc, m, "norm2", hT, gamma_row=A["norm2_g"], rows_out=m.hn_dram)
            route(nc, m, A, hT)
        experts(nc, m, A)
        combine(nc, m, A)


def project_second(nc, m, A, hT):
    with ExitStack() as mem:
        def sb(name, shape, dt=F32):
            return mem.enter_context(nc.sbuf_tensor(name, shape, dt))

        sem = m.sem
        SLOTS = 4
        PAD = max(WINDOWS)
        w = sb("qku_w", [P, SLOTS, KT, P])
        w_v = sb("v_w", [P, KT, ATT])
        w_g = sb("pool_group_w", [P, HT, P])
        edge = sb("pool_edge", [P, len(WINDOWS), PAD])
        u = sb("pool_u", [P, 2, PAD + SEQ])
        s = sb("pool_sums", [P, 2, PAD + SEQ])
        pooled = m.attT
        ps = mem.enter_context(nc.psum_tensor("qkvu_ps", [P, 4, 2, BANK], F32))
        w_in = [sem(f"qku_w_in{i}") for i in range(SLOTS)]
        v_in = sem("v_w_in")
        small_in = sem("pool_small_in")
        tile_mm = sem("qku_mm")
        tile_out = sem("qku_out")
        v_mm = sem("v_mm")
        v_out = sem("v_out")
        padded = sem("pool_padded")
        window = sem("pool_window")
        pooled_done = sem("pooled_done")
        group_mm = sem("pool_group_mm")
        steps = Steps(sem("pool_steps"))
        tiles = [3 * HT + c for c in range(HT)] + list(range(2 * HT))
        block = mem.enter_context(nc.Block())

        @block.sync
        def _(sp):
            weights = A["w_in_2"][0].rearrange("(k p) n -> p k n", p=P)
            sp.dma_start(m.bias_rows, A["rel_ext"].unsqueeze(1).to_broadcast([HEADS, P, EXT])).then_inc(m.bias_copied, 16)
            for n, c in enumerate(tiles):
                if n >= SLOTS:
                    sp.wait_ge(tile_mm, n - SLOTS + 1)
                sp.dma_start(w[:, n % SLOTS, :, :], weights[:, :, c * P:(c + 1) * P]).then_inc(w_in[n % SLOTS], 16)
                if n == SLOTS - 1:
                    sp.dma_start(edge[:], A["pool_edge"]).then_inc(small_in, 16)
                    sp.dma_start(w_g[:], A["w_pool_group_2"][0].rearrange("g c d -> c g d")).then_inc(small_in, 16)
                    sp.dma_start(w_v[:], weights[:, :, 2 * ATT:3 * ATT]).then_inc(v_in, 16)

        @block.tensor
        def _(pe):
            for n in range(len(tiles)):
                pe.wait_ge(w_in[n % SLOTS], 16 * (n // SLOTS + 1))
                if n >= 4:
                    pe.wait_ge(tile_out, n - 3)
                for half in range(2):
                    for k in range(KT):
                        last = nc.tensor.matmul(ps[:, n % 4, half, :], w[:, n % SLOTS, k, :],
                                                hT[:, k, half * BANK:(half + 1) * BANK],
                                                start=(k == 0), stop=(k == KT - 1))
                last.then_inc(tile_mm, 1)
            n_tiles = len(tiles)
            pe.wait_ge(v_in, 16)
            for t in range(TT):
                pe.wait_ge(tile_out, n_tiles - 3 + t // 2)
                for k in range(KT):
                    last = nc.tensor.matmul(ps[:, t // 2, t % 2, :], hT[:, k, t * P:(t + 1) * P], w_v[:, k, :],
                                            start=(k == 0), stop=(k == KT - 1))
                last.then_inc(v_mm, 1)
            pe.wait_ge(small_in, 32)
            for g in range(HT):
                pe.wait_ge(pooled_done, g + 1)
                pe.wait_ge(v_out, 2 * g + 2)
                for half in range(2):
                    last = nc.tensor.matmul(ps[:, g, half, :], w_g[:, g, :], pooled[:, g, half * BANK:(half + 1) * BANK],
                                            start=True, stop=True)
                last.then_inc(group_mm, 1)

        @block.scalar
        def _(act):
            for n, c in enumerate(tiles):
                act.wait_ge(tile_mm, n + 1)
                if n < HT:
                    act.wait_ge(padded, 1)
                    if n >= 2:
                        act.wait_ge(pooled_done, n - 1)
                    nc.scalar.activation(u[:, n % 2, PAD:].rearrange("p (h c) -> p h c", h=2), ps[:, n % 4, :, :],
                                         ACT.Copy).then_inc(tile_out, 1)
                else:
                    into = (m.qT if c < HT else m.kT)[:, c % HT, :]
                    nc.scalar.activation(into.rearrange("p (h c) -> p h c", h=2), ps[:, n % 4, :, :], ACT.Copy,
                                         scale=HEAD ** -0.5 if c < HT else 1.0).then_inc(tile_out, 1)
            for t in range(TT):
                act.wait_ge(v_mm, t + 1)
                nc.scalar.activation(m.v[:, t, :], ps[:, t // 2, t % 2, :], ACT.Copy).then_inc(v_out, 1)

        @block.gpsimd
        def _(pool):
            done = Steps(window)
            for g in range(HT):
                pool.wait_ge(tile_out, g + 1)
                if g:
                    pool.wait_ge(pooled_done, g)
                for i in range(g + 1):
                    src = u[:, g % 2, :] if i == 0 else s[:, (i - 1) % 2, :]
                    done.end(nc.gpsimd.tensor_tensor(s[:, i % 2, PAD:], src[:, PAD:], src[:, PAD - 2 ** i:PAD + SEQ - 2 ** i],
                                                     ALU.add))
                    done.wait(pool)
                if g == 0:
                    pool.wait_ge(small_in, 32)
                done.end(nc.gpsimd.tensor_tensor(s[:, g % 2, PAD:2 * PAD], s[:, g % 2, PAD:2 * PAD], edge[:, g, :],
                                                 ALU.mult))
                assert done.n == WINDOW_STEPS[g]

        @block.vector
        def _(dve):
            for a in (u, s):
                last = nc.vector.memset(a[:, :, 0:PAD], 0.0)
            last.then_inc(padded, 1)
            for g in range(HT):
                dve.wait_ge(window, WINDOW_STEPS[g])
                nc.vector.scalar_tensor_tensor(out=pooled[:, g, :], in0=s[:, g % 2, PAD:], scalar=1.0 / WINDOWS[g],
                                               in1=u[:, g % 2, PAD:], op0=ALU.mult, op1=ALU.subtract) \
                    .then_inc(pooled_done, 1)
            for g in range(HT):
                dve.wait_ge(group_mm, g + 1)
                nc.vector.tensor_scalar(m.poolT[:, g, :].rearrange("p (h c) -> p h c", h=2), ps[:, g, :, :],
                                        col(m.params, "pool_scale_2", g), None, ALU.mult)


WINDOW_STEPS = [sum(i + 2 for i in range(g + 1)) for g in range(HT)]


def band_attention(nc, m, A):
    with ExitStack() as mem:
        def sb(name, shape, dt=F32):
            return mem.enter_context(nc.sbuf_tensor(name, shape, dt))

        sem = m.sem
        bias = sb("bias", [P, HEADS, KEYS])
        score = sb("score", [P, 3, KEYS])
        prob = sb("prob", [P, 3, KEYS])
        top = sb("top_score", [P, TT * HEADS])
        ntop = sb("neg_top", [P, TT * HEADS])
        total = sb("total", [P, TT, HEADS])
        inv = sb("inv_total", [P, TT, HEADS])
        probT = sb("probT", [P, 2, KEY_TILES, P])
        att = sb("att", [P, 2, ATT])
        ps_s = mem.enter_context(nc.psum_tensor("score_ps", [P, 2, 2 * BANK], F32))
        ps_p = mem.enter_context(nc.psum_tensor("prob_ps", [P, 2 * BANK], F32))
        ps_o = mem.enter_context(nc.psum_tensor("att_ps", [P, BANK], F32))
        ps_t = mem.enter_context(nc.psum_tensor("attT_ps", [P, BANK], F32))
        bias_in = sem("bias_in")
        masked = sem("bias_masked")
        score_mm = sem("score_mm")
        score_out = sem("score_out")
        ntop_done = sem("ntop_done")
        exp_done = sem("exp_done")
        turned = sem("prob_turned")
        probT_done = sem("probT_done")
        pv_mm = sem("pv_mm")
        inv_done = sem("inv_done")
        att_done = sem("att_done")
        att_turned = sem("att_turned")
        attT_done = sem("attT_done")
        block = mem.enter_context(nc.Block())
        ITEMS = [(i, h) for i in range(TT) for h in range(HEADS)]
        N = len(ITEMS)

        def key_tiles(i):
            return min(i + 1, KEY_TILES)

        @block.sync
        def _(sp):
            sp.wait_ge(m.bias_copied, 16)
            for h in range(HEADS):
                rows = bass.AP(tensor=m.bias_rows.tensor, offset=h * P * EXT + P - 1, ap=[[EXT - 1, P], [1, KEYS]])
                sp.dma_start(bias[:, h, :], rows).then_inc(bias_in, 16)

        @block.gpsimd
        def _(pool):
            pool.wait_ge(bias_in, 16 * HEADS)
            nc.gpsimd.memset(bias[0:CHUNK, :, BAND:KEYS], NEG).then_inc(masked, 1)
            nc.gpsimd.memset(bias[CHUNK:P, :, 0:CHUNK], NEG).then_inc(masked, 1)

        @block.tensor
        def _(pe):
            def scores(n):
                i, h = ITEMS[n]
                rows = slice(HEAD * (h % 2), HEAD * (h % 2 + 1))
                width = key_tiles(i) * P
                first_key = (i + 1) * P - width
                if n >= 2:
                    pe.wait_ge(score_out, n - 1)
                for at in range(0, width, BANK):
                    n_keys = min(BANK, width - at)
                    last = nc.tensor.matmul(ps_s[:, n % 2, at:at + n_keys], m.qT[rows, h // 2, i * P:(i + 1) * P],
                                            m.kT[rows, h // 2, first_key + at:first_key + at + n_keys],
                                            start=True, stop=True)
                last.then_inc(score_mm, 1)

            def turn(n):
                i, h = ITEMS[n]
                pe.wait_ge(exp_done, n + 1)
                if n:
                    pe.wait_ge(probT_done, n)
                for j in range(key_tiles(i)):
                    last = nc.tensor.transpose(ps_p[:, j * P:(j + 1) * P], prob[:, n % 3, j * P:(j + 1) * P], m.ident[:])
                last.then_inc(turned, 1)

            def values(n):
                i, h = ITEMS[n]
                nk = key_tiles(i)
                pe.wait_ge(probT_done, n + 1)
                if h == 0 and i:
                    pe.wait_ge(att_done, i)
                for j in range(nk):
                    last = nc.tensor.matmul(ps_o[:, h * HEAD:(h + 1) * HEAD], probT[:, n % 2, j, :],
                                            m.v[:, i + 1 - nk + j, h * HEAD:(h + 1) * HEAD],
                                            start=(j == 0), stop=(j == nk - 1))
                last.then_inc(pv_mm, 1)

            def out(i):
                pe.wait_ge(att_done, i + 1)
                if i:
                    pe.wait_ge(attT_done, i)
                for c in range(HT):
                    last = nc.tensor.transpose(ps_t[:, c * P:(c + 1) * P], att[:, i % 2, c * P:(c + 1) * P], m.ident[:])
                last.then_inc(att_turned, 1)

            scores(0)
            scores(1)
            for n in range(N):
                if n + 2 < N:
                    scores(n + 2)
                turn(n)
                if n:
                    values(n - 1)
                if n % HEADS == 3 and n > HEADS:
                    out(n // HEADS - 1)
            values(N - 1)
            out(TT - 1)

        @block.scalar
        def _(act):
            def leave(n):
                nk = key_tiles(ITEMS[n][0])
                act.wait_ge(turned, n + 1)
                if n >= 2:
                    act.wait_ge(pv_mm, n - 1)
                nc.scalar.activation(probT[:, n % 2, 0:nk, :].rearrange("p j q -> p (j q)"), ps_p[:, 0:nk * P], ACT.Copy) \
                    .then_inc(probT_done, 1)

            for n, (i, h) in enumerate(ITEMS):
                width = key_tiles(i) * P
                act.wait_ge(ntop_done, n + 1)
                if n >= 3:
                    act.wait_ge(turned, n - 2)
                nc.scalar.activation(prob[:, n % 3, 0:width], score[:, n % 3, 0:width], ACT.Exp,
                                     bias=ntop[:, n:n + 1], accum_out=total[:, i, h:h + 1]).then_inc(exp_done, 1)
                if n:
                    leave(n - 1)
            leave(N - 1)

        @block.vector
        def _(dve):
            def head_out(i):
                dve.wait_ge(exp_done, (i + 1) * HEADS)
                nc.vector.reciprocal(inv[:, i, :], total[:, i, :]).then_inc(inv_done, 1)
                dve.wait_ge(inv_done, i + 1)
                dve.wait_ge(pv_mm, (i + 1) * HEADS)
                if i >= 2:
                    dve.wait_ge(att_turned, i - 1)
                nc.vector.tensor_tensor(att[:, i % 2, :].rearrange("p (h d) -> p h d", h=HEADS),
                                        ps_o[:].rearrange("p (h d) -> p h d", h=HEADS),
                                        inv[:, i, :].unsqueeze(2).to_broadcast([P, HEADS, HEAD]), ALU.mult) \
                    .then_inc(att_done, 1)

            def turned_out(i):
                dve.wait_ge(att_turned, i + 1)
                nc.vector.tensor_copy(m.attT[:, :, i * P:(i + 1) * P], ps_t[:].rearrange("p (c q) -> p c q", c=HT)) \
                    .then_inc(attT_done, 1)

            dve.wait_ge(masked, 2)
            for n, (i, h) in enumerate(ITEMS):
                width = key_tiles(i) * P
                dve.wait_ge(score_mm, n + 1)
                if n >= 3:
                    dve.wait_ge(exp_done, n - 2)
                nc.vector.tensor_tensor(score[:, n % 3, 0:width], ps_s[:, n % 2, 0:width],
                                        bias[:, h, KEYS - width:KEYS], ALU.add).then_inc(score_out, 1)
                dve.wait_ge(score_out, n + 1)
                nc.vector.tensor_reduce(top[:, n:n + 1], score[:, n % 3, 0:width], AX_X, ALU.max) \
                    .then_inc(m.top_done, 1)
                dve.wait_ge(m.top_done, n + 1)
                nc.vector.tensor_scalar(ntop[:, n:n + 1], top[:, n:n + 1], -1.0, None, ALU.mult).then_inc(ntop_done, 1)
                if n % HEADS == 2 and n > HEADS:
                    head_out(n // HEADS - 1)
                if n % HEADS == 5 and n > HEADS:
                    turned_out(n // HEADS - 1)
            head_out(TT - 1)
            turned_out(TT - 1)


def gated_mix(nc, m, A, hT):
    with ExitStack() as mem:
        def sb(name, shape, dt=F32):
            return mem.enter_context(nc.sbuf_tensor(name, shape, dt))

        sem = m.sem
        S = 2
        w_gate = sb("gates_w", [P, S, 2, KT, P])
        w_out = sb("branches_w", [P, S, 2, HT, P])
        gate = sb("gates", [P, S, 2, SEQ])
        part = sb("branch_parts", [P, S, 2, SEQ])
        ps_g = mem.enter_context(nc.psum_tensor("gates_ps", [P, 2, 2, BANK], F32))
        ps_y = mem.enter_context(nc.psum_tensor("branches_ps", [P, 2, 2, BANK], F32))
        w_in = [sem(f"gated_w_in{s}") for s in range(S)]
        tile_mm = sem("gated_tile_mm")
        gate_mm = sem("gates_mm")
        gate_out = sem("gates_out")
        branch_mm = sem("branches_mm")
        branch_out = sem("branches_out")
        mixed = sem("mixed")
        block = mem.enter_context(nc.Block())
        first_gate = (3 * ATT + ATT) // P

        @block.sync
        def _(sp):
            w2 = A["w_in_2"][0].rearrange("(k p) n -> p k n", p=P)
            outs = [A[n][0].rearrange("(k p) n -> p k n", p=P) for n in ("w_attn_out_2", "w_pool_out_2")]

            def load(s, d):
                for br in range(2):
                    sp.dma_start(w_gate[:, s, br, :, :], w2[:, :, bass.ds((d + (first_gate + br * KT)) * P, P)]) \
                        .then_inc(w_in[s], 16)
                    sp.dma_start(w_out[:, s, br, :, :], outs[br][:, :, bass.ds(d * P, P)]).then_inc(w_in[s], 16)

            for s in range(S):
                load(s, s)
            with sp.Fori(1, KT // S) as i:
                for s in range(S):
                    sp.wait_ge(branch_mm, (i * S + s - 1) * 2)
                    load(s, i * S + s)

        @block.tensor
        def _(pe):
            def feature_tile(s, d, use, first=False):
                pe.wait_ge(w_in[s], (use + 1) * 64)
                for br in range(2):
                    if not first:
                        pe.wait_ge(gate_out, (d - 1) * 2 + br + 1)
                    for half in range(2):
                        for k in range(KT):
                            last = nc.tensor.matmul(ps_g[:, br, half, :], w_gate[:, s, br, k, :],
                                                    hT[:, k, half * BANK:(half + 1) * BANK],
                                                    start=(k == 0), stop=(k == KT - 1))
                    last.then_inc(gate_mm, 1)
                for br, data in ((0, m.attT), (1, m.poolT)):
                    if not first:
                        pe.wait_ge(branch_out, (d - 1) * 2 + br + 1)
                    for half in range(2):
                        for k in range(HT):
                            last = nc.tensor.matmul(ps_y[:, br, half, :], w_out[:, s, br, k, :],
                                                    data[:, k, half * BANK:(half + 1) * BANK],
                                                    start=(k == 0), stop=(k == HT - 1))
                    last.then_inc(branch_mm, 1)

            for s in range(S):
                feature_tile(s, s, 0, first=(s == 0))
            with pe.Fori(1, KT // S) as i:
                for s in range(S):
                    feature_tile(s, i * S + s, i)

        @block.scalar
        def _(act):
            at, _ = COLS["b_gate_2"]

            def sigmoid(s, d, first=False):
                for br in range(2):
                    act.wait_ge(gate_mm, d * 2 + br + 1)
                    if not first:
                        act.wait_ge(mixed, d - 1)
                    nc.scalar.activation(gate[:, s, br, :].rearrange("p (h c) -> p h c", h=2), ps_g[:, br, :, :],
                                         ACT.Sigmoid, bias=m.params[:, bass.ds(d + (at + br * KT), 1)]) \
                        .then_inc(gate_out, 1)

            for s in range(S):
                sigmoid(s, s, first=True)
            with act.Fori(1, KT // S) as i:
                for s in range(S):
                    sigmoid(s, i * S + s)

        @block.vector
        def _(dve):
            with dve.Fori(0, KT // S) as i:
                for s in range(S):
                    d = i * S + s
                    for br in range(2):
                        dve.wait_ge(branch_mm, d * 2 + br + 1)
                        dve.wait_ge(gate_out, d * 2 + br + 1)
                        nc.vector.tensor_tensor(part[:, s, br, :].rearrange("p (h c) -> p h c", h=2),
                                                gate[:, s, br, :].rearrange("p (h c) -> p h c", h=2),
                                                ps_y[:, br, :, :], ALU.mult).then_inc(branch_out, 1)
                    dve.wait_ge(branch_out, d * 2 + 2)
                    nc.vector.tensor_tensor(m.mixT[:, bass.ds(d, 1), :].rearrange("p o c -> p (o c)"), part[:, s, 0, :],
                                            part[:, s, 1, :], ALU.add).then_inc(mixed, 1)


class PostNorm:

    def __init__(self, nc, m, mem, name):
        def sb(part, shape):
            return mem.enter_context(nc.sbuf_tensor(f"{name}_{part}", shape, F32))

        self.squares = sb("squares", [P, D])
        self.sums = sb("sums", [P, TT])
        self.rms = sb("rms", [P, TT])
        self.rstd = sb("rstd", [P, TT])
        self.scaled = sb("scaled", [P, 2, D])
        self.gamma = sb("gamma", [P, D])
        self.gamma_in = m.sem(f"{name}_gamma_in")
        self.squared = m.sem(f"{name}_squared")
        self.rms_done = m.sem(f"{name}_rms_done")
        self.rstd_done = m.sem(f"{name}_rstd_done")
        self.left_psum = m.sem(f"{name}_left_psum")
        self.added = m.sem(f"{name}_added")

    def scalar_part(self, nc, act, m, t, ps, product_done, count):
        act.wait_ge(product_done, count)
        if t:
            act.wait_ge(self.squared, t)
        nc.scalar.activation(self.squares[:].rearrange("p (h c) -> p h c", h=2), ps, ACT.Square,
                             accum_out=self.sums[:, t:t + 1]).then_inc(self.squared, 1)
        act.wait_ge(self.squared, t + 1)
        nc.scalar.activation(self.rms[:, t:t + 1], self.sums[:, t:t + 1], ACT.Sqrt, bias=m.eps[:], scale=1.0 / D) \
            .then_inc(self.rms_done, 1)

    def vector_part(self, nc, dve, m, t, ps):
        if t == 0:
            dve.wait_ge(self.gamma_in, 16)
        dve.wait_ge(self.rms_done, t + 1)
        nc.vector.reciprocal(self.rstd[:, t:t + 1], self.rms[:, t:t + 1]).then_inc(self.rstd_done, 1)
        dve.wait_ge(self.rstd_done, t + 1)
        nc.vector.scalar_tensor_tensor(out=self.scaled[:, t % 2, :].rearrange("p (h c) -> p h c", h=2), in0=ps,
                                       scalar=self.rstd[:, t:t + 1],
                                       in1=self.gamma[:].rearrange("p (h c) -> p h c", h=2),
                                       op0=ALU.mult, op1=ALU.mult).then_inc(self.left_psum, 1)
        dve.wait_ge(self.left_psum, t + 1)
        nc.vector.tensor_tensor(m.res[:, t, :], m.res[:, t, :], self.scaled[:, t % 2, :], ALU.add) \
            .then_inc(self.added, 1)


def mix_output(nc, m, A):
    with ExitStack() as mem:
        w = mem.enter_context(nc.sbuf_tensor("w_o_sb", [P, KT, D], F32))
        norm = PostNorm(nc, m, mem, "mix_post")
        ps = mem.enter_context(nc.psum_tensor("w_o_ps", [P, 4, 2, BANK], F32))
        w_in = m.sem("w_o_in")
        out_mm = m.sem("w_o_mm")
        block = mem.enter_context(nc.Block())

        @block.sync
        def _(sp):
            for k in range(KT):
                sp.dma_start(w[:, k, :], A["w_o_2"][0, k * P:(k + 1) * P, :]).then_inc(w_in, 16)
            sp.dma_start(norm.gamma[:], A["norm_mix_post_2"].to_broadcast([P, D])).then_inc(norm.gamma_in, 16)

        @block.tensor
        def _(pe):
            pe.wait_ge(w_in, 16 * KT)
            for t in range(TT):
                if t >= 4:
                    pe.wait_ge(norm.left_psum, t - 3)
                for half in range(2):
                    for k in range(KT):
                        last = nc.tensor.matmul(ps[:, t % 4, half, :], m.mixT[:, k, t * P:(t + 1) * P],
                                                w[:, k, half * BANK:(half + 1) * BANK],
                                                start=(k == 0), stop=(k == KT - 1))
                last.then_inc(out_mm, 1)

        @block.scalar
        def _(act):
            for t in range(TT):
                norm.scalar_part(nc, act, m, t, ps[:, t % 4, :, :], out_mm, t + 1)

        @block.vector
        def _(dve):
            for t in range(TT):
                norm.vector_part(nc, dve, m, t, ps[:, t % 4, :, :])


def ffn_up(nc, m, A, hT, prodT):
    with ExitStack() as mem:
        def sb(name, shape, dt=F32):
            return mem.enter_context(nc.sbuf_tensor(name, shape, dt))

        sem = m.sem
        S = 2
        w = sb("w_up_tiles", [P, S, 2, KT, P])
        conv = sb("ffn_conv", [P, S, 2, SEQ])
        ps = mem.enter_context(nc.psum_tensor("up_ps", [P, S, 2, 2, BANK], F32))
        w_in = [sem(f"w_up_tile_in{s}") for s in range(S)]
        mm = sem("ffn_up_mm")
        centre = sem("ffn_centre")
        taps = sem("ffn_taps")
        gelu = sem("ffn_gelu")
        prod = sem("ffn_prod")
        block = mem.enter_context(nc.Block())
        taps_at, bias_at = COLS["conv_w_2"][0], COLS["conv_b_2"][0]

        @block.sync
        def _(sp):
            weights = A["w_up_2"][0].rearrange("(k p) n -> p k n", p=P)

            def load(s, f):
                for part in range(2):
                    sp.dma_start(w[:, s, part, :, :], weights[:, :, bass.ds((f + part * FT) * P, P)]) \
                        .then_inc(w_in[s], 16)

            for s in range(S):
                load(s, s)
            with sp.Fori(1, FT // S) as i:
                for s in range(S):
                    sp.wait_ge(mm, (i * S + s - 1) * 2)
                    load(s, i * S + s)

        @block.tensor
        def _(pe):
            def tile(s, f, use, first=False):
                pe.wait_ge(w_in[s], (use + 1) * 32)
                for part in range(2):
                    if not first:
                        pe.wait_ge(taps, (f - S) * 4 + (2 * part + 2))
                    for half in range(2):
                        for k in range(KT):
                            last = nc.tensor.matmul(ps[:, s, part, half, :], w[:, s, part, k, :],
                                                    hT[:, k, half * BANK:(half + 1) * BANK],
                                                    start=(k == 0), stop=(k == KT - 1))
                    last.then_inc(mm, 1)

            for s in range(S):
                tile(s, s, 0, first=True)
            with pe.Fori(1, FT // S) as i:
                for s in range(S):
                    tile(s, i * S + s, i)

        @block.scalar
        def _(act):
            def tile(s, f, first=False):
                for part in range(2):
                    act.wait_ge(mm, f * 2 + part + 1)
                    if not first:
                        act.wait_ge(prod, f - 1)
                    nc.scalar.activation(conv[:, s, part, :].rearrange("p (h c) -> p h c", h=2), ps[:, s, part, :, :],
                                         ACT.Identity, bias=m.params[:, bass.ds(f + (bias_at + part * FT), 1)],
                                         scale=m.params[:, bass.ds(f + (taps_at + (4 + part) * FT), 1)]) \
                        .then_inc(centre, 1)
                act.wait_ge(taps, f * 4 + 4)
                nc.scalar.activation(conv[:, s, 1, :], conv[:, s, 1, :], ACT.Gelu_apprx_tanh).then_inc(gelu, 1)

            for s in range(S):
                tile(s, s, first=True)
            with act.Fori(1, FT // S) as i:
                for s in range(S):
                    tile(s, i * S + s)

        @block.vector
        def _(dve):
            with dve.Fori(0, FT // S) as i:
                for s in range(S):
                    f = i * S + s
                    for part in range(2):
                        dve.wait_ge(centre, f * 2 + part + 1)
                        raw = ps[:, s, part, :, :].rearrange("p h c -> p (h c)")
                        for back in (1, 2):
                            if back == 2:
                                dve.wait_ge(taps, f * 4 + (2 * part + 1))
                            into = conv[:, s, part, back:SEQ]
                            nc.vector.scalar_tensor_tensor(
                                out=into, in0=raw[:, 0:SEQ - back],
                                scalar=m.params[:, bass.ds(f + (taps_at + (2 * (2 - back) + part) * FT), 1)],
                                in1=into, op0=ALU.mult, op1=ALU.add).then_inc(taps, 1)
                    dve.wait_ge(gelu, f + 1)
                    nc.vector.tensor_tensor(prodT[:, bass.ds(f, 1), :].rearrange("p o c -> p (o c)"), conv[:, s, 0, :],
                                            conv[:, s, 1, :], ALU.mult).then_inc(prod, 1)


def ffn_down(nc, m, A, prodT):
    with ExitStack() as mem:
        SLOTS = 6
        QUAD = 4
        w = mem.enter_context(nc.sbuf_tensor("w_down_tiles", [P, SLOTS, D], F32))
        norm = PostNorm(nc, m, mem, "ffn_post")
        ps = mem.enter_context(nc.psum_tensor("down_ps", [P, QUAD, 2, BANK], F32))
        w_in = [m.sem(f"w_down_tile_in{i}") for i in range(SLOTS)]
        w_used = m.sem("w_down_used")
        stored = m.sem("stored")
        block = mem.enter_context(nc.Block())

        @block.sync
        def _(sp):
            sp.dma_start(norm.gamma[:], A["norm_ffn_post_2"].to_broadcast([P, D])).then_inc(norm.gamma_in, 16)
            for n in range(2 * FT):
                f = n % FT
                if n >= SLOTS:
                    sp.wait_ge(w_used, n - SLOTS + 1)
                sp.dma_start(w[:, n % SLOTS, :], A["w_down_2"][0, f * P:(f + 1) * P, :]).then_inc(w_in[n % SLOTS], 16)
            for t in range(TT):
                sp.wait_ge(norm.added, t + 1)
                sp.dma_start(A["out"][0, t * P:(t + 1) * P, :], m.res[:, t, :]).then_inc(stored, 16)
            sp.wait_ge(stored, 16 * TT)

        @block.tensor
        def _(pe):
            for n in range(2 * FT):
                turn, f = n // FT, n % FT
                pe.wait_ge(w_in[n % SLOTS], 16 * (n // SLOTS + 1))
                for q in range(QUAD):
                    t = turn * QUAD + q
                    if turn and f == 0:
                        pe.wait_ge(norm.left_psum, q + 1)
                    for half in range(2):
                        last = nc.tensor.matmul(ps[:, q, half, :], prodT[:, f, t * P:(t + 1) * P],
                                                w[:, n % SLOTS, half * BANK:(half + 1) * BANK],
                                                start=(f == 0), stop=(f == FT - 1))
                last.then_inc(w_used, 1)

        @block.scalar
        def _(act):
            for t in range(TT):
                norm.scalar_part(nc, act, m, t, ps[:, t % QUAD, :, :], w_used, (t // QUAD + 1) * FT)

        @block.vector
        def _(dve):
            for t in range(TT):
                norm.vector_part(nc, dve, m, t, ps[:, t % QUAD, :, :])


def second_block(nc, m, A):
    with ExitStack() as mem:
        def sb(name, shape):
            return mem.enter_context(nc.sbuf_tensor(name, shape, F32))

        m.bias_rows = nc.dram_tensor("bias_rows", (HEADS, P, EXT), F32).ap()
        m.bias_copied = m.sem("bias_copied")
        m.attT = sb("attT", [P, HT, SEQ])
        m.poolT = sb("poolT", [P, HT, SEQ])
        hT = sb("hT3", [P, KT, SEQ])
        norm_to_T(nc, m, "norm3", hT, gamma="norm_mix_pre_2")
        with nc.sbuf_tensor("qT", [P, HT, SEQ], F32) as m.qT, nc.sbuf_tensor("kT", [P, HT, SEQ], F32) as m.kT, \
                nc.sbuf_tensor("v", [P, TT, ATT], F32) as m.v:
            project_second(nc, m, A, hT)
            band_attention(nc, m, A)
        m.mixT = sb("mixT2", [P, KT, SEQ])
        gated_mix(nc, m, A, hT)
        mix_output(nc, m, A)
    with nc.sbuf_tensor("prodT", [P, FT, SEQ], F32) as prodT:
        with nc.sbuf_tensor("hT4", [P, KT, SEQ], F32) as hT:
            norm_to_T(nc, m, "norm4", hT, gamma="norm_ffn_pre_2")
            ffn_up(nc, m, A, hT, prodT)
        ffn_down(nc, m, A, prodT)


def build_program(nc, A):
    with ExitStack() as ctx:
        m = Shared(nc, ctx)
        with m.section(nc):
            first_mixer(nc, m, A)
        with m.section(nc):
            mixture(nc, m, A)
        with m.section(nc):
            second_block(nc, m, A)


class Shared:

    def __init__(self, nc, ctx):
        def sb(name, shape, dt=F32):
            return ctx.enter_context(nc.sbuf_tensor(name, shape, dt))

        self.sem = nc.alloc_semaphore
        self.params = sb("params", [P, N_COLS])
        self.ident = sb("ident", [P, P])
        self.ones = sb("ones", [P, P])
        self.inv_size = sb("inv_size", [P, HT])
        self.eps = sb("eps", [P, 1])
        self.res = sb("res", [P, TT, D])
        self.eps_set = self.sem("eps_set")
        self.y_dram = nc.dram_tensor("expert_rows", (ROWS, D), F32).ap()
        self.top_done = self.sem("top_done")
        self.x_in = self.sem("x_in")
        self.consts_set = self.sem("consts_set")

    @contextmanager
    def section(self, nc):
        whole, made = self.sem, []

        def sem(name):
            made.append(nc.alloc_semaphore(name))
            return made[-1]

        self.sem = sem
        yield
        self.sem = whole
        nc.clear_and_free_semaphores(made)
        nc.all_engine_barrier()


def _tables():
    j = np.arange(SEQ, dtype=np.float64)
    split = np.concatenate([j[0::2], j[1::2]])
    half = np.arange(HALF, dtype=np.float64) + 0.5
    angle = np.pi / SEQ * np.outer(split, half)
    trig = np.stack([np.cos(angle[:HALF]), np.cos(angle[HALF:]), np.sin(angle[:HALF]), np.sin(angle[HALF:])])
    back = trig.reshape(2, 2, HALF, HALF).transpose(1, 0, 3, 2) / SEQ
    whole = 2 * np.pi / SEQ * np.outer(split, np.arange(HALF, dtype=np.float64))
    scale = 1.0 / np.sqrt(SEQ * HEAD)
    dft = np.stack([np.cos(whole[:HALF]), -np.sin(whole[:HALF]), np.cos(whole[HALF:]), -np.sin(whole[HALF:])]) * scale
    d = np.arange(HEAD, dtype=np.float64)
    small = 2 * np.pi / HEAD * np.outer(d, d)
    pair = np.zeros((P, 2, P))
    for i in range(P // HEAD):
        s = slice(i * HEAD, (i + 1) * HEAD)
        pair[s, 0, s] = np.cos(small)
        pair[s, 1, s] = np.sin(small)
    heads = np.kron(np.eye(P // HEAD), np.full((HEAD, HEAD), 1.0 / HEAD))
    t = np.linspace(0.0, 1.0, SEQ, dtype=np.float32)
    w = np.float32(2.0 * np.pi / SEQ) * np.arange(SEQ, dtype=np.float32)
    f = np.linspace(1e-4, F_BANDS - 1, F_BANDS, dtype=np.float32)
    fw = (f[:, None] * w[None, :]).astype(np.float32)
    positions = np.concatenate([t[None, :], np.cos(fw), -np.sin(fw)])
    rates = np.abs(np.linspace(np.log(1e-2) / 1.5, np.log(1e-2) / 0.3, D_HYENA))
    decay = np.exp(-t[split.astype(np.int64)][:, None].astype(np.float64) * rates[None, :])
    count = np.minimum(np.arange(max(WINDOWS))[None, :] + 1, np.array(WINDOWS)[:, None])
    edge = np.broadcast_to(np.array(WINDOWS)[:, None] / count, (P, len(WINDOWS), max(WINDOWS)))
    before = np.triu(np.ones((P, P)), 1)
    out = dict(half_tables=trig, back_tables=back, dft_tables=dft, pair_table=pair, head_table=heads,
               positions=positions, decay=decay, pool_edge=edge, before=before,
               index_rows=np.stack([np.arange(EXPERTS) - 64, np.arange(EXPERTS)])[None],
               limits=CAP * np.arange(1, FULL_BLOCKS)[None, :])
    return {k: np.ascontiguousarray(v, dtype=np.float32) for k, v in out.items()}


def _laid_out(inputs):
    a = {k: np.asarray(v) for k, v in inputs.items()}
    out = _tables()
    for name in ("x", "w_in", "f_w_in", "f_w_mid", "f_w_out", "w_out", "norm2_g", "w_gate", "w_up", "w_down",
                 "w_in_2", "w_attn_out_2", "w_pool_group_2", "w_pool_out_2", "w_o_2", "norm_mix_post_2",
                 "w_up_2", "w_down_2", "norm_ffn_post_2"):
        out[name] = a[name]
    out["final_g"] = a["final_g"].reshape(1, D)

    def cols(v):
        return v.reshape(-1, P).T

    def short(v):
        return np.pad(v.T, ((0, P - v.shape[1]), (0, 0)))

    packed = {n: cols(a[n]) for n in COLS if n in a and n not in ("conv_w", "conv_w_2", "f_freq")}
    for n in ("conv_w", "conv_w_2"):
        packed[n] = a[n].reshape(3 * a[n].shape[2] // P, P).T
    packed["f_b"] = short(np.concatenate([a["f_b_in"], a["f_b_mid"][0]]))
    packed["f_freq"] = short(a["f_freq"][0])
    out["params"] = np.concatenate([packed[n] for n in COLS], axis=1)
    assert out["params"].shape == (P, N_COLS)
    out["w_router"] = np.concatenate([a["w_group"][0]] + [a["w_router"][0, g] for g in range(GROUPS)], axis=1)
    out["b_router"] = np.concatenate([a["b_group"][0], a["b_router"][0].reshape(-1)])[None, :]
    dist = np.clip(np.arange(EXT)[::-1] - (P - 1), -REL, REL) + REL
    out["rel_ext"] = a["rel_bias_2"][0][:, dist]
    return {k: np.ascontiguousarray(v) for k, v in out.items()}


def kernel(**inputs):
    import concourse.bacc as bacc
    from concourse.bass_utils import run_bass_kernel_spmd

    nc = bacc.Bacc("TRN2", target_bir_lowering=False, num_devices=1)
    arrays, A = {}, {}
    for name, a in _laid_out(inputs).items():
        arrays[f"in_{name}_dram"] = a
        A[name] = nc.dram_tensor(f"in_{name}_dram", a.shape, mybir.dt.from_np(a.dtype), kind="ExternalInput").ap()
    A["out"] = nc.dram_tensor("out_0_dram", (1, SEQ, D), F32, kind="ExternalOutput").ap()
    build_program(nc, A)
    r = run_bass_kernel_spmd(nc, [arrays], core_ids=[0])
    return r.results[0]["out_0_dram"]
```

```python
from contextlib import ExitStack, contextmanager

import numpy as np

import concourse.bass as bass
from concourse import mybir

ALU = mybir.AluOpType
ACT = mybir.ActivationFunctionType
AX_X = mybir.AxisListType.X
F32 = mybir.dt.float32
I32 = mybir.dt.int32
F32R = mybir.dt.float32r

P = 128
SEQ = 1024
D = 1024
TT = SEQ // P
KT = D // P
BANK = 512
EPS = 1e-6

D_HYENA = 512
HT = D_HYENA // P
HEAD = 64
F_EMB = 33
F_BANDS = (F_EMB - 1) // 2
F_ORDER = 64
HALF = SEQ // 2
JT = HALF // P
TWO_PI = 2.0 * np.pi

GROUPS = 4
PER_GROUP = 8
EXPERTS = GROUPS * PER_GROUP
D_EXPERT = 512
CAP = 96
OVER = 2 * SEQ // (CAP + 1)
FULL_BLOCKS = (SEQ + CAP - 1) // CAP
BLOCKS = EXPERTS + OVER
ROWS = BLOCKS * CAP

HEADS = 8
ATT = HEADS * HEAD
CHUNK = 64
BAND = 9 * CHUNK
KEYS = BAND + CHUNK
KEY_TILES = KEYS // P
REL = 256
EXT = P + KEYS - 1
WINDOWS = (2, 4, 8, 16)
D_FF = 2816
FT = D_FF // P
NEG = -1e30
ROUND = 1.5 * 2.0 ** 23
TWO_PI_HIGH = 6.28125
TWO_PI_LOW = TWO_PI - TWO_PI_HIGH
PI_BELOW = 3.1415925

COLS = {}
_at = 0
for _name, _n in (("norm1_g", KT), ("conv_w", 3 * 3 * HT), ("conv_b", 3 * HT), ("f_bias", HT), ("mix_g", KT),
                  ("norm_mix_pre_2", KT), ("b_gate_2", 2 * KT), ("pool_scale_2", HT), ("norm_ffn_pre_2", KT),
                  ("conv_w_2", 3 * 2 * FT), ("conv_b_2", 2 * FT), ("f_b", 3), ("f_freq", 3)):
    COLS[_name] = (_at, _n)
    _at += _n
N_COLS = _at


def col(params, name, i, rows=P):
    at, n = COLS[name]
    assert 0 <= i < n
    return params[0:rows, at + i:at + i + 1]


class Steps:

    def __init__(self, sem):
        self.sem = sem
        self.n = 0

    def end(self, instruction):
        self.n += 1
        instruction.then_inc(self.sem, 1)

    def wait(self, engine):
        engine.wait_ge(self.sem, self.n)


def product(nc, out, w, x, start, stop):
    (w_high, w_rest), (x_high, x_rest) = w, x
    nc.tensor.matmul(out, w_high, x_high, start=start, stop=False)
    nc.tensor.matmul(out, w_high, x_rest, start=False, stop=False)
    return nc.tensor.matmul(out, w_rest, x_high, start=False, stop=stop)


class SplitRing:

    def __init__(self, nc, m, mem, name, slots, shape, raw):
        self.nc = nc
        self.raw = raw
        self.high_part = mem.enter_context(nc.sbuf_tensor(f"{name}_high", [P, slots] + shape, F32R))
        self.rest_part = mem.enter_context(nc.sbuf_tensor(f"{name}_rest", [P, slots] + shape, F32R))
        self.raw_in = [m.sem(f"{name}_raw_in{s}") for s in range(slots)]
        self.high_done = [m.sem(f"{name}_high_done{s}") for s in range(slots)]
        self.rest_done = [m.sem(f"{name}_rest_done{s}") for s in range(slots)]
        self.used = [m.sem(f"{name}_used{s}") for s in range(slots)]

    def load(self, engine, s, use, source, first=False):
        if not first:
            engine.wait_ge(self.rest_done[s], use)
        engine.dma_start(self.raw[s], source).then_inc(self.raw_in[s], 16)

    def high(self, act, s, use, first=False):
        act.wait_ge(self.raw_in[s], (use + 1) * 16)
        if not first:
            act.wait_ge(self.used[s], use)
        self.nc.scalar.activation(self.high_part[:, s], self.raw[s], ACT.Copy).then_inc(self.high_done[s], 1)

    def rest(self, dve, s, use):
        dve.wait_ge(self.high_done[s], use + 1)
        self.nc.vector.tensor_tensor(self.rest_part[:, s], self.raw[s], self.high_part[:, s].bitcast(F32), ALU.subtract) \
            .then_inc(self.rest_done[s], 1)

    def arrived(self, pe, s, use):
        pe.wait_ge(self.rest_done[s], use + 1)

    def parts(self, s, *at):
        return self.high_part[(slice(None), s) + at], self.rest_part[(slice(None), s) + at]


class WideProduct:

    def __init__(self, nc, m, mem, name, xT, weight, raw, ps):
        def sb(part, shape):
            return mem.enter_context(nc.sbuf_tensor(f"{name}_{part}", shape, F32R))

        self.nc, self.xT, self.weight, self.raw, self.ps = nc, xT, weight, raw, ps
        self.w = sb("w_high", [P, KT, D]), sb("w_rest", [P, KT, D])
        self.x = sb("x_high", [P, 2, KT, P]), sb("x_rest", [P, 2, KT, P])
        self.raw_in = [m.sem(f"{name}_raw_in{s}") for s in range(2)]
        self.w_high = m.sem(f"{name}_w_high_done")
        self.w_rest = m.sem(f"{name}_w_rest_done")
        self.x_high = m.sem(f"{name}_x_high_done")
        self.x_rest = m.sem(f"{name}_x_rest_done")
        self.done = m.sem(f"{name}_tile_done")

    def load(self, engine):
        for k in range(KT):
            if k >= 2:
                engine.wait_ge(self.w_rest, k - 1)
            engine.dma_start(self.raw[k % 2], self.weight[k * P:(k + 1) * P, :]).then_inc(self.raw_in[k % 2], 16)

    def weight_high(self, act, k):
        act.wait_ge(self.raw_in[k % 2], 16 * (k // 2 + 1))
        self.nc.scalar.activation(self.w[0][:, k, :], self.raw[k % 2], ACT.Copy).then_inc(self.w_high, 1)

    def weight_rest(self, dve, k):
        dve.wait_ge(self.w_high, k + 1)
        self.nc.vector.tensor_tensor(self.w[1][:, k, :], self.raw[k % 2], self.w[0][:, k, :].bitcast(F32),
                                     ALU.subtract).then_inc(self.w_rest, 1)

    def tile_high(self, act, t):
        if t >= 2:
            act.wait_ge(self.done, t - 1)
        self.nc.scalar.activation(self.x[0][:, t % 2, :, :], self.xT[:, :, t * P:(t + 1) * P], ACT.Copy) \
            .then_inc(self.x_high, 1)

    def tile_rest(self, dve, t):
        dve.wait_ge(self.x_high, t + 1)
        self.nc.vector.tensor_tensor(self.x[1][:, t % 2, :, :], self.xT[:, :, t * P:(t + 1) * P],
                                     self.x[0][:, t % 2, :, :].bitcast(F32), ALU.subtract).then_inc(self.x_rest, 1)

    def tile_product(self, pe, t, free, count):
        pe.wait_ge(self.x_rest, t + 1)
        if t >= 4:
            pe.wait_ge(free, count)
        for k in range(KT):
            if t == 0:
                pe.wait_ge(self.w_rest, k + 1)
            for half in range(2):
                cols = slice(half * BANK, (half + 1) * BANK)
                last = product(self.nc, self.ps[:, t % 4, half, :], (self.x[0][:, t % 2, k, :], self.x[1][:, t % 2, k, :]),
                               (self.w[0][:, k, cols], self.w[1][:, k, cols]), start=(k == 0), stop=(k == KT - 1))
        last.then_inc(self.done, 1)


def filter_spectrum(nc, m, A):
    with ExitStack() as mem:
        def sb(name, shape, dt=F32):
            return mem.enter_context(nc.sbuf_tensor(name, shape, dt))

        sem = m.sem
        pos = sb("pos", [F_EMB, SEQ])
        f_w_in = sb("f_w_in", [F_EMB, F_ORDER])
        f_w_mid = sb("f_w_mid", [F_ORDER, 2, F_ORDER])
        f_w_out = sb("f_w_out", [F_ORDER, 2 * D_HYENA])
        arg = sb("arg", [F_ORDER, SEQ])
        turns = sb("turns", [F_ORDER, SEQ])
        hid = sb("hid", [F_ORDER, 2, SEQ])
        decay = sb("decay", [P, 2 * JT, D_HYENA])
        lag_sum = sb("lag_sum", [P, 2, JT, D_HYENA])
        lag_dif = sb("lag_dif", [P, 2, JT, D_HYENA])
        taps = sb("taps", [P, 2, 2, D_HYENA])
        sizes = sb("sizes", [P, 2, 2, D_HYENA])
        size = sb("size", [P, D_HYENA])
        table = sb("filter_table", [P, 4, HALF])
        even_part = sb("even_part", [P, JT, BANK])
        ps = mem.enter_context(nc.psum_tensor("filter_ps", [P, 8, BANK], F32))

        w_in = sem("filter_weights_in")
        decay_in = sem("decay_in")
        tab_in = [sem(f"filter_table_in{i}") for i in range(4)]
        tab_used = sem("filter_table_used")
        mlp_mm = sem("mlp_mm")
        mlp_arg = sem("mlp_arg")
        mlp_act = sem("mlp_act")
        taps_mm = sem("taps_mm")
        taps_read = sem("taps_read")
        taps_set = sem("taps_set")
        lags_done = sem("lags_done")
        abs_done = sem("abs_done")
        size_step = sem("size_step")
        norm_mm = sem("norm_mm")
        norm_done = sem("norm_done")
        even_kept = sem("even_kept")
        spec_done = sem("spec_done")
        steps = Steps(sem("filter_steps"))
        block = mem.enter_context(nc.Block())

        @block.sync
        def _(sp):
            sp.dma_start(pos[:], A["positions"]).then_inc(w_in, 16)
            sp.dma_start(f_w_in[:], A["f_w_in"][0]).then_inc(w_in, 16)
            sp.dma_start(f_w_mid[:], A["f_w_mid"][0].rearrange("l k n -> k l n")).then_inc(w_in, 16)
            sp.dma_start(m.params[:], A["params"]).then_inc(w_in, 16)
            sp.dma_start(f_w_out[:], A["f_w_out"][0]).then_inc(w_in, 16)
            sp.dma_start(decay[:], A["decay"].rearrange("(n p) c -> p n c", p=P)).then_inc(decay_in, 16)
            for n in range(4 * JT):
                if n >= 4:
                    sp.wait_ge(tab_used, n - 3)
                sp.dma_start(table[:, n % 4, :], A["half_tables"][n // JT, (n % JT) * P:(n % JT + 1) * P, :]) \
                    .then_inc(tab_in[n % 4], 16)
                if n == 3:
                    for t in range(TT):
                        sp.dma_start(m.res[:, t, :], A["x"][0, t * P:(t + 1) * P, :]).then_inc(m.x_in, 16)

        @block.gpsimd
        def _(pool):
            nc.gpsimd.memset(m.ident[:], 0.0).then_inc(m.consts_set, 1)
            nc.gpsimd.memset(m.ones[:], 1.0).then_inc(m.consts_set, 1)
            pool.wait_ge(m.consts_set, 2)
            nc.gpsimd.affine_select(out=m.ident[:], in_=m.ident[:], compare_op=ALU.not_equal, fill=1.0, base=0,
                                    pattern=[[-1, P]], channel_multiplier=1).then_inc(m.consts_set, 1)
            nc.gpsimd.memset(size[:], 0.0).then_inc(size_step, 1)
            for n in range(2 * JT):
                pool.wait_ge(abs_done, n + 1)
                for way in range(2):
                    pool.wait_ge(size_step, 2 * n + way + 1)
                    nc.gpsimd.tensor_tensor(size[:], size[:], sizes[:, n % 2, way, :], ALU.add).then_inc(size_step, 1)

        @block.tensor
        def _(pe):
            pe.wait_ge(w_in, 80)
            for layer in range(3):
                if layer:
                    pe.wait_ge(mlp_act, layer)
                for n in range(2):
                    if layer == 0:
                        w, data = f_w_in[:], pos[:, n * BANK:(n + 1) * BANK]
                    else:
                        w, data = f_w_mid[:, layer - 1, :], hid[:, (layer - 1) % 2, n * BANK:(n + 1) * BANK]
                    last = nc.tensor.matmul(ps[0:F_ORDER, n, :], w, data, start=True, stop=True)
                last.then_inc(mlp_mm, 1)
            pe.wait_ge(mlp_act, 3)
            for n in range(2 * JT):
                par, a = n // JT, n % JT
                if n >= 2:
                    pe.wait_ge(taps_read, n - 1)
                for way in range(2):
                    last = nc.tensor.matmul(ps[:, 2 + 2 * (n % 2) + way, :],
                                            hid[:, 0, 2 * P * a + par:2 * P * (a + 1):2],
                                            f_w_out[:, way * BANK:(way + 1) * BANK], start=True, stop=True)
                last.then_inc(taps_mm, 1)
            pe.wait_ge(size_step, 2 * 2 * JT + 1)
            pe.wait_ge(m.consts_set, 3)
            for c in range(HT):
                last = nc.tensor.matmul(ps[:, 6, c:c + 1], size[:, c * P:(c + 1) * P], m.ones[:, 0:1],
                                        start=True, stop=True)
            last.then_inc(norm_mm, 1)
            pe.wait_ge(lags_done, 2 * JT)
            pe.wait_ge(norm_done, 1)
            for g in range(4):
                if g >= 2:
                    pe.wait_ge(spec_done if g % 2 else even_kept, 1)
                data = lag_sum if g < 2 else lag_dif
                for a in range(JT):
                    n = g * JT + a
                    pe.wait_ge(tab_in[n % 4], 16 * (n // 4 + 1))
                    for f in range(JT):
                        last = nc.tensor.matmul(ps[:, 4 * (g % 2) + f, :], table[:, n % 4, f * P:(f + 1) * P],
                                                data[:, g % 2, a, :], start=(a == 0), stop=(a == JT - 1))
                    last.then_inc(tab_used, 1)

        @block.scalar
        def _(act):
            for layer in range(3):
                act.wait_ge(mlp_arg, layer + 1)
                nc.scalar.activation(hid[:, layer % 2, :], arg[:], ACT.Sin).then_inc(mlp_act, 1)
            for n in range(2 * JT):
                act.wait_ge(taps_set, n + 1)
                if n >= 2:
                    act.wait_ge(size_step, 2 * (n - 1) + 1)
                nc.scalar.activation(sizes[:, n % 2, :, :], taps[:, n % 2, :, :], ACT.Abs).then_inc(abs_done, 1)
            for g in (0, 2):
                act.wait_ge(tab_used, (g + 1) * JT)
                if g:
                    act.wait_ge(spec_done, 1)
                nc.scalar.activation(even_part[:], ps[:, 0:4, :], ACT.Copy).then_inc(even_kept, 1)

        @block.vector
        def _(dve):
            nc.vector.memset(m.eps[:], EPS).then_inc(m.eps_set, 1)
            for layer in range(3):
                dve.wait_ge(mlp_mm, layer + 1)
                if layer == 0:
                    dve.wait_ge(w_in, 80)
                else:
                    dve.wait_ge(mlp_act, layer)
                steps.end(nc.vector.tensor_scalar(arg[:].rearrange("p (n c) -> p n c", n=2), ps[0:F_ORDER, 0:2, :],
                                                  col(m.params, "f_b", layer, F_ORDER),
                                                  col(m.params, "f_freq", layer, F_ORDER), ALU.add, ALU.mult))
                steps.wait(dve)
                steps.end(nc.vector.tensor_scalar(turns[:], arg[:], 1.0 / TWO_PI, ROUND, ALU.mult, ALU.add))
                steps.wait(dve)
                steps.end(nc.vector.tensor_scalar(turns[:], turns[:], -ROUND, None, ALU.add))
                for part in (TWO_PI_HIGH, TWO_PI_LOW):
                    steps.wait(dve)
                    steps.end(nc.vector.scalar_tensor_tensor(out=arg[:], in0=turns[:], scalar=-part, in1=arg[:],
                                                             op0=ALU.mult, op1=ALU.add))
                steps.wait(dve)
                nc.vector.tensor_scalar(arg[:], arg[:], PI_BELOW, -PI_BELOW, ALU.min, ALU.max).then_inc(mlp_arg, 1)
            dve.wait_ge(decay_in, 16)
            for n in range(2 * JT):
                par, a = n // JT, n % JT
                dve.wait_ge(taps_mm, n + 1)
                if n >= 2:
                    dve.wait_ge(abs_done, n - 1)
                for way in range(2):
                    last = nc.vector.tensor_tensor(taps[:, n % 2, way, :], ps[:, 2 + 2 * (n % 2) + way, :],
                                                   decay[:, n, :], ALU.mult)
                last.then_inc(taps_read, 1)
                dve.wait_ge(taps_read, n + 1)
                if n == 0:
                    steps.end(nc.vector.memset(taps[0:1, 0, 1, :], 0.0))
                    steps.wait(dve)
                nc.vector.tensor_tensor(lag_sum[:, par, a, :], taps[:, n % 2, 0, :], taps[:, n % 2, 1, :], ALU.add).then_inc(taps_set, 1)
                nc.vector.tensor_tensor(lag_dif[:, par, a, :], taps[:, n % 2, 0, :], taps[:, n % 2, 1, :],
                                        ALU.subtract).then_inc(lags_done, 1)
            dve.wait_ge(norm_mm, 1)
            nc.vector.reciprocal(m.inv_size[:], ps[:, 6, 0:HT]).then_inc(norm_done, 1)
            for trig in range(2):
                dve.wait_ge(even_kept, trig + 1)
                dve.wait_ge(tab_used, (2 * trig + 2) * JT)
                nc.vector.tensor_tensor(m.K[:, trig, 0, :, :], even_part[:], ps[:, 4:8, :], ALU.add)
                nc.vector.tensor_tensor(m.K[:, trig, 1, :, :], even_part[:], ps[:, 4:8, :], ALU.subtract) \
                    .then_inc(spec_done, 1)


def norm_to_T(nc, m, name, hT, gamma=None, gamma_row=None, rows_out=None, x_ready=None, res_out=None):
    split = gamma is not None
    with ExitStack() as mem:
        def sb(part, shape, dt=F32):
            return mem.enter_context(nc.sbuf_tensor(f"{name}_{part}", shape, dt))

        def sem(part):
            return m.sem(f"{name}_{part}")

        sums = sb("sums", [P, TT])
        rms = sb("rms", [P, TT])
        rstd = sb("rstd", [P, TT])
        scaled = sb("scaled", [P, 2, D])
        squares = sb("squares", [P, D])
        ps = mem.enter_context(nc.psum_tensor(f"{name}_ps", [P, 2, KT, P], F32))
        summed = sem("summed")
        rms_done = sem("rms_done")
        rstd_done = sem("rstd_done")
        scaled_done = sem("scaled_done")
        turned = sem("turned")
        out_done = sem("out_done")
        if split:
            full = sb("full", [P, 2, KT, P])
            full_done = sem("full_done")
            high_done = sem("high_done")
        else:
            g_row = sb("gamma_row", [P, D])
            g_in = sem("gamma_in")
            stored = [sem(f"stored{i}") for i in range(2)]
        kept = sem("res_kept")
        block = mem.enter_context(nc.Block())

        @block.scalar
        def _(act):
            def leave(t):
                if split:
                    act.wait_ge(full_done, t + 1)
                    nc.scalar.activation(hT[0][:, :, t * P:(t + 1) * P], full[:, t % 2, :, :], ACT.Copy) \
                        .then_inc(high_done, 1)
                else:
                    act.wait_ge(turned, t + 1)
                    nc.scalar.activation(hT[:, :, t * P:(t + 1) * P], ps[:, t % 2, :, :], ACT.Copy) \
                        .then_inc(out_done, 1)

            act.wait_ge(m.eps_set, 1)
            if x_ready is not None:
                act.wait_ge(x_ready, 16 * TT)
            for t in range(TT):
                if t:
                    act.wait_ge(summed, t)
                nc.scalar.activation(squares[:], m.res[:, t, :], ACT.Square, accum_out=sums[:, t:t + 1]) \
                    .then_inc(summed, 1)
                act.wait_ge(summed, t + 1)
                nc.scalar.activation(rms[:, t:t + 1], sums[:, t:t + 1], ACT.Sqrt, bias=m.eps[:], scale=1.0 / D) \
                    .then_inc(rms_done, 1)
                if t:
                    leave(t - 1)
            leave(TT - 1)

        @block.gpsimd
        def _(pool):
            if split:
                for t in range(TT):
                    pool.wait_ge(rstd_done, t + 1)
                    if t >= 2:
                        pool.wait_ge(turned, t - 1)
                    nc.gpsimd.tensor_scalar(scaled[:, t % 2, :], m.res[:, t, :], rstd[:, t:t + 1], None, ALU.mult) \
                        .then_inc(scaled_done, 1)

        @block.vector
        def _(dve):
            def turn_out(t):
                dve.wait_ge(turned, t + 1)
                if t >= 2:
                    dve.wait_ge(out_done, t - 1)
                at, _ = COLS[gamma]
                scale = m.params[:, at:at + KT].unsqueeze(2).to_broadcast([P, KT, P])
                nc.vector.tensor_tensor(full[:, t % 2, :, :], ps[:, t % 2, :, :], scale, ALU.mult).then_inc(full_done, 1)

            def rest(t):
                dve.wait_ge(high_done, t + 1)
                here = slice(t * P, (t + 1) * P)
                nc.vector.tensor_tensor(hT[1][:, :, here], full[:, t % 2, :, :], hT[0][:, :, here].bitcast(F32),
                                        ALU.subtract).then_inc(out_done, 1)

            for t in range(TT):
                dve.wait_ge(rms_done, t + 1)
                nc.vector.reciprocal(rstd[:, t:t + 1], rms[:, t:t + 1]).then_inc(rstd_done, 1)
                if split:
                    if t >= 1:
                        turn_out(t - 1)
                    if t >= 2:
                        rest(t - 2)
                else:
                    dve.wait_ge(rstd_done, t + 1)
                    if t == 0:
                        dve.wait_ge(g_in, 16)
                    if t >= 2:
                        dve.wait_ge(turned, t - 1)
                        dve.wait_ge(stored[t % 2], 16 * (t // 2))
                    nc.vector.scalar_tensor_tensor(out=scaled[:, t % 2, :], in0=m.res[:, t, :],
                                                   scalar=rstd[:, t:t + 1], in1=g_row[:], op0=ALU.mult,
                                                   op1=ALU.mult).then_inc(scaled_done, 1)
            if split:
                turn_out(TT - 1)
                rest(TT - 2)
                rest(TT - 1)

        @block.tensor
        def _(pe):
            for t in range(TT):
                pe.wait_ge(scaled_done, t + 1)
                if t >= 2:
                    pe.wait_ge(full_done if split else out_done, t - 1)
                for k in range(KT):
                    last = nc.tensor.transpose(ps[:, t % 2, k, :], scaled[:, t % 2, k * P:(k + 1) * P], m.ident[:])
                last.then_inc(turned, 1)

        @block.sync
        def _(sp):
            if res_out is not None:
                sp.dma_start(res_out.rearrange("(t p) d -> p t d", p=P), m.res[:]).then_inc(kept, 16)
                sp.wait_ge(kept, 16)
            if not split:
                sp.dma_start(g_row[:], gamma_row.to_broadcast([P, D])).then_inc(g_in, 16)
                for t in range(TT):
                    sp.wait_ge(scaled_done, t + 1)
                    sp.dma_start(rows_out[t * P:(t + 1) * P, :], scaled[:, t % 2, :]).then_inc(stored[t % 2], 16)
                for s in range(2):
                    sp.wait_ge(stored[s], 16 * TT // 2)


def project_first(nc, m, A, hT):
    with ExitStack() as mem:
        sem = m.sem
        S = 2
        COUNT = 4 * HT
        ring = SplitRing(nc, m, mem, "proj_w", S, [KT, P],
                         [m.res[:, s, :].rearrange("p (k c) -> p k c", k=KT) for s in range(S)])
        conv = m.res[:, S:S + 2, :]
        zero = m.res[0:CAP, S + 2, :]
        ps = mem.enter_context(nc.psum_tensor("proj_ps", [P, 4, 2, BANK], F32))
        zero_set = sem("zero_set")
        rows_blank = sem("rows_blank")
        centre = sem("proj_centre")
        proj_out = sem("proj_out")
        steps = Steps(sem("proj_steps"))
        block = mem.enter_context(nc.Block())

        def tile_target(c):
            return (m.mixT[:, c % HT, :], m.zT[:, c % HT, :], conv[:, c % 2, :])[c // HT]

        @block.sync
        def _(sp):
            weights = A["w_in"][0].rearrange("(k p) n -> p k n", p=P)
            for s in range(S):
                ring.load(sp, s, 0, weights[:, :, s * P:(s + 1) * P], first=True)
            with sp.Fori(1, COUNT // S) as r:
                for s in range(S):
                    ring.load(sp, s, r, weights[:, :, bass.ds((r * S + s) * P, P)])

        @block.gpsimd
        def _(pool):
            nc.gpsimd.memset(zero, 0.0).then_inc(zero_set, 1)
            pool.wait_ge(zero_set, 1)
            for b in range(EXPERTS, BLOCKS):
                pool.dma_start(m.y_dram[b * CAP:(b + 1) * CAP, :], zero).then_inc(rows_blank, 16)
            pool.wait_ge(rows_blank, 16 * OVER)

        @block.tensor
        def _(pe):
            def channel_tile(s, q, use, free):
                ring.arrived(pe, s, use)
                if free is not None:
                    pe.wait_ge(proj_out, free)
                for half in range(2):
                    cols = slice(half * BANK, (half + 1) * BANK)
                    for k in range(KT):
                        last = product(nc, ps[:, q, half, :], ring.parts(s, k), (hT[0][:, k, cols], hT[1][:, k, cols]),
                                       start=(k == 0), stop=(k == KT - 1))
                last.then_inc(ring.used[s], 1)

            for q in range(4):
                channel_tile(q % S, q, q // S, None)
            with pe.Fori(1, COUNT // 4) as r:
                for q in range(4):
                    channel_tile(q % S, q, r * 2 + q // S, (r - 1) * 4 + q + 1)

        @block.scalar
        def _(act):
            for s in range(S):
                ring.high(act, s, 0, first=True)
            for c in range(COUNT):
                act.wait_ge(ring.used[c % S], c // S + 1)
                if c + S < COUNT:
                    ring.high(act, c % S, c // S + 1)
                if c < 3 * HT:
                    if c >= 2 * HT + 2:
                        act.wait_ge(proj_out, c - 1)
                    nc.scalar.activation(tile_target(c).rearrange("p (h c) -> p h c", h=2), ps[:, c % 4, :, :],
                                         ACT.Identity, bias=col(m.params, "conv_b", c),
                                         scale=col(m.params, "conv_w", 3 * HT + c)).then_inc(centre, 1)

        @block.vector
        def _(dve):
            for s in range(S):
                ring.rest(dve, s, 0)
            for c in range(COUNT):
                if c + S < COUNT:
                    ring.rest(dve, c % S, c // S + 1)
                dve.wait_ge(ring.used[c % S], c // S + 1)
                raw = ps[:, c % 4, :, :].rearrange("p h c -> p (h c)")
                if c >= 3 * HT:
                    nc.vector.tensor_copy(m.mixT[:, c - 2 * HT, :], raw).then_inc(proj_out, 1)
                    continue
                into = tile_target(c)
                dve.wait_ge(centre, c + 1)
                steps.end(nc.vector.scalar_tensor_tensor(out=into[:, 1:SEQ], in0=raw[:, 0:SEQ - 1],
                                                         scalar=col(m.params, "conv_w", c), in1=into[:, 1:SEQ],
                                                         op0=ALU.mult, op1=ALU.add))
                steps.wait(dve)
                last = nc.vector.scalar_tensor_tensor(out=into[:, 0:SEQ - 1], in0=raw[:, 1:SEQ],
                                                      scalar=col(m.params, "conv_w", 2 * 3 * HT + c),
                                                      in1=into[:, 0:SEQ - 1], op0=ALU.mult, op1=ALU.add)
                if c >= 2 * HT:
                    steps.end(last)
                    steps.wait(dve)
                    last = nc.vector.tensor_tensor(m.zT[:, c % HT, :], m.zT[:, c % HT, :], conv[:, c % 2, :], ALU.mult)
                last.then_inc(proj_out, 1)


def transform_mixes(nc, m, A):
    with ExitStack() as mem:
        def sb(name, shape, dt=F32):
            return mem.enter_context(nc.sbuf_tensor(name, shape, dt))

        sem = m.sem
        SLOTS = 4
        pair = sb("pair", [P, 2 * P])
        znat = sb("znat", [P, 2 * JT, D_HYENA])
        U = sb("U", [P, 2, 2, JT, BANK])
        even_part = sb("u_even_part", [P, JT, BANK])
        chan = sb("chan", [P, JT, HT, 2 * P])
        table = sb("mix_table", [P, SLOTS, HALF])
        ps = mem.enter_context(nc.psum_tensor("mix_ps", [P, 8, BANK], F32))

        pair_in = sem("pair_in")
        tab_in = [sem(f"mix_table_in{i}") for i in range(SLOTS)]
        tab_used = sem("mix_table_used")
        z_turned = sem("z_turned")
        z_kept = sem("z_kept")
        even_kept = sem("u_even_kept")
        u_done = sem("u_done")
        chan_mm = sem("chan_mm")
        chan_kept = sem("chan_kept")
        g_done = sem("g_done")
        four_even = sem("four_even")
        four_done = sem("four_done")
        bias_done = sem("bias_done")
        back_read = sem("back_read")
        steps = Steps(sem("mix_steps"))
        FWD, DFT, BACK = 0, 4 * JT, 8 * JT
        N_TILES = 12 * JT
        block = mem.enter_context(nc.Block())

        def table_tile(n):
            if n < DFT:
                return A["half_tables"][n // JT, (n % JT) * P:(n % JT + 1) * P, :]
            if n < BACK:
                par, a, trig = (n - DFT) // (2 * JT), (n - DFT) // 2 % JT, n % 2
                return A["dft_tables"][2 * par + trig, a * P:(a + 1) * P, :]
            par, trig, f = (n - BACK) // (2 * JT), (n - BACK) // JT % 2, n % JT
            return A["back_tables"][par, trig, f * P:(f + 1) * P, :]

        @block.sync
        def _(sp):
            sp.dma_start(pair[:], A["pair_table"].rearrange("p t c -> p (t c)")).then_inc(pair_in, 16)
            for t in range(TT):
                sp.dma_start(m.res[:, t, :], A["x"][0, t * P:(t + 1) * P, :]).then_inc(m.x_in, 16)
            for n in range(N_TILES):
                if n >= SLOTS:
                    sp.wait_ge(tab_used, n - SLOTS + 1)
                sp.dma_start(table[:, n % SLOTS, :], table_tile(n)).then_inc(tab_in[n % SLOTS], 16)

        @block.tensor
        def _(pe):
            def arrived(n):
                pe.wait_ge(tab_in[n % SLOTS], 16 * (n // SLOTS + 1))

            def channel_transform(par):
                for a in range(JT):
                    n = par * JT + a
                    if a >= 2:
                        pe.wait_ge(chan_kept, n - 1)
                    for c in range(HT):
                        last = nc.tensor.matmul(ps[:, 4 * par + 2 * (a % 2) + c // 2, (c % 2) * 2 * P:(c % 2 + 1) * 2 * P],
                                                m.mixT[:, HT + c, 2 * P * a + par:2 * P * (a + 1):2], pair[:],
                                                start=True, stop=True)
                    last.then_inc(chan_mm, 1)

            for n in range(2 * JT):
                par, a = n // JT, n % JT
                if n >= 4:
                    pe.wait_ge(z_kept, n - 3)
                for c in range(HT):
                    last = nc.tensor.transpose(ps[:, n % 4, c * P:(c + 1) * P],
                                               m.zT[:, c, 2 * P * a + par:2 * P * (a + 1):2], m.ident[:])
                last.then_inc(z_turned, 1)
            for g in range(4):
                if g < 2:
                    pe.wait_ge(z_kept, 2 * JT)
                else:
                    pe.wait_ge(u_done if g % 2 else even_kept, 1)
                for a in range(JT):
                    n = FWD + g * JT + a
                    arrived(n)
                    for f in range(JT):
                        last = nc.tensor.matmul(ps[:, 4 * (g % 2) + f, :], table[:, n % SLOTS, f * P:(f + 1) * P],
                                                znat[:, (g % 2) * JT + a, :], start=(a == 0), stop=(a == JT - 1))
                    last.then_inc(tab_used, 1)
            pe.wait_ge(pair_in, 16)
            for par in range(2):
                pe.wait_ge(u_done if par else even_kept, 2)
                channel_transform(par)
                pe.wait_ge(chan_kept, (par + 1) * JT)
                for a in range(JT):
                    for trig in range(2):
                        n = DFT + (par * JT + a) * 2 + trig
                        arrived(n)
                        for c in range(HT):
                            last = nc.tensor.matmul(ps[:, 4 * par + c, :], chan[:, a, c, trig * P:(trig + 1) * P],
                                                    table[:, n % SLOTS, :], start=(a == 0 and trig == 0),
                                                    stop=(a == JT - 1 and trig == 1))
                        last.then_inc(tab_used, 1)
            for par in range(2):
                pe.wait_ge(four_done if par else four_even, 1)
                for k in range(2 * JT):
                    trig, f = k // JT, k % JT
                    if par == 0 and trig == 0:
                        pe.wait_ge(g_done, f + 1)
                    n = BACK + par * 2 * JT + k
                    arrived(n)
                    for c in range(HT):
                        last = nc.tensor.matmul(ps[:, 4 * par + c, :], U[:, trig, par, f, c * P:(c + 1) * P],
                                                table[:, n % SLOTS, :], start=(k == 0), stop=(k == 2 * JT - 1))
                    last.then_inc(tab_used, 1)

        @block.scalar
        def _(act):
            for n in range(2 * JT):
                act.wait_ge(z_turned, n + 1)
                nc.scalar.activation(znat[:, n, :], ps[:, n % 4, :], ACT.Copy).then_inc(z_kept, 1)
            for trig in range(2):
                act.wait_ge(tab_used, FWD + (2 * trig + 1) * JT)
                if trig:
                    act.wait_ge(u_done, 1)
                nc.scalar.activation(even_part[:], ps[:, 0:4, :], ACT.Copy).then_inc(even_kept, 1)
            for par in range(2):
                for a in range(JT):
                    n = par * JT + a
                    act.wait_ge(chan_mm, n + 1)
                    if par:
                        act.wait_ge(tab_used, DFT + 2 * (a + 1))
                    b = 4 * par + 2 * (a % 2)
                    nc.scalar.activation(chan[:, a, :, :].rearrange("p (b c) n -> p b (c n)", b=2), ps[:, b:b + 2, :],
                                         ACT.Copy).then_inc(chan_kept, 1)
                if par == 0:
                    act.wait_ge(tab_used, DFT + 2 * JT)
                    act.wait_ge(u_done, 2)
                    nc.scalar.activation(even_part[:], ps[:, 0:4, :], ACT.Copy).then_inc(four_even, 1)

        @block.gpsimd
        def _(pool):
            pool.wait_ge(z_turned, 2 * JT)
            for c in range(HT):
                nc.gpsimd.tensor_scalar(m.zT[:, c, :], m.zT[:, c, :], col(m.params, "f_bias", c), None, ALU.mult) \
                    .then_inc(bias_done, 1)

        @block.vector
        def _(dve):
            for trig in range(2):
                dve.wait_ge(even_kept, trig + 1)
                dve.wait_ge(tab_used, FWD + (2 * trig + 2) * JT)
                nc.vector.tensor_tensor(U[:, trig, 0, :, :], even_part[:], ps[:, 4:8, :], ALU.add)
                nc.vector.tensor_tensor(U[:, trig, 1, :, :], even_part[:], ps[:, 4:8, :], ALU.subtract) \
                    .then_inc(u_done, 1)
            dve.wait_ge(u_done, 2)
            for f in range(JT):
                if f:
                    dve.wait_ge(g_done, f)
                for pm in range(2):
                    for i, (a, b) in enumerate(((0, 0), (1, 1), (0, 1), (1, 0))):
                        last = nc.vector.tensor_tensor(znat[:, 4 * pm + i, :], U[:, a, pm, f, :], m.K[:, b, pm, f, :],
                                                       ALU.mult)
                steps.end(last)
                steps.wait(dve)
                for pm in range(2):
                    for i, op in ((0, ALU.subtract), (2, ALU.add)):
                        last = nc.vector.tensor_tensor(znat[:, 4 * pm + i, :], znat[:, 4 * pm + i, :],
                                                       znat[:, 4 * pm + i + 1, :], op)
                steps.end(last)
                steps.wait(dve)
                for trig in range(2):
                    for par, op in ((0, ALU.add), (1, ALU.subtract)):
                        last = nc.vector.tensor_tensor(U[:, trig, par, f, :], znat[:, 2 * trig, :],
                                                       znat[:, 4 + 2 * trig, :], op)
                last.then_inc(g_done, 1)
            dve.wait_ge(four_even, 1)
            dve.wait_ge(tab_used, DFT + 4 * JT)
            nc.vector.tensor_tensor(m.mixT[:, HT:2 * HT, 0:HALF], even_part[:], ps[:, 4:8, :], ALU.add)
            nc.vector.tensor_tensor(m.mixT[:, HT:2 * HT, HALF:SEQ], even_part[:], ps[:, 4:8, :], ALU.subtract) \
                .then_inc(four_done, 1)
            dve.wait_ge(bias_done, HT)
            for par in range(2):
                dve.wait_ge(tab_used, BACK + (par + 1) * 2 * JT)
                for c in range(HT):
                    steps.end(nc.vector.scalar_tensor_tensor(
                        out=m.zT[:, c, par:SEQ:2], in0=ps[:, 4 * par + c, :], scalar=m.inv_size[:, c:c + 1],
                        in1=m.zT[:, c, par:SEQ:2], op0=ALU.mult, op1=ALU.add))
                    steps.wait(dve)
                    nc.vector.tensor_tensor(m.mixT[:, c, par:SEQ:2], m.mixT[:, c, par:SEQ:2], m.zT[:, c, par:SEQ:2],
                                            ALU.mult)


def head_norm_project(nc, m, A):
    with ExitStack() as mem:
        def sb(name, shape, dt=F32):
            return mem.enter_context(nc.sbuf_tensor(name, shape, dt))

        sem = m.sem
        NH = D // HEAD
        pick = sb("head_pick", [P, KT, NH])
        spread = sb("head_spread", [NH, KT, P])
        spread_r = sb("head_spread_r", [NH, KT, P], F32R)
        scratch = m.K[:].rearrange("p a b f c -> p (a b f c)").rearrange("p (n c) -> p n c", c=SEQ)
        sq = scratch[:, 2:4, :]
        rstd = scratch[0:NH, 4, :]
        rstd_high = sb("head_rstd_high", [NH, SEQ], F32R)
        rstd_rest = sb("head_rstd_rest", [NH, SEQ], F32R)
        ps = mem.enter_context(nc.psum_tensor("w_out_ps", [P, 4, 2, BANK], F32))
        wide = WideProduct(nc, m, mem, "w_out", m.mixT, A["w_out"][0], [scratch[:, i, :] for i in range(2)], ps)
        tables_in = sem("head_tables_in")
        spread_done = sem("head_spread_done")
        squared = sem("head_squared")
        mean_mm = sem("head_mean_mm")
        rms_done = sem("head_rms_done")
        rstd_done = sem("head_rstd_done")
        rstd_split = sem("head_rstd_split")
        spread_mm = sem("head_spread_mm")
        normed = sem("head_normed")
        added = sem("w_out_added")
        block = mem.enter_context(nc.Block())

        @block.sync
        def _(sp):
            sp.dma_start(pick[:], A["head_pick"]).then_inc(tables_in, 16)
            sp.dma_start(spread[:], A["head_spread"]).then_inc(tables_in, 16)
            wide.load(sp)

        @block.gpsimd
        def _(pool):
            for c in range(KT):
                if c >= 2:
                    pool.wait_ge(mean_mm, c - 1)
                nc.gpsimd.tensor_tensor(sq[:, c % 2, :], m.mixT[:, c, :], m.mixT[:, c, :], ALU.mult) \
                    .then_inc(squared, 1)

        @block.tensor
        def _(pe):
            pe.wait_ge(tables_in, 32)
            for c in range(KT):
                pe.wait_ge(squared, c + 1)
                for half in range(2):
                    last = nc.tensor.matmul(ps[0:NH, 0, half, :], pick[:, c, :],
                                            sq[:, c % 2, half * BANK:(half + 1) * BANK],
                                            start=(c == 0), stop=(c == KT - 1))
                last.then_inc(mean_mm, 1)
            pe.wait_ge(spread_done, 1)
            pe.wait_ge(rstd_split, 1)
            for c in range(KT):
                if c >= 4:
                    pe.wait_ge(normed, c - 3)
                for half in range(2):
                    cols = slice(half * BANK, (half + 1) * BANK)
                    nc.tensor.matmul(ps[:, c % 4, half, :], spread_r[:, c, :], rstd_high[:, cols], start=True, stop=False)
                    last = nc.tensor.matmul(ps[:, c % 4, half, :], spread_r[:, c, :], rstd_rest[:, cols],
                                            start=False, stop=True)
                last.then_inc(spread_mm, 1)
            pe.wait_ge(normed, KT)
            for t in range(TT):
                wide.tile_product(pe, t, added, t - 3)

        @block.scalar
        def _(act):
            act.wait_ge(tables_in, 32)
            nc.scalar.activation(spread_r[:], spread[:], ACT.Copy).then_inc(spread_done, 1)
            for k in range(KT):
                wide.weight_high(act, k)
            act.wait_ge(mean_mm, KT)
            nc.scalar.activation(rstd.rearrange("p (h c) -> p h c", h=2), ps[0:NH, 0, :, :], ACT.Sqrt,
                                 bias=m.eps[0:NH, :]).then_inc(rms_done, 1)
            act.wait_ge(rstd_done, 1)
            nc.scalar.activation(rstd_high[:], rstd, ACT.Copy).then_inc(rstd_done, 1)
            act.wait_ge(normed, KT)
            for t in range(TT):
                wide.tile_high(act, t)

        @block.vector
        def _(dve):
            for k in range(KT):
                wide.weight_rest(dve, k)
            dve.wait_ge(rms_done, 1)
            nc.vector.reciprocal(rstd, rstd).then_inc(rstd_done, 1)
            dve.wait_ge(rstd_done, 2)
            nc.vector.tensor_tensor(rstd_rest[:], rstd, rstd_high[:].bitcast(F32), ALU.subtract).then_inc(rstd_split, 1)
            for c in range(KT):
                dve.wait_ge(spread_mm, c + 1)
                here = m.mixT[:, c, :].rearrange("p (h c) -> p h c", h=2)
                nc.vector.scalar_tensor_tensor(out=here, in0=here, scalar=col(m.params, "mix_g", c),
                                               in1=ps[:, c % 4, :, :], op0=ALU.mult, op1=ALU.mult).then_inc(normed, 1)
            dve.wait_ge(m.x_in, 32 * TT)
            for t in range(2):
                wide.tile_rest(dve, t)
            for t in range(TT):
                dve.wait_ge(wide.done, t + 1)
                if t + 2 < TT:
                    wide.tile_rest(dve, t + 2)
                nc.vector.tensor_tensor(m.res[:, t, :].rearrange("p (h c) -> p h c", h=2),
                                        m.res[:, t, :].rearrange("p (h c) -> p h c", h=2),
                                        ps[:, t % 4, :, :], ALU.add).then_inc(added, 1)


def first_mixer(nc, m, A):
    with nc.sbuf_tensor("K", [P, 2, 2, JT, BANK], F32) as m.K:
        filter_spectrum(nc, m, A)
        with nc.sbuf_tensor("mixT", [P, KT, SEQ], F32) as m.mixT:
            with nc.sbuf_tensor("zT", [P, HT, SEQ], F32) as m.zT:
                with nc.sbuf_tensor("hT1_high", [P, KT, SEQ], F32R) as high, \
                        nc.sbuf_tensor("hT1_rest", [P, KT, SEQ], F32R) as rest:
                    norm_to_T(nc, m, "norm1", (high, rest), gamma="norm1_g", x_ready=m.x_in)
                    project_first(nc, m, A, (high, rest))
                transform_mixes(nc, m, A)
            head_norm_project(nc, m, A)


def route(nc, m, A, hT):
    with ExitStack() as mem:
        def sb(name, shape, dt=F32):
            return mem.enter_context(nc.sbuf_tensor(name, shape, dt))

        sem = m.sem
        NL = GROUPS + EXPERTS
        w = sb("router_w", [P, KT, NL])
        b = sb("router_b", [P, NL])
        before = sb("before", [P, P])
        idx = sb("index_row", [P, 2, EXPERTS])
        limits = sb("limits", [P, FULL_BLOCKS - 1])
        logits = sb("logits", [P, TT, NL])
        gmax = sb("gmax", [P, TT])
        gdiff = sb("gdiff", [P, TT, GROUPS])
        gexp = sb("gexp", [P, TT, GROUPS])
        gmask = sb("gmask", [P, TT, GROUPS])
        pg = sb("pg", [P, TT])
        part = sb("part", [P, 2, TT, PER_GROUP])
        sel = sb("sel", [P, TT, PER_GROUP])
        cand = sb("cand", [P, TT, PER_GROUP])
        first = sb("first", [P, TT])
        hot = sb("hot", [P, 2, TT, PER_GROUP])
        top = sb("top", [P, 2, TT])
        diff = sb("diff", [P, TT])
        ratio = sb("ratio", [P, TT])
        M = sb("M", [P, 2, TT, EXPERTS])
        both = sb("both", [P, TT, EXPERTS])
        earlier = sb("earlier", [P, TT + 1, EXPERTS])
        rank = sb("rank", [P, TT + 1, EXPERTS])
        over = sb("over", [P, EXPERTS, FULL_BLOCKS - 1])
        n_over = sb("n_over", [P, EXPERTS])
        incl = sb("incl", [P, EXPERTS])
        excl = sb("excl", [P, EXPERTS])
        prod = sb("prod", [P, TT, EXPERTS])
        r_of = sb("r_of", [P, 2, TT])
        e_of = sb("e_of", [P, 2, TT])
        s_of = sb("s_of", [P, 2, TT])
        steps_in = sb("steps_in", [P, 2, TT, FULL_BLOCKS - 1])
        full = sb("full", [P, 2, TT])
        blk = sb("blk", [P, 2, TT])
        posf = sb("posf", [P, 2, TT])
        pos = sb("pos_i", [P, 2, TT], I32)
        tokens = sb("token_ids", [P, TT], I32)
        blank = sb("blank", [CAP, BLOCKS], I32)
        ends = sb("ends", [1, OVER, EXPERTS])
        over_f = sb("over_f", [1, OVER + 1])
        ps = mem.enter_context(nc.psum_tensor("route_ps", [P, 2, BANK], F32))

        w_in = sem("router_in")
        logit_mm = sem("logit_mm")
        gdiff_done = sem("gdiff_done")
        gexp_done = sem("gexp_done")
        diff_done = sem("diff_done")
        ratio_done = sem("ratio_done")
        pairs_done = sem("pairs_done")
        rank_mm = sem("rank_mm")
        pos_done = sem("pos_done")
        ids_set = sem("ids_set")
        blanked = sem("blanked")
        listed = sem("listed")
        steps = Steps(sem("route_steps"))
        block = mem.enter_context(nc.Block())

        @block.sync
        def _(sp):
            sp.dma_start(w[:], A["w_router"].rearrange("(k p) n -> p k n", p=P)).then_inc(w_in, 16)
            sp.dma_start(b[:], A["b_router"].to_broadcast([P, NL])).then_inc(w_in, 16)
            sp.dma_start(before[:], A["before"]).then_inc(w_in, 16)
            sp.dma_start(idx[:], A["index_rows"].to_broadcast([P, 2, EXPERTS])).then_inc(w_in, 16)
            sp.dma_start(limits[:], A["limits"].to_broadcast([P, FULL_BLOCKS - 1])).then_inc(w_in, 16)

        @block.gpsimd
        def _(pool):
            nc.gpsimd.iota(tokens[:], pattern=[[P, TT]], base=0, channel_multiplier=1).then_inc(ids_set, 1)
            nc.gpsimd.memset(blank[:], 0).then_inc(ids_set, 1)
            pool.wait_ge(ids_set, 2)
            pool.dma_start(m.row_list.rearrange("(p b) o -> p (b o)", p=CAP), blank[:]).then_inc(blanked, 16)
            pool.wait_ge(blanked, 16)
            pool.wait_ge(pos_done, 1)
            for slot in range(2):
                for t in range(TT):
                    pool.indirect_dma_start(m.row_list, bass.IndirectOffsetOnAxis(ap=pos[:, slot, t:t + 1], axis=0),
                                            tokens[:, t:t + 1], None).then_inc(listed, 16)
            pool.wait_ge(listed, 16 * 2 * TT)

        @block.tensor
        def _(pe):
            pe.wait_ge(w_in, 80)
            for t in range(TT):
                for k in range(KT):
                    last = nc.tensor.matmul(ps[:, 0, t * NL:(t + 1) * NL], hT[:, k, t * P:(t + 1) * P], w[:, k, :],
                                            start=(k == 0), stop=(k == KT - 1))
            last.then_inc(logit_mm, 1)
            pe.wait_ge(pairs_done, 1)
            for t in range(TT + 1):
                out = ps[:, 1, t * EXPERTS:(t + 1) * EXPERTS]
                if t < TT:
                    nc.tensor.matmul(out, before[:], both[:, t, :], start=True, stop=False)
                last = nc.tensor.matmul(out, m.ones[:], earlier[:, t, :], start=(t == TT), stop=True)
            last.then_inc(rank_mm, 1)

        @block.scalar
        def _(act):
            act.wait_ge(gdiff_done, 1)
            nc.scalar.activation(gexp[:], gdiff[:], ACT.Exp).then_inc(gexp_done, 1)
            act.wait_ge(diff_done, 1)
            nc.scalar.activation(ratio[:], diff[:], ACT.Exp).then_inc(ratio_done, 1)

        @block.vector
        def _(dve):
            def step(instruction):
                steps.end(instruction)
                steps.wait(dve)

            def wide(a, n):
                return a.unsqueeze(2).to_broadcast([P, TT, n])

            def over_tiles(a, n):
                return a.unsqueeze(1).to_broadcast([P, TT, n])

            def first_of(mask_out, values, largest, n):
                c = cand[:, :, 0:n]
                step(nc.vector.tensor_tensor(c, values, wide(largest, n), ALU.is_equal))
                step(nc.vector.tensor_tensor(c, c, over_tiles(idx[:, 0, 0:n], n), ALU.mult))
                step(nc.vector.tensor_reduce(first[:], c, AX_X, ALU.min))
                step(nc.vector.tensor_tensor(mask_out, over_tiles(idx[:, 0, 0:n], n), wide(first[:], n), ALU.is_equal))

            dve.wait_ge(w_in, 80)
            dve.wait_ge(logit_mm, 1)
            step(nc.vector.tensor_tensor(logits[:], ps[:, 0, 0:TT * NL].rearrange("p (t n) -> p t n", t=TT),
                                         over_tiles(b[:], NL), ALU.add))
            group = logits[:, :, 0:GROUPS]
            step(nc.vector.tensor_reduce(gmax[:], group, AX_X, ALU.max))
            nc.vector.tensor_tensor(gdiff[:], group, wide(gmax[:], GROUPS), ALU.subtract).then_inc(gdiff_done, 1)
            first_of(gmask[:], group, gmax[:], GROUPS)
            dve.wait_ge(gexp_done, 1)
            step(nc.vector.tensor_reduce(pg[:], gexp[:], AX_X, ALU.add))
            step(nc.vector.reciprocal(pg[:], pg[:]))
            for g in range(GROUPS):
                of_g = logits[:, :, GROUPS + g * PER_GROUP:GROUPS + (g + 1) * PER_GROUP]
                mask = gmask[:, :, g:g + 1].to_broadcast([P, TT, PER_GROUP])
                if g == 0:
                    step(nc.vector.tensor_tensor(sel[:], of_g, mask, ALU.mult))
                else:
                    step(nc.vector.tensor_tensor(part[:, 0], of_g, mask, ALU.mult))
                    step(nc.vector.tensor_tensor(sel[:], sel[:], part[:, 0], ALU.add))
            for slot in range(2):
                step(nc.vector.tensor_reduce(top[:, slot, :], sel[:], AX_X, ALU.max))
                first_of(hot[:, slot], sel[:], top[:, slot, :], PER_GROUP)
                if slot == 0:
                    step(nc.vector.scalar_tensor_tensor(out=sel[:], in0=hot[:, 0], scalar=NEG, in1=sel[:],
                                                        op0=ALU.mult, op1=ALU.add))
            nc.vector.tensor_tensor(diff[:], top[:, 1, :], top[:, 0, :], ALU.subtract).then_inc(diff_done, 1)
            for slot in range(2):
                for g in range(GROUPS):
                    last = nc.vector.tensor_tensor(M[:, slot, :, g * PER_GROUP:(g + 1) * PER_GROUP], hot[:, slot],
                                                   gmask[:, :, g:g + 1].to_broadcast([P, TT, PER_GROUP]), ALU.mult)
            step(last)
            step(nc.vector.tensor_tensor(both[:], M[:, 0], M[:, 1], ALU.add))
            step(nc.vector.memset(earlier[:, 0, :], 0.0))
            for t in range(TT):
                last = nc.vector.tensor_tensor(earlier[:, t + 1, :], earlier[:, t, :], both[:, t, :], ALU.add)
                if t < TT - 1:
                    step(last)
            last.then_inc(pairs_done, 1)
            dve.wait_ge(ratio_done, 1)
            step(nc.vector.tensor_scalar(diff[:], ratio[:], 1.0, None, ALU.add))
            step(nc.vector.reciprocal(diff[:], diff[:]))
            step(nc.vector.tensor_tensor(m.pair_w[:, 0, :], diff[:], pg[:], ALU.mult))
            step(nc.vector.tensor_tensor(m.pair_w[:, 1, :], m.pair_w[:, 0, :], ratio[:], ALU.mult))
            dve.wait_ge(rank_mm, 1)
            step(nc.vector.tensor_copy(rank[:], ps[:, 1, 0:(TT + 1) * EXPERTS].rearrange("p (t e) -> p t e", t=TT + 1)))
            n_lim = FULL_BLOCKS - 1
            step(nc.vector.tensor_tensor(over[:], rank[:, TT, :].unsqueeze(2).to_broadcast([P, EXPERTS, n_lim]),
                                         limits[:].unsqueeze(1).to_broadcast([P, EXPERTS, n_lim]), ALU.is_gt))
            step(nc.vector.tensor_reduce(n_over[:], over[:], AX_X, ALU.add))
            step(nc.vector.tensor_tensor_scan(incl[:], m.ones[:, 0:EXPERTS], n_over[:], 0.0, ALU.mult, ALU.add))
            step(nc.vector.tensor_tensor(excl[:], incl[:], n_over[:], ALU.subtract))
            for slot in range(2):
                for out, table in ((r_of, rank[:, 0:TT, :]), (e_of, over_tiles(idx[:, 1, :], EXPERTS)),
                                   (s_of, over_tiles(excl[:], EXPERTS))):
                    step(nc.vector.tensor_tensor(prod[:], M[:, slot], table, ALU.mult))
                    step(nc.vector.tensor_reduce(out[:, slot, :], prod[:], AX_X, ALU.add))
            for slot in range(2):
                step(nc.vector.tensor_tensor(steps_in[:, slot], wide(r_of[:, slot, :], n_lim), over_tiles(limits[:], n_lim),
                                             ALU.is_ge))
                step(nc.vector.tensor_reduce(full[:, slot, :], steps_in[:, slot], AX_X, ALU.add))
            step(nc.vector.tensor_tensor(blk[:], s_of[:], full[:], ALU.add))
            step(nc.vector.tensor_tensor(blk[:], blk[:], e_of[:], ALU.subtract))
            step(nc.vector.tensor_scalar(blk[:], blk[:], float(EXPERTS - 1), None, ALU.add))
            step(nc.vector.scalar_tensor_tensor(out=blk[:], in0=full[:], scalar=1.0, in1=blk[:], op0=ALU.min,
                                                op1=ALU.mult))
            step(nc.vector.tensor_tensor(blk[:], blk[:], e_of[:], ALU.add))
            step(nc.vector.scalar_tensor_tensor(out=r_of[:], in0=full[:], scalar=-float(CAP), in1=r_of[:],
                                                op0=ALU.mult, op1=ALU.add))
            step(nc.vector.scalar_tensor_tensor(out=posf[:], in0=r_of[:], scalar=float(BLOCKS), in1=blk[:],
                                                op0=ALU.mult, op1=ALU.add))
            nc.vector.tensor_copy(pos[:], posf[:]).then_inc(pos_done, 1)
            step(nc.vector.scalar_tensor_tensor(out=blk[:], in0=blk[:], scalar=float(CAP), in1=r_of[:],
                                                op0=ALU.mult, op1=ALU.add))
            step(nc.vector.tensor_copy(m.pair_row[:], blk[:]))
            step(nc.vector.tensor_tensor(ends[:], incl[0:1, :].unsqueeze(1).to_broadcast([1, OVER, EXPERTS]),
                                         idx[0:1, 1, 0:OVER].unsqueeze(2).to_broadcast([1, OVER, EXPERTS]), ALU.is_le))
            step(nc.vector.tensor_reduce(over_f[:, 0:OVER], ends[:], AX_X, ALU.add))
            step(nc.vector.tensor_scalar(over_f[:, 0:OVER], over_f[:, 0:OVER], float(EXPERTS - 1), None, ALU.min))
            step(nc.vector.tensor_copy(over_f[:, OVER:OVER + 1], incl[0:1, EXPERTS - 1:EXPERTS]))
            step(nc.vector.tensor_copy(m.over_table[:], over_f[:]))


def experts(nc, m, A):
    with ExitStack() as mem:
        def sb(name, shape, dt=F32):
            return mem.enter_context(nc.sbuf_tensor(name, shape, dt))

        sem = m.sem
        S = 2
        FE = D_EXPERT // P
        w_g = sb("w_gate_sb", [P, S, KT, D_EXPERT])
        w_u = sb("w_up_sb", [P, S, KT, D_EXPERT])
        w_d = sb("w_down_sb", [P, S, FE, D])
        idx_all = sb("row_ids", [CAP, BLOCKS], I32)
        idx = sb("block_ids", [CAP, S], I32)
        rows = sb("rows", [CAP, S, D])
        xT = sb("xT", [P, S, KT, CAP])
        act_out = sb("gate_act", [P, S, FE, CAP])
        hidT = sb("hidT", [P, S, FE, CAP])
        y = sb("y_rows", [CAP, S, D])
        ps_x = mem.enter_context(nc.psum_tensor("x_ps", [P, KT, P], F32))
        ps_h = mem.enter_context(nc.psum_tensor("h_ps", [P, S, 2, FE, P], F32))
        ps_y = mem.enter_context(nc.psum_tensor("y_ps", [P, 2, BANK], F32))

        ids_in = sem("row_ids_in")
        g_in = [sem(f"w_gate_in{s}") for s in range(S)]
        u_in = [sem(f"w_up_in{s}") for s in range(S)]
        d_in = [sem(f"w_down_in{s}") for s in range(S)]
        idx_set = [sem(f"block_ids_set{s}") for s in range(S)]
        rows_in = [sem(f"rows_in{s}") for s in range(S)]
        turned = [sem(f"rows_turned{s}") for s in range(S)]
        xT_done = [sem(f"xT_done{s}") for s in range(S)]
        gate_mm = [sem(f"gate_mm{s}") for s in range(S)]
        up_mm = [sem(f"up_mm{s}") for s in range(S)]
        act_done = [sem(f"gate_act_done{s}") for s in range(S)]
        hid_done = [sem(f"hid_done{s}") for s in range(S)]
        down_mm = [sem(f"down_mm{s}") for s in range(S)]
        y_left = [sem(f"y_left{s}") for s in range(S)]
        y_right = [sem(f"y_right{s}") for s in range(S)]
        y_out = [sem(f"y_stored{s}") for s in range(S)]
        block = mem.enter_context(nc.Block())
        waited_sp = sem("waited_sp")
        waited_pool = sem("waited_pool")
        PAIRS = EXPERTS // S


        def over_blocks(engine, body):
            count = engine.value_load(m.over_table[0:1, OVER:OVER + 1], min_val=0, max_val=OVER)
            with engine.Fori(0, OVER) as j:
                with engine.If(j < count):
                    body(j)
            return count

        @block.sync
        def _(sp):
            def load(s, e, use, first=False):
                for (w, name, arrived, read) in ((w_g, "w_gate", g_in, gate_mm), (w_u, "w_up", u_in, up_mm),
                                                 (w_d, "w_down", d_in, down_mm)):
                    if not first:
                        sp.wait_ge(read[s], use)
                    sp.dma_start(w[:, s, :, :], A[name][0, bass.ds(e, 1)].rearrange("o (k p) n -> p (o k) n", p=P)) \
                        .then_inc(arrived[s], 16)

            def store(s, b, use):
                sp.wait_ge(y_left[s], use + 1)
                sp.wait_ge(y_right[s], use + 1)
                sp.dma_start(m.y_dram[bass.ds(b * CAP, CAP), :], y[:, s, :]).then_inc(y_out[s], 16)

            sp.dma_start(idx_all[:], m.row_list.rearrange("(p b) o -> p (b o)", p=CAP)).then_inc(ids_in, 16)
            for s in range(S):
                load(s, s, 0, first=True)
            with sp.Fori(0, PAIRS - 1) as i:
                for s in range(S):
                    load(s, i * S + (S + s), i + 1)
                    store(s, i * S + s, i)
            for s in range(S):
                store(s, EXPERTS - S + s, PAIRS - 1)

            def over(j):
                e = sp.value_load(m.over_table[0:1, bass.ds(j, 1)], min_val=0, max_val=EXPERTS - 1)
                load(0, e, j + PAIRS)
                store(0, j + EXPERTS, j + PAIRS)

            count = over_blocks(sp, over)
            sp.wait_ge(y_out[0], (count + PAIRS) * 16)
            sp.sem_inc(waited_sp, 1)
            sp.wait_ge(y_out[1], PAIRS * 16)

        @block.gpsimd
        def _(pool):
            def gather(s, b, use, first=False):
                if not first:
                    pool.wait_ge(turned[s], use)
                nc.gpsimd.tensor_copy(idx[:, s:s + 1], idx_all[:, bass.ds(b, 1)]).then_inc(idx_set[s], 1)
                pool.wait_ge(idx_set[s], use + 1)
                pool.sem_inc(waited_pool, 1)
                pool.indirect_dma_start(rows[:, s, :], None, m.hn_dram,
                                        bass.IndirectOffsetOnAxis(ap=idx[:, s:s + 1], axis=0)).then_inc(rows_in[s], 16)

            pool.wait_ge(ids_in, 16)
            for s in range(S):
                gather(s, s, 0, first=True)
            with pool.Fori(1, PAIRS) as i:
                for s in range(S):
                    gather(s, i * S + s, i)
            over_blocks(pool, lambda j: gather(0, j + EXPERTS, j + PAIRS))

        @block.tensor
        def _(pe):
            def turn(s, use, before=None):
                pe.wait_ge(rows_in[s], (use + 1) * 16)
                if before is not None:
                    pe.wait_ge(xT_done[before[0]], before[1] + 1)
                for k in range(KT):
                    last = nc.tensor.transpose(ps_x[:, k, 0:CAP], rows[:, s, k * P:(k + 1) * P], m.ident[0:CAP, 0:CAP])
                last.then_inc(turned[s], 1)

            def gate_up(s, use):
                pe.wait_ge(xT_done[s], use + 1)
                for i, (w, arrived, done) in enumerate(((w_g, g_in, gate_mm), (w_u, u_in, up_mm))):
                    pe.wait_ge(arrived[s], (use + 1) * 16)
                    for f in range(FE):
                        for k in range(KT):
                            last = nc.tensor.matmul(ps_h[:, s, i, f, 0:CAP], w[:, s, k, f * P:(f + 1) * P],
                                                    xT[:, s, k, :], start=(k == 0), stop=(k == KT - 1))
                    last.then_inc(done[s], 1)

            def down(s, use, before=None):
                pe.wait_ge(hid_done[s], use + 1)
                pe.wait_ge(d_in[s], (use + 1) * 16)
                if before is not None:
                    pe.wait_ge(y_left[before[0]], before[1] + 1)
                    pe.wait_ge(y_right[before[0]], before[1] + 1)
                for half in range(2):
                    for f in range(FE):
                        last = nc.tensor.matmul(ps_y[0:CAP, half, :], hidT[:, s, f, :],
                                                w_d[:, s, f, half * BANK:(half + 1) * BANK],
                                                start=(f == 0), stop=(f == FE - 1))
                last.then_inc(down_mm[s], 1)

            turn(0, 0)
            gate_up(0, 0)
            turn(1, 0, before=(0, 0))
            down(0, 0)
            with pe.Fori(0, PAIRS - 1) as i:
                gate_up(1, i)
                turn(0, i + 1, before=(1, i))
                down(1, i, before=(0, i))
                gate_up(0, i + 1)
                turn(1, i + 1, before=(0, i + 1))
                down(0, i + 1, before=(1, i))
            gate_up(1, PAIRS - 1)
            down(1, PAIRS - 1, before=(0, PAIRS - 1))

            def over(j):
                turn(0, j + PAIRS)
                gate_up(0, j + PAIRS)
                down(0, j + PAIRS, before=(0, j + (PAIRS - 1)))

            pe.wait_ge(y_left[1], PAIRS)
            pe.wait_ge(y_right[1], PAIRS)
            over_blocks(pe, over)

        @block.scalar
        def _(act):
            def gate(s, use, first=False):
                act.wait_ge(gate_mm[s], use + 1)
                if not first:
                    act.wait_ge(hid_done[s], use)
                nc.scalar.activation(act_out[:, s, :, :], ps_h[:, s, 0, :, 0:CAP], ACT.Silu).then_inc(act_done[s], 1)

            def left(s, use, first=False):
                act.wait_ge(down_mm[s], use + 1)
                if not first:
                    act.wait_ge(y_out[s], use * 16)
                nc.scalar.activation(y[:, s, 0:BANK], ps_y[0:CAP, 0, :], ACT.Copy).then_inc(y_left[s], 1)

            for s in range(S):
                gate(s, 0, first=True)
                left(s, 0, first=True)
            with act.Fori(1, PAIRS) as i:
                for s in range(S):
                    gate(s, i)
                    left(s, i)

            def over(j):
                gate(0, j + PAIRS)
                left(0, j + PAIRS)

            over_blocks(act, over)

        @block.vector
        def _(dve):
            def x_out(s, use, first=False):
                dve.wait_ge(turned[s], use + 1)
                if not first:
                    dve.wait_ge(up_mm[s], use)
                nc.vector.tensor_copy(xT[:, s, :, :], ps_x[:, :, 0:CAP]).then_inc(xT_done[s], 1)

            def hidden(s, use, first=False):
                dve.wait_ge(up_mm[s], use + 1)
                dve.wait_ge(act_done[s], use + 1)
                if not first:
                    dve.wait_ge(down_mm[s], use)
                nc.vector.tensor_tensor(hidT[:, s, :, :], act_out[:, s, :, :], ps_h[:, s, 1, :, 0:CAP], ALU.mult) \
                    .then_inc(hid_done[s], 1)

            def right(s, use, first=False):
                dve.wait_ge(down_mm[s], use + 1)
                if not first:
                    dve.wait_ge(y_out[s], use * 16)
                nc.vector.tensor_copy(y[:, s, BANK:D], ps_y[0:CAP, 1, :]).then_inc(y_right[s], 1)

            def pair(i, first=False):
                hidden(0, i, first)
                x_out(1, i, first)
                right(0, i, first)
                hidden(1, i, first)
                if not (isinstance(i, int) and i == PAIRS - 1):
                    x_out(0, i + 1)
                right(1, i, first)

            x_out(0, 0, first=True)
            pair(0, first=True)
            with dve.Fori(1, PAIRS - 1) as i:
                pair(i)
            pair(PAIRS - 1)

            def over(j):
                x_out(0, j + PAIRS)
                hidden(0, j + PAIRS)
                right(0, j + PAIRS)

            over_blocks(dve, over)


def combine(nc, m, A):
    with ExitStack() as mem:
        def sb(name, shape, dt=F32):
            return mem.enter_context(nc.sbuf_tensor(name, shape, dt))

        sem = m.sem
        BUF = 3
        y = sb("y_pairs", [P, BUF, 2, D])
        g_row = sb("final_gamma", [P, D])
        squares = sb("final_squares", [P, D])
        sums = sb("final_sums", [P, TT])
        rms = sb("final_rms", [P, TT])
        rstd = sb("final_rstd", [P, TT])
        y_in = [sem(f"y_in{i}") for i in range(BUF)]
        g_in = sem("final_gamma_in")
        summed = sem("combined")
        squared = sem("final_squared")
        rms_done = sem("final_rms_done")
        steps = Steps(sem("combine_steps"))
        block = mem.enter_context(nc.Block())

        @block.sync
        def _(sp):
            sp.dma_start(g_row[:], A["final_g"].to_broadcast([P, D])).then_inc(g_in, 16)

        @block.gpsimd
        def _(pool):
            for t in range(TT):
                if t >= BUF:
                    pool.wait_ge(summed, t - BUF + 1)
                for slot in range(2):
                    pool.indirect_dma_start(y[:, t % BUF, slot, :], None, m.y_dram,
                                            bass.IndirectOffsetOnAxis(ap=m.pair_row[:, slot, t:t + 1], axis=0)) \
                        .then_inc(y_in[t % BUF], 16)

        @block.scalar
        def _(act):
            for t in range(TT):
                act.wait_ge(summed, t + 1)
                if t:
                    act.wait_ge(squared, t)
                nc.scalar.activation(squares[:], m.res[:, t, :], ACT.Square, accum_out=sums[:, t:t + 1]) \
                    .then_inc(squared, 1)
                act.wait_ge(squared, t + 1)
                nc.scalar.activation(rms[:, t:t + 1], sums[:, t:t + 1], ACT.Sqrt, bias=m.eps[:], scale=1.0 / D) \
                    .then_inc(rms_done, 1)

        @block.vector
        def _(dve):
            def normalise(t):
                dve.wait_ge(rms_done, t + 1)
                steps.end(nc.vector.reciprocal(rstd[:, t:t + 1], rms[:, t:t + 1]))
                steps.wait(dve)
                nc.vector.scalar_tensor_tensor(out=m.res[:, t, :], in0=m.res[:, t, :], scalar=rstd[:, t:t + 1],
                                               in1=g_row[:], op0=ALU.mult, op1=ALU.mult)

            dve.wait_ge(g_in, 16)
            for t in range(TT):
                dve.wait_ge(y_in[t % BUF], 32 * (t // BUF + 1))
                for slot in range(2):
                    last = nc.vector.scalar_tensor_tensor(out=m.res[:, t, :], in0=y[:, t % BUF, slot, :],
                                                          scalar=m.pair_w[:, slot, t:t + 1], in1=m.res[:, t, :],
                                                          op0=ALU.mult, op1=ALU.add)
                    if slot == 0:
                        steps.end(last)
                        steps.wait(dve)
                last.then_inc(summed, 1)
                if t:
                    normalise(t - 1)
            normalise(TT - 1)


def mixture(nc, m, A):
    with ExitStack() as mem:
        m.pair_w = mem.enter_context(nc.sbuf_tensor("pair_w", [P, 2, TT], F32))
        m.pair_row = mem.enter_context(nc.sbuf_tensor("pair_row", [P, 2, TT], I32))
        m.over_table = mem.enter_context(nc.sbuf_tensor("over_table", [1, OVER + 1], I32))
        m.hn_dram = nc.dram_tensor("normed_rows", (SEQ, D), F32).ap()
        m.row_list = nc.dram_tensor("row_list", (CAP * BLOCKS, 1), I32).ap()
        with nc.sbuf_tensor("hT2", [P, KT, SEQ], F32) as hT:
            norm_to_T(nc, m, "norm2", hT, gamma_row=A["norm2_g"], rows_out=m.hn_dram)
            route(nc, m, A, hT)
        experts(nc, m, A)
        combine(nc, m, A)


def project_second(nc, m, A, hT):
    with ExitStack() as mem:
        sem = m.sem
        S = 2
        PAD = max(WINDOWS)
        LONG = PAD + SEQ
        place = m.res[:].rearrange("p t d -> p (t d)")
        ring = SplitRing(nc, m, mem, "qkvu_w", S, [KT, P],
                         [place[:, s * D:(s + 1) * D].rearrange("p (k c) -> p k c", k=KT) for s in range(S)])
        u = place[:, 2 * D:2 * D + 2 * LONG].rearrange("p (n c) -> p n c", n=2)
        sums = place[:, 5 * D:5 * D + 2 * LONG].rearrange("p (n c) -> p n c", n=2)
        w_g = mem.enter_context(nc.sbuf_tensor("pool_group_w", [P, HT, P], F32))
        edge = mem.enter_context(nc.sbuf_tensor("pool_edge", [P, len(WINDOWS), PAD], F32))
        pooled = m.attT
        ps = mem.enter_context(nc.psum_tensor("qkvu_ps", [P, 4, 2, BANK], F32))
        small_in = sem("pool_small_in")
        job_mm = sem("qkvu_job_mm")
        job_out = sem("qkvu_job_out")
        padded = sem("pool_padded")
        window = sem("pool_window")
        pooled_done = sem("pooled_done")
        block = mem.enter_context(nc.Block())
        jobs = [("u", 0), ("u", 1), ("q", 0), ("u", 2), ("g", 0), ("q", 1), ("u", 3), ("g", 1), ("q", 2), ("q", 3),
                ("g", 2), ("k", 0), ("k", 1), ("g", 3), ("k", 2), ("k", 3)]
        J = {job: j for j, job in enumerate(jobs)}
        first_col = {"q": 0, "k": ATT, "u": 3 * ATT}
        tiles = [job for job in jobs if job[0] != "g"]
        ring_n = {job: n for n, job in enumerate(tiles)}
        NW = len(tiles) + KT // 2

        def ring_source(n):
            if n < len(tiles):
                kind, c = tiles[n]
                at = first_col[kind] + c * P
                return A["w_in_2"][0].rearrange("(k p) n -> p k n", p=P)[:, :, at:at + P]
            k = 2 * (n - len(tiles))
            return A["w_in_2"][0, k * P:(k + 2) * P, 2 * ATT:3 * ATT].rearrange("(k p) (b c) -> p k b c", p=P, c=P)

        @block.sync
        def _(sp):
            sp.dma_start(m.bias_rows, A["rel_ext"].unsqueeze(1).to_broadcast([HEADS, P, EXT])).then_inc(m.bias_copied, 16)
            sp.dma_start(edge[:], A["pool_edge"]).then_inc(small_in, 16)
            sp.dma_start(w_g[:], A["w_pool_group_2"][0].rearrange("g c d -> c g d")).then_inc(small_in, 16)
            for n in range(NW):
                s, use = n % S, n // S
                if use:
                    sp.wait_ge(ring.rest_done[s], use)
                if n < len(tiles):
                    sp.dma_start(ring.raw[s], ring_source(n)).then_inc(ring.raw_in[s], 16)
                else:
                    sp.dma_start(ring.raw[s].rearrange("p (k b) c -> p k b c", k=2), ring_source(n)) \
                        .then_inc(ring.raw_in[s], 16)

        @block.tensor
        def _(pe):
            pe.wait_ge(small_in, 32)
            for j, (kind, c) in enumerate(jobs):
                if j >= 4:
                    pe.wait_ge(job_out, j - 3)
                if kind == "g":
                    pe.wait_ge(pooled_done, c + 1)
                    for half in range(2):
                        last = nc.tensor.matmul(ps[:, j % 4, half, :], w_g[:, c, :],
                                                pooled[:, c, half * BANK:(half + 1) * BANK], start=True, stop=True)
                    last.then_inc(job_mm, 1)
                    continue
                n = ring_n[kind, c]
                ring.arrived(pe, n % S, n // S)
                for half in range(2):
                    cols = slice(half * BANK, (half + 1) * BANK)
                    for k in range(KT):
                        last = product(nc, ps[:, j % 4, half, :], ring.parts(n % S, k),
                                       (hT[0][:, k, cols], hT[1][:, k, cols]), start=(k == 0), stop=(k == KT - 1))
                last.then_inc(ring.used[n % S], 1)
            pe.wait_ge(job_out, len(jobs))
            for kk in range(KT // 2):
                n = len(tiles) + kk
                ring.arrived(pe, n % S, n // S)
                for t in range(TT):
                    here = slice(t * P, (t + 1) * P)
                    for i in range(2):
                        k = 2 * kk + i
                        w = [part[:, n % S, 4 * i:4 * i + 4, :].rearrange("p b c -> p (b c)")
                             for part in (ring.high_part, ring.rest_part)]
                        last = product(nc, ps[:, t // 2, t % 2, :], (hT[0][:, k, here], hT[1][:, k, here]), w,
                                       start=(k == 0), stop=(k == KT - 1))
                last.then_inc(ring.used[n % S], 1)

        def job_done(engine, j):
            kind, c = jobs[j]
            if kind == "g":
                engine.wait_ge(job_mm, c + 1)
            else:
                n = ring_n[kind, c]
                engine.wait_ge(ring.used[n % S], n // S + 1)

        @block.scalar
        def _(act):
            split = 0
            for n in range(S):
                ring.high(act, n, 0, first=True)
            split = S
            for j, (kind, c) in enumerate(jobs):
                job_done(act, j)
                if kind != "g" and split < NW:
                    ring.high(act, split % S, split // S)
                    split += 1
                if j:
                    act.wait_ge(job_out, j)
                out = None
                if kind == "u":
                    act.wait_ge(padded, 1)
                    if c >= 2:
                        act.wait_ge(pooled_done, c - 1)
                    out = u[:, c % 2, PAD:]
                elif kind != "g":
                    out = (m.qT if kind == "q" else m.kT)[:, c, :]
                if out is not None:
                    nc.scalar.activation(out.rearrange("p (h c) -> p h c", h=2), ps[:, j % 4, :, :], ACT.Copy,
                                         scale=HEAD ** -0.5 if kind == "q" else 1.0).then_inc(job_out, 1)
            while split < NW:
                ring.high(act, split % S, split // S)
                split += 1
            n = NW - 1
            act.wait_ge(ring.used[n % S], n // S + 1)
            for t in range(TT):
                last = nc.scalar.activation(m.v[:, t, :], ps[:, t // 2, t % 2, :], ACT.Copy)

        @block.gpsimd
        def _(pool):
            done = Steps(window)
            for g in range(HT):
                pool.wait_ge(job_out, J["u", g] + 1)
                if g:
                    pool.wait_ge(pooled_done, g)
                for i in range(g + 1):
                    src = u[:, g % 2, :] if i == 0 else sums[:, (i - 1) % 2, :]
                    done.end(nc.gpsimd.tensor_tensor(sums[:, i % 2, PAD:], src[:, PAD:], src[:, PAD - 2 ** i:LONG - 2 ** i],
                                                     ALU.add))
                    done.wait(pool)
                if g == 0:
                    pool.wait_ge(small_in, 32)
                done.end(nc.gpsimd.tensor_tensor(sums[:, g % 2, PAD:2 * PAD], sums[:, g % 2, PAD:2 * PAD], edge[:, g, :],
                                                 ALU.mult))
                assert done.n == WINDOW_STEPS[g]

        @block.vector
        def _(dve):
            for a in (u, sums):
                last = nc.vector.memset(a[:, :, 0:PAD], 0.0)
            last.then_inc(padded, 1)
            for n in range(S):
                ring.rest(dve, n, 0)
            split, pooled_next = S, 0
            for j, (kind, c) in enumerate(jobs):
                if kind != "g":
                    if split < NW:
                        ring.rest(dve, split % S, split // S)
                        split += 1
                    if pooled_next < HT and J["u", pooled_next] < j:
                        g = pooled_next
                        dve.wait_ge(window, WINDOW_STEPS[g])
                        nc.vector.scalar_tensor_tensor(out=pooled[:, g, :], in0=sums[:, g % 2, PAD:],
                                                       scalar=1.0 / WINDOWS[g], in1=u[:, g % 2, PAD:], op0=ALU.mult,
                                                       op1=ALU.subtract).then_inc(pooled_done, 1)
                        pooled_next += 1
                else:
                    job_done(dve, j)
                    dve.wait_ge(job_out, j)
                    nc.vector.tensor_scalar(m.poolT[:, c, :].rearrange("p (h c) -> p h c", h=2), ps[:, j % 4, :, :],
                                            col(m.params, "pool_scale_2", c), None, ALU.mult).then_inc(job_out, 1)
            while split < NW:
                ring.rest(dve, split % S, split // S)
                split += 1


WINDOW_STEPS = [sum(i + 2 for i in range(g + 1)) for g in range(HT)]


def band_attention(nc, m, A):
    with ExitStack() as mem:
        def sb(name, shape, dt=F32):
            return mem.enter_context(nc.sbuf_tensor(name, shape, dt))

        sem = m.sem
        bias = m.res[:].rearrange("p t d -> p (t d)")[:, 0:HEADS * KEYS].rearrange("p (h k) -> p h k", h=HEADS)
        score = sb("score", [P, 3, KEYS])
        prob = sb("prob", [P, 3, KEYS])
        top = sb("top_score", [P, TT * HEADS])
        ntop = sb("neg_top", [P, TT * HEADS])
        total = sb("total", [P, TT, HEADS])
        inv = sb("inv_total", [P, TT, HEADS])
        probT = sb("probT", [P, 2, KEY_TILES, P])
        att = sb("att", [P, 2, ATT])
        ps_s = mem.enter_context(nc.psum_tensor("score_ps", [P, 2, 2 * BANK], F32))
        ps_p = mem.enter_context(nc.psum_tensor("prob_ps", [P, 2 * BANK], F32))
        ps_o = mem.enter_context(nc.psum_tensor("att_ps", [P, BANK], F32))
        ps_t = mem.enter_context(nc.psum_tensor("attT_ps", [P, BANK], F32))
        bias_in = sem("bias_in")
        masked = sem("bias_masked")
        score_mm = sem("score_mm")
        score_out = sem("score_out")
        ntop_done = sem("ntop_done")
        exp_done = sem("exp_done")
        turned = sem("prob_turned")
        probT_done = sem("probT_done")
        pv_mm = sem("pv_mm")
        inv_done = sem("inv_done")
        att_done = sem("att_done")
        att_turned = sem("att_turned")
        attT_done = sem("attT_done")
        block = mem.enter_context(nc.Block())
        ITEMS = [(i, h) for i in range(TT) for h in range(HEADS)]
        N = len(ITEMS)

        def key_tiles(i):
            return min(i + 1, KEY_TILES)

        @block.sync
        def _(sp):
            sp.wait_ge(m.bias_copied, 16)
            for h in range(HEADS):
                rows = bass.AP(tensor=m.bias_rows.tensor, offset=h * P * EXT + P - 1, ap=[[EXT - 1, P], [1, KEYS]])
                sp.dma_start(bias[:, h, :], rows).then_inc(bias_in, 16)

        @block.gpsimd
        def _(pool):
            pool.wait_ge(bias_in, 16 * HEADS)
            nc.gpsimd.memset(bias[0:CHUNK, :, BAND:KEYS], NEG).then_inc(masked, 1)
            nc.gpsimd.memset(bias[CHUNK:P, :, 0:CHUNK], NEG).then_inc(masked, 1)

        @block.tensor
        def _(pe):
            def scores(n):
                i, h = ITEMS[n]
                rows = slice(HEAD * (h % 2), HEAD * (h % 2 + 1))
                width = key_tiles(i) * P
                first_key = (i + 1) * P - width
                if n >= 2:
                    pe.wait_ge(score_out, n - 1)
                for at in range(0, width, BANK):
                    n_keys = min(BANK, width - at)
                    last = nc.tensor.matmul(ps_s[:, n % 2, at:at + n_keys], m.qT[rows, h // 2, i * P:(i + 1) * P],
                                            m.kT[rows, h // 2, first_key + at:first_key + at + n_keys],
                                            start=True, stop=True)
                last.then_inc(score_mm, 1)

            def turn(n):
                i, h = ITEMS[n]
                pe.wait_ge(exp_done, n + 1)
                if n:
                    pe.wait_ge(probT_done, n)
                for j in range(key_tiles(i)):
                    last = nc.tensor.transpose(ps_p[:, j * P:(j + 1) * P], prob[:, n % 3, j * P:(j + 1) * P], m.ident[:])
                last.then_inc(turned, 1)

            def values(n):
                i, h = ITEMS[n]
                nk = key_tiles(i)
                pe.wait_ge(probT_done, n + 1)
                if h == 0 and i:
                    pe.wait_ge(att_done, i)
                for j in range(nk):
                    last = nc.tensor.matmul(ps_o[:, h * HEAD:(h + 1) * HEAD], probT[:, n % 2, j, :],
                                            m.v[:, i + 1 - nk + j, h * HEAD:(h + 1) * HEAD],
                                            start=(j == 0), stop=(j == nk - 1))
                last.then_inc(pv_mm, 1)

            def out(i):
                pe.wait_ge(att_done, i + 1)
                if i:
                    pe.wait_ge(attT_done, i)
                for c in range(HT):
                    last = nc.tensor.transpose(ps_t[:, c * P:(c + 1) * P], att[:, i % 2, c * P:(c + 1) * P], m.ident[:])
                last.then_inc(att_turned, 1)

            scores(0)
            scores(1)
            for n in range(N):
                if n + 2 < N:
                    scores(n + 2)
                turn(n)
                if n:
                    values(n - 1)
                if n % HEADS == 3 and n > HEADS:
                    out(n // HEADS - 1)
            values(N - 1)
            out(TT - 1)

        @block.scalar
        def _(act):
            def leave(n):
                nk = key_tiles(ITEMS[n][0])
                act.wait_ge(turned, n + 1)
                if n >= 2:
                    act.wait_ge(pv_mm, n - 1)
                nc.scalar.activation(probT[:, n % 2, 0:nk, :].rearrange("p j q -> p (j q)"), ps_p[:, 0:nk * P], ACT.Copy) \
                    .then_inc(probT_done, 1)

            for n, (i, h) in enumerate(ITEMS):
                width = key_tiles(i) * P
                act.wait_ge(ntop_done, n + 1)
                if n >= 3:
                    act.wait_ge(turned, n - 2)
                nc.scalar.activation(prob[:, n % 3, 0:width], score[:, n % 3, 0:width], ACT.Exp,
                                     bias=ntop[:, n:n + 1], accum_out=total[:, i, h:h + 1]).then_inc(exp_done, 1)
                if n:
                    leave(n - 1)
            leave(N - 1)

        @block.vector
        def _(dve):
            def head_out(i):
                dve.wait_ge(exp_done, (i + 1) * HEADS)
                nc.vector.reciprocal(inv[:, i, :], total[:, i, :]).then_inc(inv_done, 1)
                dve.wait_ge(inv_done, i + 1)
                dve.wait_ge(pv_mm, (i + 1) * HEADS)
                if i >= 2:
                    dve.wait_ge(att_turned, i - 1)
                nc.vector.tensor_tensor(att[:, i % 2, :].rearrange("p (h d) -> p h d", h=HEADS),
                                        ps_o[:].rearrange("p (h d) -> p h d", h=HEADS),
                                        inv[:, i, :].unsqueeze(2).to_broadcast([P, HEADS, HEAD]), ALU.mult) \
                    .then_inc(att_done, 1)

            def turned_out(i):
                dve.wait_ge(att_turned, i + 1)
                nc.vector.tensor_copy(m.attT[:, :, i * P:(i + 1) * P], ps_t[:].rearrange("p (c q) -> p c q", c=HT)) \
                    .then_inc(attT_done, 1)

            dve.wait_ge(masked, 2)
            for n, (i, h) in enumerate(ITEMS):
                width = key_tiles(i) * P
                dve.wait_ge(score_mm, n + 1)
                if n >= 3:
                    dve.wait_ge(exp_done, n - 2)
                nc.vector.tensor_tensor(score[:, n % 3, 0:width], ps_s[:, n % 2, 0:width],
                                        bias[:, h, KEYS - width:KEYS], ALU.add).then_inc(score_out, 1)
                dve.wait_ge(score_out, n + 1)
                nc.vector.tensor_reduce(top[:, n:n + 1], score[:, n % 3, 0:width], AX_X, ALU.max) \
                    .then_inc(m.top_done, 1)
                dve.wait_ge(m.top_done, n + 1)
                nc.vector.tensor_scalar(ntop[:, n:n + 1], top[:, n:n + 1], -1.0, None, ALU.mult).then_inc(ntop_done, 1)
                if n % HEADS == 2 and n > HEADS:
                    head_out(n // HEADS - 1)
                if n % HEADS == 5 and n > HEADS:
                    turned_out(n // HEADS - 1)
            head_out(TT - 1)
            turned_out(TT - 1)


def gated_mix(nc, m, A, hT):
    with ExitStack() as mem:
        sem = m.sem
        S = 2
        place = [m.res[:, i, :] for i in range(TT)]
        ring = SplitRing(nc, m, mem, "gates_w", S, [KT, P], [place[s].rearrange("p (k c) -> p k c", k=KT) for s in range(S)])
        w_out = mem.enter_context(nc.sbuf_tensor("branches_w", [P, 2, S, HT, P], F32))
        gate = [place[2 + s] for s in range(S)]
        part = [place[4 + s] for s in range(S)]
        ps_g = mem.enter_context(nc.psum_tensor("gates_ps", [P, S, 2, BANK], F32))
        ps_y = mem.enter_context(nc.psum_tensor("branches_ps", [P, S, 2, BANK], F32))
        w_in = [[sem(f"branch_w_in{s}{odd}") for odd in range(2)] for s in range(S)]
        gate_out = [sem(f"gate_out{s}") for s in range(S)]
        branch_mm = [sem(f"branch_mm{s}") for s in range(S)]
        branch_out = [sem(f"branch_out{s}") for s in range(S)]
        mixed = sem("mixed")
        block = mem.enter_context(nc.Block())
        first_gate = 4 * ATT // P
        w2 = A["w_in_2"][0].rearrange("(k p) n -> p k n", p=P)
        outs = [A[n][0].rearrange("(k p) n -> p k n", p=P) for n in ("w_attn_out_2", "w_pool_out_2")]

        @block.sync
        def _(sp):
            def load(s, d, odd, first_gate_load, first_out_load):
                ring.load(sp, s, d, w2[:, :, bass.ds((d + (first_gate + s * KT)) * P, P)], first=first_gate_load)
                if not first_out_load:
                    sp.wait_ge(branch_mm[s], d - 1)
                sp.dma_start(w_out[:, odd, s, :, :], outs[s][:, :, bass.ds(d * P, P)]).then_inc(w_in[s][odd], 16)

            for d in range(2):
                for s in range(S):
                    load(s, d, d, d == 0, True)
            with sp.Fori(1, KT // 2) as i:
                for odd in range(2):
                    for s in range(S):
                        load(s, i * 2 + odd, odd, False, False)

        @block.tensor
        def _(pe):
            def feature_tile(d, odd, use, first=False):
                for s in range(S):
                    ring.arrived(pe, s, d)
                    if not first:
                        pe.wait_ge(gate_out[s], d)
                    for half in range(2):
                        cols = slice(half * BANK, (half + 1) * BANK)
                        for k in range(KT):
                            last = product(nc, ps_g[:, s, half, :], ring.parts(s, k), (hT[0][:, k, cols], hT[1][:, k, cols]),
                                           start=(k == 0), stop=(k == KT - 1))
                    last.then_inc(ring.used[s], 1)
                for s, data in enumerate((m.attT, m.poolT)):
                    pe.wait_ge(w_in[s][odd], (use + 1) * 16)
                    if not first:
                        pe.wait_ge(branch_out[s], d)
                    for half in range(2):
                        for k in range(HT):
                            last = nc.tensor.matmul(ps_y[:, s, half, :], w_out[:, odd, s, k, :],
                                                    data[:, k, half * BANK:(half + 1) * BANK],
                                                    start=(k == 0), stop=(k == HT - 1))
                    last.then_inc(branch_mm[s], 1)

            for d in range(2):
                feature_tile(d, d, 0, first=(d == 0))
            with pe.Fori(1, KT // 2) as i:
                for odd in range(2):
                    feature_tile(i * 2 + odd, odd, i)

        @block.scalar
        def _(act):
            at, _ = COLS["b_gate_2"]

            def sigmoid(d, first=False, last=False):
                for s in range(S):
                    act.wait_ge(ring.used[s], d + 1)
                    if not last:
                        ring.high(act, s, d + 1)
                    if not first:
                        act.wait_ge(branch_out[s], d)
                    nc.scalar.activation(gate[s].rearrange("p (h c) -> p h c", h=2), ps_g[:, s, :, :],
                                         ACT.Sigmoid, bias=m.params[:, bass.ds(d + (at + s * KT), 1)]) \
                        .then_inc(gate_out[s], 1)

            for s in range(S):
                ring.high(act, s, 0, first=True)
            sigmoid(0, first=True)
            with act.Fori(1, KT - 1) as d:
                sigmoid(d)
            sigmoid(KT - 1, last=True)

        @block.vector
        def _(dve):
            def mix(d, first=False, last=False):
                if not last:
                    for s in range(S):
                        ring.rest(dve, s, d + 1)
                for s in range(S):
                    dve.wait_ge(branch_mm[s], d + 1)
                    dve.wait_ge(gate_out[s], d + 1)
                    nc.vector.tensor_tensor(part[s].rearrange("p (h c) -> p h c", h=2),
                                            gate[s].rearrange("p (h c) -> p h c", h=2),
                                            ps_y[:, s, :, :], ALU.mult).then_inc(branch_out[s], 1)
                dve.wait_ge(branch_out[1], d + 1)
                nc.vector.tensor_tensor(m.mixT[:, bass.ds(d, 1), :].rearrange("p o c -> p (o c)"), part[0],
                                        part[1], ALU.add).then_inc(mixed, 1)
                dve.wait_ge(mixed, d + 1)

            for s in range(S):
                ring.rest(dve, s, 0)
            mix(0, first=True)
            with dve.Fori(1, KT - 1) as d:
                mix(d)
            mix(KT - 1, last=True)


class PostNorm:

    def __init__(self, nc, m, mem, name):
        def sb(part, shape):
            return mem.enter_context(nc.sbuf_tensor(f"{name}_{part}", shape, F32))

        self.squares = sb("squares", [P, D])
        self.sums = sb("sums", [P, TT])
        self.rms = sb("rms", [P, TT])
        self.rstd = sb("rstd", [P, TT])
        self.scaled = sb("scaled", [P, 2, D])
        self.gamma = sb("gamma", [P, D])
        self.gamma_in = m.sem(f"{name}_gamma_in")
        self.res_in = m.sem(f"{name}_res_in")
        self.squared = m.sem(f"{name}_squared")
        self.rms_done = m.sem(f"{name}_rms_done")
        self.rstd_done = m.sem(f"{name}_rstd_done")
        self.left_psum = m.sem(f"{name}_left_psum")
        self.added = m.sem(f"{name}_added")

    def scalar_part(self, nc, act, m, t, ps):
        if t:
            act.wait_ge(self.squared, t)
        nc.scalar.activation(self.squares[:].rearrange("p (h c) -> p h c", h=2), ps, ACT.Square,
                             accum_out=self.sums[:, t:t + 1]).then_inc(self.squared, 1)
        act.wait_ge(self.squared, t + 1)
        nc.scalar.activation(self.rms[:, t:t + 1], self.sums[:, t:t + 1], ACT.Sqrt, bias=m.eps[:], scale=1.0 / D) \
            .then_inc(self.rms_done, 1)

    def vector_part(self, nc, dve, m, t, ps):
        if t == 0:
            dve.wait_ge(self.gamma_in, 16)
            dve.wait_ge(self.res_in, 16)
        dve.wait_ge(self.rms_done, t + 1)
        nc.vector.reciprocal(self.rstd[:, t:t + 1], self.rms[:, t:t + 1]).then_inc(self.rstd_done, 1)
        dve.wait_ge(self.rstd_done, t + 1)
        nc.vector.scalar_tensor_tensor(out=self.scaled[:, t % 2, :].rearrange("p (h c) -> p h c", h=2), in0=ps,
                                       scalar=self.rstd[:, t:t + 1],
                                       in1=self.gamma[:].rearrange("p (h c) -> p h c", h=2),
                                       op0=ALU.mult, op1=ALU.mult).then_inc(self.left_psum, 1)
        dve.wait_ge(self.left_psum, t + 1)
        nc.vector.tensor_tensor(m.res[:, t, :], m.res[:, t, :], self.scaled[:, t % 2, :], ALU.add) \
            .then_inc(self.added, 1)


def mix_output(nc, m, A, raw):
    with ExitStack() as mem:
        norm = PostNorm(nc, m, mem, "mix_post")
        ps = mem.enter_context(nc.psum_tensor("w_o_ps", [P, 4, 2, BANK], F32))
        wide = WideProduct(nc, m, mem, "w_o", m.mixT, A["w_o_2"][0], raw, ps)
        block = mem.enter_context(nc.Block())

        @block.sync
        def _(sp):
            wide.load(sp)
            sp.dma_start(norm.gamma[:], A["norm_mix_post_2"].to_broadcast([P, D])).then_inc(norm.gamma_in, 16)
            sp.dma_start(m.res[:], m.res_dram.rearrange("(t p) d -> p t d", p=P)).then_inc(norm.res_in, 16)

        @block.tensor
        def _(pe):
            for t in range(TT):
                wide.tile_product(pe, t, norm.left_psum, t - 3)

        @block.scalar
        def _(act):
            wide.tile_high(act, 0)
            for k in range(KT):
                wide.weight_high(act, k)
            wide.tile_high(act, 1)
            for t in range(TT):
                act.wait_ge(wide.done, t + 1)
                if t + 2 < TT:
                    wide.tile_high(act, t + 2)
                norm.scalar_part(nc, act, m, t, ps[:, t % 4, :, :])

        @block.vector
        def _(dve):
            wide.tile_rest(dve, 0)
            for k in range(KT):
                wide.weight_rest(dve, k)
            wide.tile_rest(dve, 1)
            for t in range(TT):
                if t + 2 < TT:
                    wide.tile_rest(dve, t + 2)
                norm.vector_part(nc, dve, m, t, ps[:, t % 4, :, :])


def ffn_up(nc, m, A, hT, prodT):
    with ExitStack() as mem:
        sem = m.sem
        S = 2
        ring = SplitRing(nc, m, mem, "w_up_2", S, [KT, P], [m.res[:, s, :].rearrange("p (k c) -> p k c", k=KT) for s in range(S)])
        gates = m.res[:, S:2 * S, :]
        ps = mem.enter_context(nc.psum_tensor("up_ps", [P, 2, S, 2, BANK], F32))
        centre = [sem(f"ffn_centre{s}") for s in range(S)]
        near = [sem(f"ffn_near_tap{s}") for s in range(S)]
        far = [sem(f"ffn_far_tap{s}") for s in range(S)]
        gelu = sem("ffn_gelu")
        prod = sem("ffn_prod")
        block = mem.enter_context(nc.Block())
        taps_at, bias_at = COLS["conv_w_2"][0], COLS["conv_b_2"][0]
        weights = A["w_up_2"][0].rearrange("(k p) n -> p k n", p=P)

        def tile_of(f, odd, s):
            return gates[:, odd, :] if s else prodT[:, bass.ds(f, 1), :].rearrange("p o c -> p (o c)")

        @block.sync
        def _(sp):
            for s in range(S):
                ring.load(sp, s, 0, weights[:, :, s * D_FF:s * D_FF + P], first=True)
            with sp.Fori(1, FT) as f:
                for s in range(S):
                    ring.load(sp, s, f, weights[:, :, bass.ds((f + s * FT) * P, P)])

        @block.tensor
        def _(pe):
            def tile(f, odd, first=False):
                for s in range(S):
                    ring.arrived(pe, s, f)
                    if not first:
                        pe.wait_ge(far[s], f - 1)
                    for half in range(2):
                        cols = slice(half * BANK, (half + 1) * BANK)
                        for k in range(KT):
                            last = product(nc, ps[:, odd, s, half, :], ring.parts(s, k),
                                           (hT[0][:, k, cols], hT[1][:, k, cols]), start=(k == 0), stop=(k == KT - 1))
                    last.then_inc(ring.used[s], 1)

            for f in range(2):
                tile(f, f, first=True)
            with pe.Fori(1, FT // 2) as i:
                for odd in range(2):
                    tile(i * 2 + odd, odd)

        @block.scalar
        def _(act):
            def tile(f, odd, first=False, last=False):
                for s in range(S):
                    act.wait_ge(ring.used[s], f + 1)
                    if not last:
                        ring.high(act, s, f + 1)
                    if s and not first:
                        act.wait_ge(prod, f - 1)
                    nc.scalar.activation(tile_of(f, odd, s).rearrange("p (h c) -> p h c", h=2), ps[:, odd, s, :, :],
                                         ACT.Identity, bias=m.params[:, bass.ds(f + (bias_at + s * FT), 1)],
                                         scale=m.params[:, bass.ds(f + (taps_at + (4 + s) * FT), 1)]) \
                        .then_inc(centre[s], 1)
                act.wait_ge(far[1], f + 1)
                nc.scalar.activation(gates[:, odd, :], gates[:, odd, :], ACT.Gelu_apprx_tanh).then_inc(gelu, 1)

            for s in range(S):
                ring.high(act, s, 0, first=True)
            for f in range(2):
                tile(f, f, first=True)
            with act.Fori(1, FT // 2 - 1) as i:
                for odd in range(2):
                    tile(i * 2 + odd, odd)
            tile(FT - 2, 0)
            tile(FT - 1, 1, last=True)

        @block.vector
        def _(dve):
            def tile(f, odd, last=False):
                for s in range(S):
                    if not last:
                        ring.rest(dve, s, f + 1)
                    dve.wait_ge(centre[s], f + 1)
                    raw = ps[:, odd, s, :, :].rearrange("p h c -> p (h c)")
                    for back, done in ((1, near), (2, far)):
                        if back == 2:
                            dve.wait_ge(near[s], f + 1)
                        into = tile_of(f, odd, s)[:, back:SEQ]
                        nc.vector.scalar_tensor_tensor(
                            out=into, in0=raw[:, 0:SEQ - back],
                            scalar=m.params[:, bass.ds(f + (taps_at + (2 * (2 - back) + s) * FT), 1)],
                            in1=into, op0=ALU.mult, op1=ALU.add).then_inc(done[s], 1)
                dve.wait_ge(gelu, f + 1)
                value = tile_of(f, odd, 0)
                nc.vector.tensor_tensor(value, value, gates[:, odd, :], ALU.mult).then_inc(prod, 1)

            for s in range(S):
                ring.rest(dve, s, 0)
            with dve.Fori(0, FT // 2 - 1) as i:
                for odd in range(2):
                    tile(i * 2 + odd, odd)
            tile(FT - 2, 0)
            tile(FT - 1, 1, last=True)


def ffn_down(nc, m, A, prodT):
    with ExitStack() as mem:
        sem = m.sem
        S = 3
        QUAD = 4
        N = 2 * FT
        raw = mem.enter_context(nc.sbuf_tensor("w_down_raw", [P, S, D], F32))
        ring = SplitRing(nc, m, mem, "w_down_2", S, [D], [raw[:, s, :] for s in range(S)])
        x_high = mem.enter_context(nc.sbuf_tensor("prod_high", [P, S, QUAD * P], F32R))
        x_rest = mem.enter_context(nc.sbuf_tensor("prod_rest", [P, S, QUAD * P], F32R))
        norm = PostNorm(nc, m, mem, "ffn_post")
        ps = mem.enter_context(nc.psum_tensor("down_ps", [P, QUAD, 2, BANK], F32))
        x_high_done = sem("prod_high_done")
        x_rest_done = sem("prod_rest_done")
        stored = sem("stored")
        block = mem.enter_context(nc.Block())

        def hidden(n):
            return prodT[:, n % FT, n // FT * QUAD * P:(n // FT + 1) * QUAD * P]

        @block.sync
        def _(sp):
            for n in range(N):
                f = n % FT
                ring.load(sp, n % S, n // S, A["w_down_2"][0, f * P:(f + 1) * P, :], first=(n < S))
                if n == S:
                    sp.dma_start(norm.gamma[:], A["norm_ffn_post_2"].to_broadcast([P, D])).then_inc(norm.gamma_in, 16)
                    sp.dma_start(m.res[:], m.res_dram.rearrange("(t p) d -> p t d", p=P)).then_inc(norm.res_in, 16)
            for t in range(TT):
                sp.wait_ge(norm.added, t + 1)
                sp.dma_start(A["out"][0, t * P:(t + 1) * P, :], m.res[:, t, :]).then_inc(stored, 16)
            sp.wait_ge(stored, 16 * TT)

        @block.tensor
        def _(pe):
            for n in range(N):
                turn, f, s = n // FT, n % FT, n % S
                ring.arrived(pe, s, n // S)
                pe.wait_ge(x_rest_done, n + 1)
                for q in range(QUAD):
                    if turn and f == 0:
                        pe.wait_ge(norm.left_psum, q + 1)
                    here = slice(q * P, (q + 1) * P)
                    for half in range(2):
                        last = product(nc, ps[:, q, half, :], (x_high[:, s, here], x_rest[:, s, here]),
                                       ring.parts(s, slice(half * BANK, (half + 1) * BANK)),
                                       start=(f == 0), stop=(f == FT - 1))
                last.then_inc(ring.used[s], 1)

        def quad_done(engine, turn):
            n = (turn + 1) * FT - 1
            engine.wait_ge(ring.used[n % S], n // S + 1)

        @block.scalar
        def _(act):
            for n in range(N):
                ring.high(act, n % S, n // S, first=(n < S))
                nc.scalar.activation(x_high[:, n % S, :], hidden(n), ACT.Copy).then_inc(x_high_done, 1)
                if n == FT + S - 1:
                    quad_done(act, 0)
                    for t in range(QUAD):
                        norm.scalar_part(nc, act, m, t, ps[:, t, :, :])
            quad_done(act, 1)
            for t in range(QUAD, TT):
                norm.scalar_part(nc, act, m, t, ps[:, t % QUAD, :, :])

        @block.vector
        def _(dve):
            for n in range(N):
                ring.rest(dve, n % S, n // S)
                dve.wait_ge(x_high_done, n + 1)
                nc.vector.tensor_tensor(x_rest[:, n % S, :], hidden(n), x_high[:, n % S, :].bitcast(F32), ALU.subtract) \
                    .then_inc(x_rest_done, 1)
                if n == FT + S - 1:
                    for t in range(QUAD):
                        norm.vector_part(nc, dve, m, t, ps[:, t, :, :])
            for t in range(QUAD, TT):
                norm.vector_part(nc, dve, m, t, ps[:, t % QUAD, :, :])


def second_block(nc, m, A):
    m.res_dram = nc.dram_tensor("residual", (SEQ, D), F32).ap()
    m.bias_rows = nc.dram_tensor("bias_rows", (HEADS, P, EXT), F32).ap()
    m.bias_copied = m.sem("bias_copied")
    with ExitStack() as mem:
        m.mixT = mem.enter_context(nc.sbuf_tensor("mixT2", [P, KT, SEQ], F32))
        with ExitStack() as mem2:
            def sb(name, shape, dt=F32):
                return mem2.enter_context(nc.sbuf_tensor(name, shape, dt))

            m.attT = sb("attT", [P, HT, SEQ])
            m.poolT = sb("poolT", [P, HT, SEQ])
            hT = sb("hT3_high", [P, KT, SEQ], F32R), sb("hT3_rest", [P, KT, SEQ], F32R)
            norm_to_T(nc, m, "norm3", hT, gamma="norm_mix_pre_2", res_out=m.res_dram)
            m.qT = m.mixT[:, 0:HT, :]
            m.kT = m.mixT[:, HT:2 * HT, :]
            with nc.sbuf_tensor("v", [P, TT, ATT], F32) as m.v:
                project_second(nc, m, A, hT)
                band_attention(nc, m, A)
            gated_mix(nc, m, A, hT)
        with nc.sbuf_tensor("w_o_raw", [P, 2, D], F32) as raw:
            mix_output(nc, m, A, [raw[:, i, :] for i in range(2)])
    with nc.sbuf_tensor("prodT", [P, FT, SEQ], F32) as prodT:
        with nc.sbuf_tensor("hT4_high", [P, KT, SEQ], F32R) as high, nc.sbuf_tensor("hT4_rest", [P, KT, SEQ], F32R) as rest:
            norm_to_T(nc, m, "norm4", (high, rest), gamma="norm_ffn_pre_2", res_out=m.res_dram)
            ffn_up(nc, m, A, (high, rest), prodT)
        ffn_down(nc, m, A, prodT)


def build_program(nc, A):
    with ExitStack() as ctx:
        m = Shared(nc, ctx)
        with m.section(nc):
            first_mixer(nc, m, A)
        with m.section(nc):
            mixture(nc, m, A)
        with m.section(nc):
            second_block(nc, m, A)


class Shared:

    def __init__(self, nc, ctx):
        def sb(name, shape, dt=F32):
            return ctx.enter_context(nc.sbuf_tensor(name, shape, dt))

        self.sem = nc.alloc_semaphore
        self.params = sb("params", [P, N_COLS])
        self.ident = sb("ident", [P, P])
        self.ones = sb("ones", [P, P])
        self.inv_size = sb("inv_size", [P, HT])
        self.eps = sb("eps", [P, 1])
        self.res = sb("res", [P, TT, D])
        self.eps_set = self.sem("eps_set")
        self.y_dram = nc.dram_tensor("expert_rows", (ROWS, D), F32).ap()
        self.top_done = self.sem("top_done")
        self.x_in = self.sem("x_in")
        self.consts_set = self.sem("consts_set")

    @contextmanager
    def section(self, nc):
        whole, made = self.sem, []

        def sem(name):
            made.append(nc.alloc_semaphore(name))
            return made[-1]

        self.sem = sem
        yield
        self.sem = whole
        nc.clear_and_free_semaphores(made)
        nc.all_engine_barrier()


def _tables():
    j = np.arange(SEQ, dtype=np.float64)
    split = np.concatenate([j[0::2], j[1::2]])
    half = np.arange(HALF, dtype=np.float64) + 0.5
    angle = np.pi / SEQ * np.outer(split, half)
    trig = np.stack([np.cos(angle[:HALF]), np.cos(angle[HALF:]), np.sin(angle[:HALF]), np.sin(angle[HALF:])])
    back = trig.reshape(2, 2, HALF, HALF).transpose(1, 0, 3, 2) / SEQ
    whole = 2 * np.pi / SEQ * np.outer(split, np.arange(HALF, dtype=np.float64))
    scale = 1.0 / np.sqrt(SEQ * HEAD)
    dft = np.stack([np.cos(whole[:HALF]), -np.sin(whole[:HALF]), np.cos(whole[HALF:]), -np.sin(whole[HALF:])]) * scale
    d = np.arange(HEAD, dtype=np.float64)
    small = 2 * np.pi / HEAD * np.outer(d, d)
    pair = np.zeros((P, 2, P))
    for i in range(P // HEAD):
        s = slice(i * HEAD, (i + 1) * HEAD)
        pair[s, 0, s] = np.cos(small)
        pair[s, 1, s] = np.sin(small)
    in_head = (np.arange(D)[:, None] // HEAD == np.arange(D // HEAD)).reshape(KT, P, D // HEAD)
    t = np.linspace(0.0, 1.0, SEQ, dtype=np.float32)
    w = np.float32(2.0 * np.pi / SEQ) * np.arange(SEQ, dtype=np.float32)
    f = np.linspace(1e-4, F_BANDS - 1, F_BANDS, dtype=np.float32)
    fw = (f[:, None] * w[None, :]).astype(np.float32)
    positions = np.concatenate([t[None, :], np.cos(fw), -np.sin(fw)])
    rates = np.abs(np.linspace(np.log(1e-2) / 1.5, np.log(1e-2) / 0.3, D_HYENA))
    decay = np.exp(-t[split.astype(np.int64)][:, None].astype(np.float64) * rates[None, :])
    count = np.minimum(np.arange(max(WINDOWS))[None, :] + 1, np.array(WINDOWS)[:, None])
    edge = np.broadcast_to(np.array(WINDOWS)[:, None] / count, (P, len(WINDOWS), max(WINDOWS)))
    before = np.triu(np.ones((P, P)), 1)
    out = dict(half_tables=trig, back_tables=back, dft_tables=dft, pair_table=pair, head_pick=in_head.transpose(1, 0, 2) / HEAD,
               head_spread=in_head.transpose(2, 0, 1),
               positions=positions, decay=decay, pool_edge=edge, before=before,
               index_rows=np.stack([np.arange(EXPERTS) - 64, np.arange(EXPERTS)])[None],
               limits=CAP * np.arange(1, FULL_BLOCKS)[None, :])
    return {k: np.ascontiguousarray(v, dtype=np.float32) for k, v in out.items()}


def _laid_out(inputs):
    a = {k: np.asarray(v) for k, v in inputs.items()}
    out = _tables()
    for name in ("x", "w_in", "f_w_in", "f_w_mid", "f_w_out", "w_out", "norm2_g", "w_gate", "w_up", "w_down",
                 "w_in_2", "w_attn_out_2", "w_pool_group_2", "w_pool_out_2", "w_o_2", "norm_mix_post_2",
                 "w_up_2", "w_down_2", "norm_ffn_post_2"):
        out[name] = a[name]
    out["final_g"] = a["final_g"].reshape(1, D)

    def cols(v):
        return v.reshape(-1, P).T

    def short(v):
        return np.pad(v.T, ((0, P - v.shape[1]), (0, 0)))

    packed = {n: cols(a[n]) for n in COLS if n in a and n not in ("conv_w", "conv_w_2", "f_freq")}
    for n in ("conv_w", "conv_w_2"):
        packed[n] = a[n].reshape(3 * a[n].shape[2] // P, P).T
    packed["f_b"] = short(np.concatenate([a["f_b_in"], a["f_b_mid"][0]]))
    packed["f_freq"] = short(a["f_freq"][0])
    out["params"] = np.concatenate([packed[n] for n in COLS], axis=1)
    assert out["params"].shape == (P, N_COLS)
    out["w_router"] = np.concatenate([a["w_group"][0]] + [a["w_router"][0, g] for g in range(GROUPS)], axis=1)
    out["b_router"] = np.concatenate([a["b_group"][0], a["b_router"][0].reshape(-1)])[None, :]
    dist = np.clip(np.arange(EXT)[::-1] - (P - 1), -REL, REL) + REL
    out["rel_ext"] = a["rel_bias_2"][0][:, dist]
    return {k: np.ascontiguousarray(v) for k, v in out.items()}


def kernel(**inputs):
    import concourse.bacc as bacc
    from concourse.bass_utils import run_bass_kernel_spmd

    nc = bacc.Bacc("TRN2", target_bir_lowering=False, num_devices=1)
    arrays, A = {}, {}
    for name, a in _laid_out(inputs).items():
        arrays[f"in_{name}_dram"] = a
        A[name] = nc.dram_tensor(f"in_{name}_dram", a.shape, mybir.dt.from_np(a.dtype), kind="ExternalInput").ap()
    A["out"] = nc.dram_tensor("out_0_dram", (1, SEQ, D), F32, kind="ExternalOutput").ap()
    build_program(nc, A)
    r = run_bass_kernel_spmd(nc, [arrays], core_ids=[0])
    return r.results[0]["out_0_dram"]
```

```python
from contextlib import ExitStack, contextmanager

import numpy as np

import concourse.bass as bass
from concourse import mybir

ALU = mybir.AluOpType
ACT = mybir.ActivationFunctionType
AX_X = mybir.AxisListType.X
F32 = mybir.dt.float32
I32 = mybir.dt.int32


F32R = mybir.dt.float32r

P = 128
SEQ = 1024
D = 1024
TT = SEQ // P
KT = D // P
BANK = 512
EPS = 1e-6

D_HYENA = 512
HT = D_HYENA // P
HEAD = 64
F_EMB = 33
F_BANDS = (F_EMB - 1) // 2
F_ORDER = 64
HALF = SEQ // 2
JT = HALF // P
TWO_PI = 2.0 * np.pi

GROUPS = 4
PER_GROUP = 8
EXPERTS = GROUPS * PER_GROUP
D_EXPERT = 512
CAP = 88
OVER = 2 * SEQ // (CAP + 1)
FULL_BLOCKS = (SEQ + CAP - 1) // CAP
BLOCKS = EXPERTS + OVER
ROWS = BLOCKS * CAP
NL = GROUPS + EXPERTS
WSLOTS = 3

HEADS = 8
ATT = HEADS * HEAD
CHUNK = 64
BAND = 9 * CHUNK
KEYS = BAND + CHUNK
KEY_TILES = KEYS // P
REL = 256
EXT = P + KEYS - 1
WINDOWS = (2, 4, 8, 16)
D_FF = 2816
FT = D_FF // P
NEG = -1e30
ROUND = 1.5 * 2.0 ** 23
TWO_PI_HIGH = 6.28125
TWO_PI_LOW = TWO_PI - TWO_PI_HIGH
PI_BELOW = 3.1415925

COLS = {}
_at = 0
for _name, _n in (("norm1_g", KT), ("conv_w", 3 * 3 * HT), ("conv_b", 3 * HT), ("f_bias", HT), ("mix_g", KT),
                  ("norm_mix_pre_2", KT), ("b_gate_2", 2 * KT), ("pool_scale_2", HT), ("norm_ffn_pre_2", KT),
                  ("conv_w_2", 3 * 2 * FT), ("conv_b_2", 2 * FT), ("f_b", 3), ("f_freq", 3)):
    COLS[_name] = (_at, _n)
    _at += _n
N_COLS = _at


def col(params, name, i, rows=P):
    at, n = COLS[name]
    assert 0 <= i < n
    return params[0:rows, at + i:at + i + 1]


class Steps:

    def __init__(self, sem):
        self.sem = sem
        self.n = 0

    def end(self, instruction):
        self.n += 1
        instruction.then_inc(self.sem, 1)

    def wait(self, engine):
        engine.wait_ge(self.sem, self.n)


def product(nc, out, w, x, start, stop):
    (w_high, w_rest), (x_high, x_rest) = w, x
    nc.tensor.matmul(out, w_high, x_high, start=start, stop=False)
    nc.tensor.matmul(out, w_high, x_rest, start=False, stop=False)
    return nc.tensor.matmul(out, w_rest, x_high, start=False, stop=stop)


def keep_clock(nc, m, out, n):
    for _ in range(n):
        nc.tensor.matmul(out, m.ident[:], m.ones[:], start=True, stop=True)


class SplitRing:

    def __init__(self, nc, m, mem, name, slots, shape, raw):
        self.nc = nc
        self.raw = raw
        self.high_part = mem.enter_context(nc.sbuf_tensor(f"{name}_high", [P, slots] + shape, F32R))
        self.rest_part = mem.enter_context(nc.sbuf_tensor(f"{name}_rest", [P, slots] + shape, F32R))
        self.raw_in = [m.sem(f"{name}_raw_in{s}") for s in range(slots)]
        self.high_done = [m.sem(f"{name}_high_done{s}") for s in range(slots)]
        self.rest_done = [m.sem(f"{name}_rest_done{s}") for s in range(slots)]
        self.used = [m.sem(f"{name}_used{s}") for s in range(slots)]

    def load(self, engine, s, use, source, first=False):
        if not first:
            engine.wait_ge(self.rest_done[s], use)
        engine.dma_start(self.raw[s], source).then_inc(self.raw_in[s], 16)

    def high(self, act, s, use, first=False):
        act.wait_ge(self.raw_in[s], (use + 1) * 16)
        if not first:
            act.wait_ge(self.used[s], use)
        self.nc.scalar.activation(self.high_part[:, s], self.raw[s], ACT.Copy).then_inc(self.high_done[s], 1)

    def rest(self, dve, s, use):
        dve.wait_ge(self.high_done[s], use + 1)
        self.nc.vector.tensor_tensor(self.rest_part[:, s], self.raw[s], self.high_part[:, s].bitcast(F32), ALU.subtract) \
            .then_inc(self.rest_done[s], 1)

    def arrived(self, pe, s, use):
        pe.wait_ge(self.rest_done[s], use + 1)

    def parts(self, s, *at):
        return self.high_part[(slice(None), s) + at], self.rest_part[(slice(None), s) + at]


class WideProduct:

    def __init__(self, nc, m, mem, name, xT, weight, raw, ps):
        def sb(part, shape):
            return mem.enter_context(nc.sbuf_tensor(f"{name}_{part}", shape, F32R))

        self.nc, self.xT, self.weight, self.raw, self.ps = nc, xT, weight, raw, ps
        self.w = sb("w_high", [P, KT, D]), sb("w_rest", [P, KT, D])
        self.x = sb("x_high", [P, 2, KT, P]), sb("x_rest", [P, 2, KT, P])
        self.raw_in = [m.sem(f"{name}_raw_in{s}") for s in range(2)]
        self.w_high = m.sem(f"{name}_w_high_done")
        self.w_rest = m.sem(f"{name}_w_rest_done")
        self.x_high = m.sem(f"{name}_x_high_done")
        self.x_rest = m.sem(f"{name}_x_rest_done")
        self.done = m.sem(f"{name}_tile_done")

    def load(self, engine):
        for k in range(KT):
            if k >= 2:
                engine.wait_ge(self.w_rest, k - 1)
            engine.dma_start(self.raw[k % 2], self.weight[k * P:(k + 1) * P, :]).then_inc(self.raw_in[k % 2], 16)

    def weight_high(self, act, k):
        act.wait_ge(self.raw_in[k % 2], 16 * (k // 2 + 1))
        self.nc.scalar.activation(self.w[0][:, k, :], self.raw[k % 2], ACT.Copy).then_inc(self.w_high, 1)

    def weight_rest(self, dve, k):
        dve.wait_ge(self.w_high, k + 1)
        self.nc.vector.tensor_tensor(self.w[1][:, k, :], self.raw[k % 2], self.w[0][:, k, :].bitcast(F32),
                                     ALU.subtract).then_inc(self.w_rest, 1)

    def tile_high(self, act, t):
        if t >= 2:
            act.wait_ge(self.done, t - 1)
        self.nc.scalar.activation(self.x[0][:, t % 2, :, :], self.xT[:, :, t * P:(t + 1) * P], ACT.Copy) \
            .then_inc(self.x_high, 1)

    def tile_rest(self, dve, t):
        dve.wait_ge(self.x_high, t + 1)
        self.nc.vector.tensor_tensor(self.x[1][:, t % 2, :, :], self.xT[:, :, t * P:(t + 1) * P],
                                     self.x[0][:, t % 2, :, :].bitcast(F32), ALU.subtract).then_inc(self.x_rest, 1)

    def tile_product(self, pe, t, free, count):
        pe.wait_ge(self.x_rest, t + 1)
        if t >= 4:
            pe.wait_ge(free, count)
        for k in range(KT):
            if t == 0:
                pe.wait_ge(self.w_rest, k + 1)
            for half in range(2):
                cols = slice(half * BANK, (half + 1) * BANK)
                last = product(self.nc, self.ps[:, t % 4, half, :], (self.x[0][:, t % 2, k, :], self.x[1][:, t % 2, k, :]),
                               (self.w[0][:, k, cols], self.w[1][:, k, cols]), start=(k == 0), stop=(k == KT - 1))
        last.then_inc(self.done, 1)


def filter_spectrum(nc, m, A):
    with ExitStack() as mem:
        def sb(name, shape, dt=F32):
            return mem.enter_context(nc.sbuf_tensor(name, shape, dt))

        sem = m.sem
        assert 2 * F_ORDER == P
        pos = sb("pos", [P, BANK])
        f_w_in = sb("f_w_in", [P, F_ORDER])
        f_w_mid = sb("f_w_mid", [P, 2, F_ORDER])
        f_w_out = sb("f_w_out", [P, 2 * D_HYENA])
        arg = sb("arg", [P, BANK])
        turns = sb("turns", [P, BANK])
        hid = sb("hid", [P, 2, BANK])
        decay = sb("decay", [P, 2 * JT, D_HYENA])
        lag_sum = sb("lag_sum", [P, 2, JT, D_HYENA])
        lag_dif = sb("lag_dif", [P, 2, JT, D_HYENA])
        taps = sb("taps", [P, 2, 2, D_HYENA])
        sizes = sb("sizes", [P, 2, 2, D_HYENA])
        size = sb("size", [P, D_HYENA])
        table = sb("filter_table", [P, 4, HALF])
        even_part = sb("even_part", [P, JT, BANK])
        ps = mem.enter_context(nc.psum_tensor("filter_ps", [P, 8, BANK], F32))

        w_in = sem("filter_weights_in")
        out_in = sem("filter_out_weights_in")
        decay_in = sem("decay_in")
        tab_in = [sem(f"filter_table_in{i}") for i in range(4)]
        tab_used = sem("filter_table_used")
        mlp_mm = sem("mlp_mm")
        mlp_arg = sem("mlp_arg")
        mlp_act = sem("mlp_act")
        taps_mm = sem("taps_mm")
        taps_read = sem("taps_read")
        taps_set = sem("taps_set")
        lags_done = sem("lags_done")
        abs_done = sem("abs_done")
        size_step = sem("size_step")
        norm_mm = sem("norm_mm")
        norm_done = sem("norm_done")
        even_kept = sem("even_kept")
        spec_done = sem("spec_done")
        steps = Steps(sem("filter_steps"))
        block = mem.enter_context(nc.Block())

        @block.sync
        def _(sp):
            for n in range(2):
                at = n * F_ORDER
                sp.dma_start(pos[at:at + F_EMB, :], A["positions"][:, n * BANK:(n + 1) * BANK]).then_inc(w_in, 16)
                sp.dma_start(f_w_in[at:at + F_EMB, :], A["f_w_in"][0]).then_inc(w_in, 16)
                sp.dma_start(f_w_mid[at:at + F_ORDER], A["f_w_mid"][0].rearrange("l k n -> k l n")).then_inc(w_in, 16)
            sp.dma_start(m.params[:], A["params"]).then_inc(w_in, 16)
            for n in range(2):
                sp.dma_start(f_w_out[n * F_ORDER:(n + 1) * F_ORDER, :], A["f_w_out"][0]).then_inc(out_in, 16)
            sp.dma_start(decay[:], A["decay"].rearrange("(n p) c -> p n c", p=P)).then_inc(decay_in, 16)
            for n in range(4 * JT):
                if n >= 4:
                    sp.wait_ge(tab_used, n - 3)
                sp.dma_start(table[:, n % 4, :], A["half_tables"][n // JT, (n % JT) * P:(n % JT + 1) * P, :]) \
                    .then_inc(tab_in[n % 4], 16)
                if n == 3:
                    for t in range(TT):
                        sp.dma_start(m.res[:, t, :], A["x"][0, t * P:(t + 1) * P, :]).then_inc(m.x_in, 16)

        @block.gpsimd
        def _(pool):
            nc.gpsimd.memset(m.ident[:], 0.0).then_inc(m.consts_set, 1)
            nc.gpsimd.memset(m.ones[:], 1.0).then_inc(m.consts_set, 1)
            pool.wait_ge(m.consts_set, 2)
            nc.gpsimd.affine_select(out=m.ident[:], in_=m.ident[:], compare_op=ALU.not_equal, fill=1.0, base=0,
                                    pattern=[[-1, P]], channel_multiplier=1).then_inc(m.consts_set, 1)
            nc.gpsimd.memset(size[:], 0.0).then_inc(size_step, 1)
            for n in range(2 * JT):
                pool.wait_ge(abs_done, n + 1)
                for way in range(2):
                    pool.wait_ge(size_step, 2 * n + way + 1)
                    nc.gpsimd.tensor_tensor(size[:], size[:], sizes[:, n % 2, way, :], ALU.add).then_inc(size_step, 1)

        @block.tensor
        def _(pe):
            pe.wait_ge(w_in, 7 * 16)
            for layer in range(3):
                if layer:
                    pe.wait_ge(mlp_act, layer)
                for n in range(2):
                    at = n * F_ORDER
                    if layer == 0:
                        w, data = f_w_in[at:at + F_EMB, :], pos[at:at + F_EMB, :]
                    else:
                        w, data = f_w_mid[at:at + F_ORDER, layer - 1, :], hid[at:at + F_ORDER, (layer - 1) % 2, :]
                    last = nc.tensor.matmul(ps[at:at + F_ORDER, 0, :], w, data, start=True, stop=True)
                last.then_inc(mlp_mm, 1)
            pe.wait_ge(mlp_act, 3)
            pe.wait_ge(out_in, 32)
            for n in range(2 * JT):
                par, a = n // JT, n % JT
                if n >= 2:
                    pe.wait_ge(taps_read, n - 1)
                half, within = a // (JT // 2), a % (JT // 2)
                rows = slice(half * F_ORDER, (half + 1) * F_ORDER)
                for way in range(2):
                    last = nc.tensor.matmul(ps[:, 2 + 2 * (n % 2) + way, :],
                                            hid[rows, 0, 2 * P * within + par:2 * P * (within + 1):2],
                                            f_w_out[rows, way * BANK:(way + 1) * BANK], start=True, stop=True)
                last.then_inc(taps_mm, 1)
            pe.wait_ge(lags_done, 2 * JT)
            for g in range(4):
                if g == 1:
                    pe.wait_ge(size_step, 2 * 2 * JT + 1)
                    pe.wait_ge(m.consts_set, 3)
                    for c in range(HT):
                        last = nc.tensor.matmul(ps[:, 6, c:c + 1], size[:, c * P:(c + 1) * P], m.ones[:, 0:1],
                                                start=True, stop=True)
                    last.then_inc(norm_mm, 1)
                    pe.wait_ge(norm_done, 1)
                if g >= 2:
                    pe.wait_ge(spec_done if g % 2 else even_kept, 1)
                data = lag_sum if g < 2 else lag_dif
                for a in range(JT):
                    n = g * JT + a
                    pe.wait_ge(tab_in[n % 4], 16 * (n // 4 + 1))
                    for f in range(JT):
                        last = nc.tensor.matmul(ps[:, 4 * (g % 2) + f, :], table[:, n % 4, f * P:(f + 1) * P],
                                                data[:, g % 2, a, :], start=(a == 0), stop=(a == JT - 1))
                    last.then_inc(tab_used, 1)

        @block.scalar
        def _(act):
            for layer in range(3):
                act.wait_ge(mlp_arg, layer + 1)
                nc.scalar.activation(hid[:, layer % 2, :], arg[:], ACT.Sin).then_inc(mlp_act, 1)
            for n in range(2 * JT):
                act.wait_ge(taps_set, n + 1)
                if n >= 2:
                    act.wait_ge(size_step, 2 * (n - 1) + 1)
                nc.scalar.activation(sizes[:, n % 2, :, :], taps[:, n % 2, :, :], ACT.Abs).then_inc(abs_done, 1)
            for g in (0, 2):
                act.wait_ge(tab_used, (g + 1) * JT)
                if g:
                    act.wait_ge(spec_done, 1)
                nc.scalar.activation(even_part[:], ps[:, 0:4, :], ACT.Copy).then_inc(even_kept, 1)

        @block.vector
        def _(dve):
            nc.vector.memset(m.eps[:], EPS).then_inc(m.eps_set, 1)
            for layer in range(3):
                dve.wait_ge(mlp_mm, layer + 1)
                if layer == 0:
                    dve.wait_ge(w_in, 7 * 16)
                else:
                    dve.wait_ge(mlp_act, layer)
                steps.end(nc.vector.tensor_scalar(arg[:], ps[:, 0, :], col(m.params, "f_b", layer),
                                                  col(m.params, "f_freq", layer), ALU.add, ALU.mult))
                steps.wait(dve)
                steps.end(nc.vector.tensor_scalar(turns[:], arg[:], 1.0 / TWO_PI, ROUND, ALU.mult, ALU.add))
                steps.wait(dve)
                steps.end(nc.vector.tensor_scalar(turns[:], turns[:], -ROUND, None, ALU.add))
                for part in (TWO_PI_HIGH, TWO_PI_LOW):
                    steps.wait(dve)
                    steps.end(nc.vector.scalar_tensor_tensor(out=arg[:], in0=turns[:], scalar=-part, in1=arg[:],
                                                             op0=ALU.mult, op1=ALU.add))
                steps.wait(dve)
                nc.vector.tensor_scalar(arg[:], arg[:], PI_BELOW, -PI_BELOW, ALU.min, ALU.max).then_inc(mlp_arg, 1)
            dve.wait_ge(decay_in, 16)
            for n in range(2 * JT):
                par, a = n // JT, n % JT
                dve.wait_ge(taps_mm, n + 1)
                if n >= 2:
                    dve.wait_ge(abs_done, n - 1)
                for way in range(2):
                    last = nc.vector.tensor_tensor(taps[:, n % 2, way, :], ps[:, 2 + 2 * (n % 2) + way, :],
                                                   decay[:, n, :], ALU.mult)
                last.then_inc(taps_read, 1)
                dve.wait_ge(taps_read, n + 1)
                if n == 0:
                    steps.end(nc.vector.memset(taps[0:1, 0, 1, :], 0.0))
                    steps.wait(dve)
                nc.vector.tensor_tensor(lag_sum[:, par, a, :], taps[:, n % 2, 0, :], taps[:, n % 2, 1, :], ALU.add).then_inc(taps_set, 1)
                nc.vector.tensor_tensor(lag_dif[:, par, a, :], taps[:, n % 2, 0, :], taps[:, n % 2, 1, :],
                                        ALU.subtract).then_inc(lags_done, 1)
            dve.wait_ge(norm_mm, 1)
            nc.vector.reciprocal(m.inv_size[:], ps[:, 6, 0:HT]).then_inc(norm_done, 1)
            for trig in range(2):
                dve.wait_ge(even_kept, trig + 1)
                dve.wait_ge(tab_used, (2 * trig + 2) * JT)
                nc.vector.tensor_tensor(m.K[:, trig, 0, :, :], even_part[:], ps[:, 4:8, :], ALU.add)
                nc.vector.tensor_tensor(m.K[:, trig, 1, :, :], even_part[:], ps[:, 4:8, :], ALU.subtract) \
                    .then_inc(spec_done, 1)


def norm_to_T(nc, m, name, hT, gamma=None, gamma_row=None, rows_out=None, x_ready=None, res_out=None,
              loads_before=None, loads_after=None, tile_use=None,
              scratch=None, next_ring=None):
    split = gamma is not None
    with ExitStack() as mem:
        def sb(part, shape, dt=F32):
            return mem.enter_context(nc.sbuf_tensor(f"{name}_{part}", shape, dt))

        def sem(part):
            return m.sem(f"{name}_{part}")

        sums = sb("sums", [P, TT])
        rms = sb("rms", [P, TT])
        rstd = sb("rstd", [P, TT])
        if scratch is None:
            scaled, squares = sb("scaled", [P, 2, D]), sb("squares", [P, D])
        else:
            scaled, squares = scratch[:, 0:2, :], scratch[:, 2, :]
        ps = mem.enter_context(nc.psum_tensor(f"{name}_ps", [P, 2, KT, P], F32))
        summed = sem("summed")
        rms_done = sem("rms_done")
        rstd_done = sem("rstd_done")
        scaled_done = sem("scaled_done")
        turned = sem("turned")
        out_done = sem("out_done")
        if split:
            full = scratch[:, 3:5, :].rearrange("p s (k c) -> p s k c", k=KT)
            full_done = sem("full_done")
            high_done = sem("high_done")
        else:
            g_row = sb("gamma_row", [P, D])
            g_in = sem("gamma_in")
            stored = [sem(f"stored{i}") for i in range(2)]
        kept = sem("res_kept")
        tile_groups = {TT - 3: range(TT // 2), TT - 1: range(TT // 2, TT)}
        block = mem.enter_context(nc.Block())

        @block.scalar
        def _(act):
            def leave(t):
                if split:
                    act.wait_ge(full_done, t + 1)
                    nc.scalar.activation(hT[0][:, :, t * P:(t + 1) * P], full[:, t % 2, :, :], ACT.Copy) \
                        .then_inc(high_done, 1)
                else:
                    act.wait_ge(turned, t + 1)
                    nc.scalar.activation(hT[:, :, t * P:(t + 1) * P], ps[:, t % 2, :, :], ACT.Copy) \
                        .then_inc(out_done, 1)

            act.wait_ge(m.eps_set, 1)
            if x_ready is not None:
                act.wait_ge(x_ready, 16 * TT)
            for t in range(TT):
                if t:
                    act.wait_ge(summed, t)
                nc.scalar.activation(squares[:, 0:D], m.res[:, t, :], ACT.Square, accum_out=sums[:, t:t + 1]) \
                    .then_inc(summed, 1)
                act.wait_ge(summed, t + 1)
                nc.scalar.activation(rms[:, t:t + 1], sums[:, t:t + 1], ACT.Sqrt, bias=m.eps[:], scale=1.0 / D) \
                    .then_inc(rms_done, 1)
                if t >= 2:
                    leave(t - 2)
            leave(TT - 2)
            if next_ring is not None:
                for s in range(len(next_ring[1])):
                    next_ring[0].high(act, s, 0, first=True)
            leave(TT - 1)

        @block.gpsimd
        def _(pool):
            if split:
                for t in range(TT):
                    pool.wait_ge(high_done, t + 1)
                    here = slice(t * P, (t + 1) * P)
                    nc.gpsimd.tensor_tensor(hT[1][:, :, here], full[:, t % 2, :, :], hT[0][:, :, here].bitcast(F32),
                                            ALU.subtract).then_inc(out_done, 1)

        @block.vector
        def _(dve):
            def turn_out(t):
                dve.wait_ge(turned, t + 1)
                if t >= 2:
                    dve.wait_ge(out_done, t - 1)
                at, _ = COLS[gamma]
                scale = m.params[:, at:at + KT].unsqueeze(2).to_broadcast([P, KT, P])
                nc.vector.tensor_tensor(full[:, t % 2, :, :], ps[:, t % 2, :, :], scale, ALU.mult).then_inc(full_done, 1)

            for t in range(TT):
                dve.wait_ge(rms_done, t + 1)
                nc.vector.reciprocal(rstd[:, t:t + 1], rms[:, t:t + 1]).then_inc(rstd_done, 1)
                dve.wait_ge(rstd_done, t + 1)
                if split:
                    if t >= 2:
                        dve.wait_ge(turned, t - 1)
                    nc.vector.tensor_scalar(scaled[:, t % 2, :], m.res[:, t, :], rstd[:, t:t + 1], None, ALU.mult) \
                        .then_inc(scaled_done, 1)
                    if t >= 1:
                        turn_out(t - 1)
                else:
                    if t == 0:
                        dve.wait_ge(g_in, 16)
                    if t >= 2:
                        dve.wait_ge(turned, t - 1)
                        dve.wait_ge(stored[t % 2], 16 * (t // 2))
                    nc.vector.scalar_tensor_tensor(out=scaled[:, t % 2, :], in0=m.res[:, t, :],
                                                   scalar=rstd[:, t:t + 1], in1=g_row[:], op0=ALU.mult,
                                                   op1=ALU.mult).then_inc(scaled_done, 1)
            if split:
                turn_out(TT - 1)
                if next_ring is not None:
                    for s in range(len(next_ring[1])):
                        next_ring[0].rest(dve, s, 0)

        @block.tensor
        def _(pe):
            for t in range(TT):
                pe.wait_ge(scaled_done, t + 1)
                if t >= 2:
                    pe.wait_ge(full_done if split else out_done, t - 1)
                for k in range(KT):
                    last = nc.tensor.transpose(ps[:, t % 2, k, :], scaled[:, t % 2, k * P:(k + 1) * P], m.ident[:])
                last.then_inc(turned, 1)
                if tile_use is not None and t in tile_groups:
                    for done in tile_groups[t]:
                        pe.wait_ge(out_done, done + 1)
                        tile_use(pe, done)

        @block.sync
        def _(sp):
            if not split:
                sp.dma_start(g_row[:], gamma_row.to_broadcast([P, D])).then_inc(g_in, 16)
            if loads_before is not None:
                loads_before(sp)
            if res_out is not None:
                sp.dma_start(res_out.rearrange("(t p) d -> p t d", p=P), m.res[:]).then_inc(kept, 16)
                sp.wait_ge(kept, 16)
            if next_ring is not None:
                ring, sources = next_ring
                for s, source in enumerate(sources):
                    sp.wait_ge(scaled_done, s + 1)
                    ring.load(sp, s, 0, source, first=True)
                if loads_after is not None:
                    loads_after(sp)
            if not split:
                for t in range(TT):
                    sp.wait_ge(scaled_done, t + 1)
                    sp.dma_start(rows_out[t * P:(t + 1) * P, :], scaled[:, t % 2, :]).then_inc(stored[t % 2], 16)
                if loads_after is not None:
                    loads_after(sp)
                for s in range(2):
                    sp.wait_ge(stored[s], 16 * TT // 2)


def first_ring(nc, m, mem, A):
    ring = SplitRing(nc, m, mem, "proj_w", 2, [KT, P], [m.res[:, s, :].rearrange("p (k c) -> p k c", k=KT) for s in range(2)])
    weights = A["w_in"][0].rearrange("(k p) n -> p k n", p=P)
    return ring, [weights[:, :, s * P:(s + 1) * P] for s in range(2)]


def project_first(nc, m, A, hT, ring):
    with ExitStack() as mem:
        sem = m.sem
        S = 2
        COUNT = 4 * HT
        conv = m.res[:, S:S + 2, :]
        zero = m.res[0:CAP, S + 2, :]
        ps = mem.enter_context(nc.psum_tensor("proj_ps", [P, 4, 2, BANK], F32))
        zero_set = sem("zero_set")
        rows_blank = sem("rows_blank")
        centre = sem("proj_centre")
        proj_out = sem("proj_out")
        steps = Steps(sem("proj_steps"))
        block = mem.enter_context(nc.Block())

        def tile_target(c):
            return (m.mixT[:, c % HT, :], m.zT[:, c % HT, :], conv[:, c % 2, :])[c // HT]

        @block.sync
        def _(sp):
            weights = A["w_in"][0].rearrange("(k p) n -> p k n", p=P)
            with sp.Fori(1, COUNT // S) as r:
                for s in range(S):
                    ring.load(sp, s, r, weights[:, :, bass.ds((r * S + s) * P, P)])

        @block.gpsimd
        def _(pool):
            nc.gpsimd.memset(zero, 0.0).then_inc(zero_set, 1)
            pool.wait_ge(zero_set, 1)
            for b in range(EXPERTS, BLOCKS):
                pool.dma_start(m.y_dram[b * CAP:(b + 1) * CAP, :], zero).then_inc(rows_blank, 16)
            pool.wait_ge(rows_blank, 16 * OVER)

        @block.tensor
        def _(pe):
            def channel_tile(s, q, use, free):
                ring.arrived(pe, s, use)
                if free is not None:
                    pe.wait_ge(proj_out, free)
                for half in range(2):
                    cols = slice(half * BANK, (half + 1) * BANK)
                    for k in range(KT):
                        last = product(nc, ps[:, q, half, :], ring.parts(s, k), (hT[0][:, k, cols], hT[1][:, k, cols]),
                                       start=(k == 0), stop=(k == KT - 1))
                last.then_inc(ring.used[s], 1)

            for q in range(4):
                channel_tile(q % S, q, q // S, None)
            with pe.Fori(1, COUNT // 4) as r:
                for q in range(4):
                    channel_tile(q % S, q, r * 2 + q // S, (r - 1) * 4 + q + 1)

        @block.scalar
        def _(act):
            for c in range(COUNT):
                act.wait_ge(ring.used[c % S], c // S + 1)
                if c + S < COUNT:
                    ring.high(act, c % S, c // S + 1)
                if c < 3 * HT:
                    if c >= 2 * HT + 2:
                        act.wait_ge(proj_out, c - 1)
                    nc.scalar.activation(tile_target(c).rearrange("p (h c) -> p h c", h=2), ps[:, c % 4, :, :],
                                         ACT.Identity, bias=col(m.params, "conv_b", c),
                                         scale=col(m.params, "conv_w", 3 * HT + c)).then_inc(centre, 1)

        @block.vector
        def _(dve):
            for c in range(COUNT):
                if c + S < COUNT:
                    ring.rest(dve, c % S, c // S + 1)
                dve.wait_ge(ring.used[c % S], c // S + 1)
                raw = ps[:, c % 4, :, :].rearrange("p h c -> p (h c)")
                if c >= 3 * HT:
                    nc.vector.tensor_copy(m.mixT[:, c - 2 * HT, :], raw).then_inc(proj_out, 1)
                    continue
                into = tile_target(c)
                dve.wait_ge(centre, c + 1)
                steps.end(nc.vector.scalar_tensor_tensor(out=into[:, 1:SEQ], in0=raw[:, 0:SEQ - 1],
                                                         scalar=col(m.params, "conv_w", c), in1=into[:, 1:SEQ],
                                                         op0=ALU.mult, op1=ALU.add))
                steps.wait(dve)
                last = nc.vector.scalar_tensor_tensor(out=into[:, 0:SEQ - 1], in0=raw[:, 1:SEQ],
                                                      scalar=col(m.params, "conv_w", 2 * 3 * HT + c),
                                                      in1=into[:, 0:SEQ - 1], op0=ALU.mult, op1=ALU.add)
                if c >= 2 * HT:
                    steps.end(last)
                    steps.wait(dve)
                    last = nc.vector.tensor_tensor(m.zT[:, c % HT, :], m.zT[:, c % HT, :], conv[:, c % 2, :], ALU.mult)
                last.then_inc(proj_out, 1)


def transform_mixes(nc, m, A):
    with ExitStack() as mem:
        def sb(name, shape, dt=F32):
            return mem.enter_context(nc.sbuf_tensor(name, shape, dt))

        sem = m.sem
        SLOTS = 4
        pair = sb("pair", [P, 2 * P])
        znat = sb("znat", [P, 2 * JT, D_HYENA])
        U = sb("U", [P, 2, 2, JT, BANK])
        even_part = sb("u_even_part", [P, JT, BANK])
        chan = sb("chan", [P, JT, HT, 2 * P])
        table = sb("mix_table", [P, SLOTS, HALF])
        ps = mem.enter_context(nc.psum_tensor("mix_ps", [P, 8, BANK], F32))

        pair_in = sem("pair_in")
        tab_in = [sem(f"mix_table_in{i}") for i in range(SLOTS)]
        tab_used = sem("mix_table_used")
        z_turned = sem("z_turned")
        z_kept = sem("z_kept")
        even_kept = sem("u_even_kept")
        u_done = sem("u_done")
        chan_mm = sem("chan_mm")
        chan_kept = sem("chan_kept")
        g_done = sem("g_done")
        four_even = sem("four_even")
        four_done = sem("four_done")
        bias_done = sem("bias_done")
        steps = Steps(sem("mix_steps"))
        FWD, DFT, BACK = 0, 4 * JT, 8 * JT
        N_TILES = 12 * JT
        block = mem.enter_context(nc.Block())

        def table_tile(n):
            if n < DFT:
                return A["half_tables"][n // JT, (n % JT) * P:(n % JT + 1) * P, :]
            if n < BACK:
                par, a, trig = (n - DFT) // (2 * JT), (n - DFT) // 2 % JT, n % 2
                return A["dft_tables"][2 * par + trig, a * P:(a + 1) * P, :]
            par, trig, f = (n - BACK) // (2 * JT), (n - BACK) // JT % 2, n % JT
            return A["back_tables"][par, trig, f * P:(f + 1) * P, :]

        @block.sync
        def _(sp):
            sp.dma_start(pair[:], A["pair_table"].rearrange("p t c -> p (t c)")).then_inc(pair_in, 16)
            for n in range(N_TILES):
                if n >= SLOTS:
                    sp.wait_ge(tab_used, n - SLOTS + 1)
                if SLOTS <= n < SLOTS + TT:
                    t = n - SLOTS
                    sp.dma_start(m.res[:, t, :], A["x"][0, t * P:(t + 1) * P, :]).then_inc(m.x_in, 16)
                sp.dma_start(table[:, n % SLOTS, :], table_tile(n)).then_inc(tab_in[n % SLOTS], 16)

        @block.tensor
        def _(pe):
            def arrived(n):
                pe.wait_ge(tab_in[n % SLOTS], 16 * (n // SLOTS + 1))

            def channel_transform(par):
                for a in range(JT):
                    n = par * JT + a
                    if a >= 2:
                        pe.wait_ge(chan_kept, n - 1)
                    for c in range(HT):
                        last = nc.tensor.matmul(ps[:, 4 * par + 2 * (a % 2) + c // 2, (c % 2) * 2 * P:(c % 2 + 1) * 2 * P],
                                                m.mixT[:, HT + c, 2 * P * a + par:2 * P * (a + 1):2], pair[:],
                                                start=True, stop=True)
                    last.then_inc(chan_mm, 1)

            for n in range(2 * JT):
                par, a = n // JT, n % JT
                if n >= 4:
                    pe.wait_ge(z_kept, n - 3)
                for c in range(HT):
                    last = nc.tensor.transpose(ps[:, n % 4, c * P:(c + 1) * P],
                                               m.zT[:, c, 2 * P * a + par:2 * P * (a + 1):2], m.ident[:])
                last.then_inc(z_turned, 1)
            for g in range(4):
                if g < 2:
                    pe.wait_ge(z_kept, 2 * JT)
                else:
                    pe.wait_ge(u_done if g % 2 else even_kept, 1)
                for a in range(JT):
                    n = FWD + g * JT + a
                    arrived(n)
                    for f in range(JT):
                        last = nc.tensor.matmul(ps[:, 4 * (g % 2) + f, :], table[:, n % SLOTS, f * P:(f + 1) * P],
                                                znat[:, (g % 2) * JT + a, :], start=(a == 0), stop=(a == JT - 1))
                    last.then_inc(tab_used, 1)
            pe.wait_ge(pair_in, 16)
            for par in range(2):
                pe.wait_ge(u_done if par else even_kept, 2)
                channel_transform(par)
                pe.wait_ge(chan_kept, (par + 1) * JT)
                for a in range(JT):
                    for trig in range(2):
                        n = DFT + (par * JT + a) * 2 + trig
                        arrived(n)
                        for c in range(HT):
                            last = nc.tensor.matmul(ps[:, 4 * par + c, :], chan[:, a, c, trig * P:(trig + 1) * P],
                                                    table[:, n % SLOTS, :], start=(a == 0 and trig == 0),
                                                    stop=(a == JT - 1 and trig == 1))
                        last.then_inc(tab_used, 1)
            for par in range(2):
                pe.wait_ge(four_done if par else four_even, 1)
                for k in range(2 * JT):
                    trig, f = k // JT, k % JT
                    if par == 0 and trig == 0:
                        pe.wait_ge(g_done, f + 1)
                    n = BACK + par * 2 * JT + k
                    arrived(n)
                    for c in range(HT):
                        last = nc.tensor.matmul(ps[:, 4 * par + c, :], U[:, trig, par, f, c * P:(c + 1) * P],
                                                table[:, n % SLOTS, :], start=(k == 0), stop=(k == 2 * JT - 1))
                    last.then_inc(tab_used, 1)

        @block.scalar
        def _(act):
            for n in range(2 * JT):
                act.wait_ge(z_turned, n + 1)
                nc.scalar.activation(znat[:, n, :], ps[:, n % 4, :], ACT.Copy).then_inc(z_kept, 1)
            for trig in range(2):
                act.wait_ge(tab_used, FWD + (2 * trig + 1) * JT)
                if trig:
                    act.wait_ge(u_done, 1)
                nc.scalar.activation(even_part[:], ps[:, 0:4, :], ACT.Copy).then_inc(even_kept, 1)
            for par in range(2):
                for a in range(JT):
                    n = par * JT + a
                    act.wait_ge(chan_mm, n + 1)
                    if par:
                        act.wait_ge(tab_used, DFT + 2 * (a + 1))
                    b = 4 * par + 2 * (a % 2)
                    nc.scalar.activation(chan[:, a, :, :].rearrange("p (b c) n -> p b (c n)", b=2), ps[:, b:b + 2, :],
                                         ACT.Copy).then_inc(chan_kept, 1)
                if par == 0:
                    act.wait_ge(tab_used, DFT + 2 * JT)
                    act.wait_ge(u_done, 2)
                    nc.scalar.activation(even_part[:], ps[:, 0:4, :], ACT.Copy).then_inc(four_even, 1)

        @block.gpsimd
        def _(pool):
            pool.wait_ge(z_turned, 2 * JT)
            for c in range(HT):
                nc.gpsimd.tensor_scalar(m.zT[:, c, :], m.zT[:, c, :], col(m.params, "f_bias", c), None, ALU.mult) \
                    .then_inc(bias_done, 1)

        @block.vector
        def _(dve):
            for trig in range(2):
                dve.wait_ge(even_kept, trig + 1)
                dve.wait_ge(tab_used, FWD + (2 * trig + 2) * JT)
                nc.vector.tensor_tensor(U[:, trig, 0, :, :], even_part[:], ps[:, 4:8, :], ALU.add)
                nc.vector.tensor_tensor(U[:, trig, 1, :, :], even_part[:], ps[:, 4:8, :], ALU.subtract) \
                    .then_inc(u_done, 1)
            dve.wait_ge(u_done, 2)
            for f in range(JT):
                if f:
                    dve.wait_ge(g_done, f)
                for pm in range(2):
                    for i, (a, b) in enumerate(((0, 0), (1, 1), (0, 1), (1, 0))):
                        last = nc.vector.tensor_tensor(znat[:, 4 * pm + i, :], U[:, a, pm, f, :], m.K[:, b, pm, f, :],
                                                       ALU.mult)
                steps.end(last)
                steps.wait(dve)
                for pm in range(2):
                    for i, op in ((0, ALU.subtract), (2, ALU.add)):
                        last = nc.vector.tensor_tensor(znat[:, 4 * pm + i, :], znat[:, 4 * pm + i, :],
                                                       znat[:, 4 * pm + i + 1, :], op)
                steps.end(last)
                steps.wait(dve)
                for trig in range(2):
                    for par, op in ((0, ALU.add), (1, ALU.subtract)):
                        last = nc.vector.tensor_tensor(U[:, trig, par, f, :], znat[:, 2 * trig, :],
                                                       znat[:, 4 + 2 * trig, :], op)
                last.then_inc(g_done, 1)
            dve.wait_ge(four_even, 1)
            dve.wait_ge(tab_used, DFT + 4 * JT)
            nc.vector.tensor_tensor(m.mixT[:, HT:2 * HT, 0:HALF], even_part[:], ps[:, 4:8, :], ALU.add)
            nc.vector.tensor_tensor(m.mixT[:, HT:2 * HT, HALF:SEQ], even_part[:], ps[:, 4:8, :], ALU.subtract) \
                .then_inc(four_done, 1)
            dve.wait_ge(bias_done, HT)
            for par in range(2):
                dve.wait_ge(tab_used, BACK + (par + 1) * 2 * JT)
                for c in range(HT):
                    steps.end(nc.vector.scalar_tensor_tensor(
                        out=m.zT[:, c, par:SEQ:2], in0=ps[:, 4 * par + c, :], scalar=m.inv_size[:, c:c + 1],
                        in1=m.zT[:, c, par:SEQ:2], op0=ALU.mult, op1=ALU.add))
                    steps.wait(dve)
                    nc.vector.tensor_tensor(m.mixT[:, c, par:SEQ:2], m.mixT[:, c, par:SEQ:2], m.zT[:, c, par:SEQ:2],
                                            ALU.mult)


def head_norm_project(nc, m, A):
    with ExitStack() as mem:
        def sb(name, shape, dt=F32):
            return mem.enter_context(nc.sbuf_tensor(name, shape, dt))

        sem = m.sem
        NH = D // HEAD
        pick = sb("head_pick", [P, KT, NH])
        spread = sb("head_spread", [NH, KT, P])
        spread_r = sb("head_spread_r", [NH, KT, P], F32R)
        scratch = m.K[:].rearrange("p a b f c -> p (a b f c)").rearrange("p (n c) -> p n c", c=SEQ)
        sq = scratch[:, 2:4, :]
        rstd = scratch[0:NH, 4, :]
        rstd_high = sb("head_rstd_high", [NH, SEQ], F32R)
        rstd_rest = sb("head_rstd_rest", [NH, SEQ], F32R)
        ps = mem.enter_context(nc.psum_tensor("w_out_ps", [P, 4, 2, BANK], F32))
        wide = WideProduct(nc, m, mem, "w_out", m.mixT, A["w_out"][0], [scratch[:, i, :] for i in range(2)], ps)
        tables_in = sem("head_tables_in")
        spread_done = sem("head_spread_done")
        even_squared = sem("head_even_squared")
        odd_squared = sem("head_odd_squared")
        mean_mm = sem("head_mean_mm")
        rms_done = sem("head_rms_done")
        rstd_done = sem("head_rstd_done")
        rstd_split = sem("head_rstd_split")
        spread_mm = sem("head_spread_mm")
        normed = sem("head_normed")
        added = sem("w_out_added")
        block = mem.enter_context(nc.Block())

        @block.sync
        def _(sp):
            sp.dma_start(pick[:], A["head_pick"]).then_inc(tables_in, 16)
            sp.dma_start(spread[:], A["head_spread"]).then_inc(tables_in, 16)
            wide.load(sp)

        @block.gpsimd
        def _(pool):
            for c in range(0, KT, 2):
                if c >= 2:
                    pool.wait_ge(mean_mm, c - 1)
                nc.gpsimd.tensor_tensor(sq[:, 0, :], m.mixT[:, c, :], m.mixT[:, c, :], ALU.mult) \
                    .then_inc(even_squared, 1)

        @block.tensor
        def _(pe):
            pe.wait_ge(tables_in, 32)
            for c in range(KT):
                pe.wait_ge(odd_squared if c % 2 else even_squared, c // 2 + 1)
                for half in range(2):
                    last = nc.tensor.matmul(ps[0:NH, 0, half, :], pick[:, c, :],
                                            sq[:, c % 2, half * BANK:(half + 1) * BANK],
                                            start=(c == 0), stop=(c == KT - 1))
                last.then_inc(mean_mm, 1)
            pe.wait_ge(spread_done, 1)
            pe.wait_ge(rstd_split, 1)
            for c in range(KT):
                if c >= 4:
                    pe.wait_ge(normed, c - 3)
                for half in range(2):
                    cols = slice(half * BANK, (half + 1) * BANK)
                    nc.tensor.matmul(ps[:, c % 4, half, :], spread_r[:, c, :], rstd_high[:, cols], start=True, stop=False)
                    last = nc.tensor.matmul(ps[:, c % 4, half, :], spread_r[:, c, :], rstd_rest[:, cols],
                                            start=False, stop=True)
                last.then_inc(spread_mm, 1)
            pe.wait_ge(normed, KT)
            for t in range(TT):
                wide.tile_product(pe, t, added, t - 3)

        @block.scalar
        def _(act):
            for c in range(1, KT, 2):
                if c >= 2:
                    act.wait_ge(mean_mm, c - 1)
                nc.scalar.activation(sq[:, 1, :], m.mixT[:, c, :], ACT.Square).then_inc(odd_squared, 1)
                for k in range(c - 1, c + 1):
                    wide.weight_high(act, k)
            act.wait_ge(tables_in, 32)
            nc.scalar.activation(spread_r[:], spread[:], ACT.Copy).then_inc(spread_done, 1)
            act.wait_ge(mean_mm, KT)
            nc.scalar.activation(rstd.rearrange("p (h c) -> p h c", h=2), ps[0:NH, 0, :, :], ACT.Sqrt,
                                 bias=m.eps[0:NH, :]).then_inc(rms_done, 1)
            act.wait_ge(rstd_done, 1)
            nc.scalar.activation(rstd_high[:], rstd, ACT.Copy).then_inc(rstd_done, 1)
            act.wait_ge(normed, KT)
            for t in range(TT):
                wide.tile_high(act, t)

        @block.vector
        def _(dve):
            for k in range(KT):
                wide.weight_rest(dve, k)
            dve.wait_ge(rms_done, 1)
            nc.vector.reciprocal(rstd, rstd).then_inc(rstd_done, 1)
            dve.wait_ge(rstd_done, 2)
            nc.vector.tensor_tensor(rstd_rest[:], rstd, rstd_high[:].bitcast(F32), ALU.subtract).then_inc(rstd_split, 1)
            for c in range(KT):
                dve.wait_ge(spread_mm, c + 1)
                here = m.mixT[:, c, :].rearrange("p (h c) -> p h c", h=2)
                nc.vector.scalar_tensor_tensor(out=here, in0=here, scalar=col(m.params, "mix_g", c),
                                               in1=ps[:, c % 4, :, :], op0=ALU.mult, op1=ALU.mult).then_inc(normed, 1)
            dve.wait_ge(m.x_in, 32 * TT)
            for t in range(2):
                wide.tile_rest(dve, t)
            for t in range(TT):
                dve.wait_ge(wide.done, t + 1)
                if t + 2 < TT:
                    wide.tile_rest(dve, t + 2)
                nc.vector.tensor_tensor(m.res[:, t, :].rearrange("p (h c) -> p h c", h=2),
                                        m.res[:, t, :].rearrange("p (h c) -> p h c", h=2),
                                        ps[:, t % 4, :, :], ALU.add).then_inc(added, 1)


def first_mixer(nc, m, A):
    with nc.sbuf_tensor("K", [P, 2, 2, JT, BANK], F32) as m.K:
        filter_spectrum(nc, m, A)
        with nc.sbuf_tensor("mixT", [P, KT, SEQ], F32) as m.mixT:
            with nc.sbuf_tensor("zT", [P, HT, SEQ], F32) as m.zT:
                with nc.sbuf_tensor("hT1_high", [P, KT, SEQ], F32R) as high, \
                        nc.sbuf_tensor("hT1_rest", [P, KT, SEQ], F32R) as rest, ExitStack() as mem:
                    ring, sources = first_ring(nc, m, mem, A)
                    norm_to_T(nc, m, "norm1", (high, rest), gamma="norm1_g", x_ready=m.x_in,
                              scratch=m.mixT[:, 0:5, :], next_ring=(ring, sources))
                    project_first(nc, m, A, (high, rest), ring)
                transform_mixes(nc, m, A)
            head_norm_project(nc, m, A)


class Router:

    def __init__(self, nc, m, mem):
        def sb(name, shape, dt=F32):
            return mem.enter_context(nc.sbuf_tensor(name, shape, dt))

        self.w = sb("router_w", [P, KT, NL])
        self.b = sb("router_b", [P, NL])
        self.before = sb("before", [P, P])
        self.idx = sb("index_row", [P, 2, EXPERTS])
        self.limits = sb("limits", [P, FULL_BLOCKS - 1])
        self.count = sb("count_row", [P, CAP])
        self.tokens = sb("token_ids", [P, TT])
        self.loaded = m.sem("router_in")
        self.logit_mm = m.sem("logit_mm")
        self.ps = mem.enter_context(nc.psum_tensor("route_ps", [P, 2, BANK], F32))

    def load(self, sp, A):
        sp.dma_start(self.w[:], A["w_router"].rearrange("(k p) n -> p k n", p=P)).then_inc(self.loaded, 16)
        sp.dma_start(self.b[:], A["b_router"].to_broadcast([P, NL])).then_inc(self.loaded, 16)
        sp.dma_start(self.before[:], A["before"]).then_inc(self.loaded, 16)
        sp.dma_start(self.idx[:], A["index_rows"].to_broadcast([P, 2, EXPERTS])).then_inc(self.loaded, 16)
        sp.dma_start(self.limits[:], A["limits"].to_broadcast([P, FULL_BLOCKS - 1])).then_inc(self.loaded, 16)
        sp.dma_start(self.count[:], A["count_row"].to_broadcast([P, CAP])).then_inc(self.loaded, 16)
        sp.dma_start(self.tokens[:], A["token_ids"]).then_inc(self.loaded, 16)

    def logits(self, nc, pe, hT, t):
        if t == 0:
            pe.wait_ge(self.loaded, 112)
        for k in range(KT):
            last = nc.tensor.matmul(self.ps[:, 0, t * NL:(t + 1) * NL], hT[:, k, t * P:(t + 1) * P], self.w[:, k, :],
                                    start=(k == 0), stop=(k == KT - 1))
        last.then_inc(self.logit_mm, 1)


class ExpertWeights:

    def __init__(self, m):
        self.gate, self.up, self.down = [], [], []
        self.gate_in = [m.sem(f"w_gate_in{s}") for s in range(WSLOTS)]
        self.up_in = [m.sem(f"w_up_in{s}") for s in range(WSLOTS)]
        self.down_in = [m.sem(f"w_down_in{s}") for s in range(WSLOTS)]

    def add_place(self, nc, mem):
        s = len(self.gate)
        self.gate.append(mem.enter_context(nc.sbuf_tensor(f"w_gate_sb{s}", [P, KT, D_EXPERT], F32)))
        self.up.append(mem.enter_context(nc.sbuf_tensor(f"w_up_sb{s}", [P, KT, D_EXPERT], F32)))
        self.down.append(mem.enter_context(nc.sbuf_tensor(f"w_down_sb{s}", [P, D_EXPERT // P, D], F32)))

    def load(self, engine, A, s, e, used=None):
        for i, (w, name, arrived) in enumerate(((self.gate, "w_gate", self.gate_in), (self.up, "w_up", self.up_in),
                                                (self.down, "w_down", self.down_in))):
            if used is not None:
                engine.wait_ge(*used[i])
            engine.dma_start(w[s][:], A[name][0, bass.ds(e, 1)].rearrange("o (k p) n -> p (o k) n", p=P)) \
                .then_inc(arrived[s], 16)


def route(nc, m, A, router, weights):
    with ExitStack() as mem:
        def sb(name, shape, dt=F32):
            return mem.enter_context(nc.sbuf_tensor(name, shape, dt))

        sem = m.sem
        b, before, idx, limits, ps = router.b, router.before, router.idx, router.limits, router.ps
        logits = sb("logits", [P, TT, NL])
        gmax = sb("gmax", [P, TT])
        gdiff = sb("gdiff", [P, TT, GROUPS])
        gexp = sb("gexp", [P, TT, GROUPS])
        gmask = sb("gmask", [P, TT, GROUPS])
        pg = sb("pg", [P, TT])
        part = sb("part", [P, TT, PER_GROUP])
        sel = sb("sel", [P, TT, PER_GROUP])
        cand = sb("cand", [P, TT, PER_GROUP])
        first = sb("first", [P, TT])
        hot = sb("hot", [P, 2, TT, PER_GROUP])
        top = sb("top", [P, 2, TT])
        diff = sb("diff", [P, TT])
        ratio = sb("ratio", [P, TT])
        M = sb("M", [P, 2, TT, EXPERTS])
        both = sb("both", [P, TT, EXPERTS])
        earlier = sb("earlier", [P, TT + 1, EXPERTS])
        rank = sb("rank", [P, TT + 1, EXPERTS])
        n_over = sb("n_over", [P, EXPERTS])
        incl = sb("incl", [P, EXPERTS])
        excl = sb("excl", [P, EXPERTS])
        prod = sb("prod", [P, TT, EXPERTS])
        r_of = sb("r_of", [P, 2, TT])
        e_of = sb("e_of", [P, 2, TT])
        s_of = sb("s_of", [P, 2, TT])
        steps_in = sb("steps_in", [P, 2, TT, FULL_BLOCKS - 1])
        full = sb("full", [P, 2, TT])
        blk = sb("blk", [P, 2, TT])
        at_row = sb("at_row", [P, 2, TT, CAP])
        over = at_row[:].rearrange("p s t c -> p (s t c)")[:, 0:EXPERTS * (FULL_BLOCKS - 1)] \
            .rearrange("p (e n) -> p e n", e=EXPERTS)
        in_block = sb("in_block", [P, 2, TT, BLOCKS])
        ends = sb("ends", [1, OVER, EXPERTS])
        over_f = sb("over_f", [1, OVER + 1])

        gdiff_done = sem("gdiff_done")
        gexp_done = sem("gexp_done")
        diff_done = sem("diff_done")
        ratio_done = sem("ratio_done")
        pairs_done = sem("pairs_done")
        rank_mm = sem("rank_mm")
        places_done = sem("places_done")
        list_mm = sem("row_list_mm")
        steps = Steps(sem("route_steps"))
        block = mem.enter_context(nc.Block())

        @block.sync
        def _(sp):
            weights.load(sp, A, WSLOTS - 1, WSLOTS - 1)

        @block.tensor
        def _(pe):
            pe.wait_ge(pairs_done, 1)
            nc.tensor.matmul(ps[:, 1, 0:(TT + 1) * EXPERTS], m.ones[:], earlier[:].rearrange("p t e -> p (t e)"),
                             start=True, stop=False)
            last = nc.tensor.matmul(ps[:, 1, 0:TT * EXPERTS], before[:], both[:].rearrange("p t e -> p (t e)"),
                                    start=False, stop=True)
            last.then_inc(rank_mm, 1)
            pe.wait_ge(places_done, 1)
            for slot in range(2):
                for t in range(TT):
                    last = nc.tensor.matmul(ps[0:CAP, 0, 0:BLOCKS], at_row[:, slot, t, :], in_block[:, slot, t, :],
                                            start=(slot == 0 and t == 0), stop=(slot == 1 and t == TT - 1))
            last.then_inc(list_mm, 1)

        @block.scalar
        def _(act):
            act.wait_ge(gdiff_done, 1)
            nc.scalar.activation(gexp[:], gdiff[:], ACT.Exp).then_inc(gexp_done, 1)
            act.wait_ge(diff_done, 1)
            nc.scalar.activation(ratio[:], diff[:], ACT.Exp).then_inc(ratio_done, 1)

        @block.vector
        def _(dve):
            def step(instruction):
                steps.end(instruction)
                steps.wait(dve)

            def wide(a, n):
                return a.unsqueeze(2).to_broadcast([P, TT, n])

            def over_tiles(a, n):
                return a.unsqueeze(1).to_broadcast([P, TT, n])

            def first_of(mask_out, values, largest, n):
                c = cand[:, :, 0:n]
                step(nc.vector.tensor_tensor(c, values, wide(largest, n), ALU.is_equal))
                step(nc.vector.tensor_tensor(c, c, over_tiles(idx[:, 0, 0:n], n), ALU.mult))
                step(nc.vector.tensor_reduce(first[:], c, AX_X, ALU.min))
                step(nc.vector.tensor_tensor(mask_out, over_tiles(idx[:, 0, 0:n], n), wide(first[:], n), ALU.is_equal))

            dve.wait_ge(router.loaded, 112)
            dve.wait_ge(router.logit_mm, TT)
            step(nc.vector.tensor_tensor(logits[:], ps[:, 0, 0:TT * NL].rearrange("p (t n) -> p t n", t=TT),
                                         over_tiles(b[:], NL), ALU.add))
            group = logits[:, :, 0:GROUPS]
            step(nc.vector.tensor_reduce(gmax[:], group, AX_X, ALU.max))
            nc.vector.tensor_tensor(gdiff[:], group, wide(gmax[:], GROUPS), ALU.subtract).then_inc(gdiff_done, 1)
            first_of(gmask[:], group, gmax[:], GROUPS)
            dve.wait_ge(gexp_done, 1)
            step(nc.vector.tensor_reduce(pg[:], gexp[:], AX_X, ALU.add))
            step(nc.vector.reciprocal(pg[:], pg[:]))
            for g in range(GROUPS):
                of_g = logits[:, :, GROUPS + g * PER_GROUP:GROUPS + (g + 1) * PER_GROUP]
                mask = gmask[:, :, g:g + 1].to_broadcast([P, TT, PER_GROUP])
                if g == 0:
                    step(nc.vector.tensor_tensor(sel[:], of_g, mask, ALU.mult))
                else:
                    step(nc.vector.tensor_tensor(part[:], of_g, mask, ALU.mult))
                    step(nc.vector.tensor_tensor(sel[:], sel[:], part[:], ALU.add))
            for slot in range(2):
                step(nc.vector.tensor_reduce(top[:, slot, :], sel[:], AX_X, ALU.max))
                first_of(hot[:, slot], sel[:], top[:, slot, :], PER_GROUP)
                if slot == 0:
                    step(nc.vector.scalar_tensor_tensor(out=sel[:], in0=hot[:, 0], scalar=NEG, in1=sel[:],
                                                        op0=ALU.mult, op1=ALU.add))
            nc.vector.tensor_tensor(diff[:], top[:, 1, :], top[:, 0, :], ALU.subtract).then_inc(diff_done, 1)
            for slot in range(2):
                for g in range(GROUPS):
                    last = nc.vector.tensor_tensor(M[:, slot, :, g * PER_GROUP:(g + 1) * PER_GROUP], hot[:, slot],
                                                   gmask[:, :, g:g + 1].to_broadcast([P, TT, PER_GROUP]), ALU.mult)
            step(last)
            step(nc.vector.tensor_tensor(both[:], M[:, 0], M[:, 1], ALU.add))
            step(nc.vector.memset(earlier[:, 0, :], 0.0))
            for t in range(TT):
                last = nc.vector.tensor_tensor(earlier[:, t + 1, :], earlier[:, t, :], both[:, t, :], ALU.add)
                if t < TT - 1:
                    step(last)
            last.then_inc(pairs_done, 1)
            dve.wait_ge(ratio_done, 1)
            step(nc.vector.tensor_scalar(diff[:], ratio[:], 1.0, None, ALU.add))
            step(nc.vector.reciprocal(diff[:], diff[:]))
            step(nc.vector.tensor_tensor(m.pair_w[:, 0, :], diff[:], pg[:], ALU.mult))
            step(nc.vector.tensor_tensor(m.pair_w[:, 1, :], m.pair_w[:, 0, :], ratio[:], ALU.mult))
            dve.wait_ge(rank_mm, 1)
            step(nc.vector.tensor_copy(rank[:], ps[:, 1, 0:(TT + 1) * EXPERTS].rearrange("p (t e) -> p t e", t=TT + 1)))
            n_lim = FULL_BLOCKS - 1
            step(nc.vector.tensor_tensor(over, rank[:, TT, :].unsqueeze(2).to_broadcast([P, EXPERTS, n_lim]),
                                         limits[:].unsqueeze(1).to_broadcast([P, EXPERTS, n_lim]), ALU.is_gt))
            step(nc.vector.tensor_reduce(n_over[:], over, AX_X, ALU.add))
            step(nc.vector.tensor_tensor_scan(incl[:], m.ones[:, 0:EXPERTS], n_over[:], 0.0, ALU.mult, ALU.add))
            step(nc.vector.tensor_tensor(excl[:], incl[:], n_over[:], ALU.subtract))
            for slot in range(2):
                for out, table in ((r_of, rank[:, 0:TT, :]), (e_of, over_tiles(idx[:, 1, :], EXPERTS)),
                                   (s_of, over_tiles(excl[:], EXPERTS))):
                    step(nc.vector.tensor_tensor(prod[:], M[:, slot], table, ALU.mult))
                    step(nc.vector.tensor_reduce(out[:, slot, :], prod[:], AX_X, ALU.add))
            for slot in range(2):
                step(nc.vector.tensor_tensor(steps_in[:, slot], wide(r_of[:, slot, :], n_lim), over_tiles(limits[:], n_lim),
                                             ALU.is_ge))
                step(nc.vector.tensor_reduce(full[:, slot, :], steps_in[:, slot], AX_X, ALU.add))
            step(nc.vector.tensor_tensor(blk[:], s_of[:], full[:], ALU.add))
            step(nc.vector.tensor_tensor(blk[:], blk[:], e_of[:], ALU.subtract))
            step(nc.vector.tensor_scalar(blk[:], blk[:], float(EXPERTS - 1), None, ALU.add))
            step(nc.vector.scalar_tensor_tensor(out=blk[:], in0=full[:], scalar=1.0, in1=blk[:], op0=ALU.min,
                                                op1=ALU.mult))
            step(nc.vector.tensor_tensor(blk[:], blk[:], e_of[:], ALU.add))
            step(nc.vector.scalar_tensor_tensor(out=r_of[:], in0=full[:], scalar=-float(CAP), in1=r_of[:],
                                                op0=ALU.mult, op1=ALU.add))
            pairs = [P, 2 * TT]
            nc.vector.tensor_tensor(at_row[:].rearrange("p s t c -> p (s t) c"),
                                    r_of[:].rearrange("p s t -> p (s t)").unsqueeze(2).to_broadcast(pairs + [CAP]),
                                    router.count[:].unsqueeze(1).to_broadcast(pairs + [CAP]), ALU.is_equal)
            step(nc.vector.tensor_tensor(in_block[:].rearrange("p s t c -> p (s t) c"),
                                         blk[:].rearrange("p s t -> p (s t)").unsqueeze(2).to_broadcast(pairs + [BLOCKS]),
                                         router.count[:, 0:BLOCKS].unsqueeze(1).to_broadcast(pairs + [BLOCKS]),
                                         ALU.is_equal))
            for slot in range(2):
                last = nc.vector.tensor_tensor(in_block[:, slot], in_block[:, slot], wide(router.tokens[:], BLOCKS),
                                               ALU.mult)
            last.then_inc(places_done, 1)
            step(nc.vector.scalar_tensor_tensor(out=blk[:], in0=blk[:], scalar=float(CAP), in1=r_of[:],
                                                op0=ALU.mult, op1=ALU.add))
            step(nc.vector.tensor_copy(m.pair_row[:], blk[:]))
            step(nc.vector.tensor_tensor(ends[:], incl[0:1, :].unsqueeze(1).to_broadcast([1, OVER, EXPERTS]),
                                         idx[0:1, 1, 0:OVER].unsqueeze(2).to_broadcast([1, OVER, EXPERTS]), ALU.is_le))
            step(nc.vector.tensor_reduce(over_f[:, 0:OVER], ends[:], AX_X, ALU.add))
            step(nc.vector.tensor_scalar(over_f[:, 0:OVER], over_f[:, 0:OVER], float(EXPERTS - 1), None, ALU.min))
            step(nc.vector.tensor_copy(over_f[:, OVER:OVER + 1], incl[0:1, EXPERTS - 1:EXPERTS]))
            nc.vector.tensor_copy(m.over_table[:], over_f[:])
            dve.wait_ge(list_mm, 1)
            nc.vector.tensor_copy(m.row_ids[:], ps[0:CAP, 0, 0:BLOCKS])


def experts(nc, m, A, weights):
    with ExitStack() as mem:
        def sb(name, shape, dt=F32):
            return mem.enter_context(nc.sbuf_tensor(name, shape, dt))

        sem = m.sem
        S = WSLOTS
        FE = D_EXPERT // P
        idx = sb("block_ids", [CAP, S], I32)
        rows = sb("rows", [CAP, S, D])
        xT = sb("xT", [P, KT, CAP])
        act_out = sb("gate_act", [P, FE, CAP])
        hidT = sb("hidT", [P, FE, CAP])
        y = sb("y_rows", [CAP, D])
        ps_x = mem.enter_context(nc.psum_tensor("x_ps", [P, KT, P], F32))
        ps_h = mem.enter_context(nc.psum_tensor("h_ps", [P, 2, FE, P], F32))
        ps_y = mem.enter_context(nc.psum_tensor("y_ps", [P, 2, BANK], F32))

        idx_set = [sem(f"block_ids_set{s}") for s in range(S)]
        rows_in = [sem(f"rows_in{s}") for s in range(S)]
        turned = sem("rows_turned")
        xT_done = sem("xT_done")
        gate_mm = sem("gate_mm")
        up_mm = sem("up_mm")
        act_done = sem("gate_act_done")
        hid_done = sem("hid_done")
        down_mm = sem("down_mm")
        y_left = sem("y_left")
        y_right = sem("y_right")
        y_out = sem("y_stored")
        block = mem.enter_context(nc.Block())
        waited_sp = sem("waited_sp")
        waited_pool = sem("waited_pool")
        ROUNDS, REST = EXPERTS // S, EXPERTS % S
        LAST = EXPERTS - 1
        OVER_SLOT = REST

        def over_blocks(engine, body):
            count = engine.value_load(m.over_table[0:1, OVER:OVER + 1], min_val=0, max_val=OVER)
            with engine.If(count > 0):
                with engine.Fori(0, OVER) as j:
                    with engine.If(j < count):
                        body(j)
            return count

        @block.sync
        def _(sp):
            def reload(s, e, read):
                weights.load(sp, A, s, e, used=((gate_mm, read), (up_mm, read), (down_mm, read)))

            def store(b):
                sp.wait_ge(y_left, b + 1)
                sp.wait_ge(y_right, b + 1)
                sp.dma_start(m.y_dram[bass.ds(b * CAP, CAP), :], y[:]).then_inc(y_out, 16)

            with sp.Fori(0, ROUNDS - 1) as i:
                for s in range(S):
                    reload(s, i * S + (S + s), i * S + (s + 1))
                    store(i * S + s)
            for b in range(EXPERTS - S - REST, EXPERTS):
                if b + S < EXPERTS:
                    reload(b % S, b + S, b + 1)
                store(b)

            def over(j):
                e = sp.value_load(m.over_table[0:1, bass.ds(j, 1)], min_val=0, max_val=EXPERTS - 1)
                reload(OVER_SLOT, e, j + EXPERTS)
                store(j + EXPERTS)

            count = over_blocks(sp, over)
            sp.wait_ge(y_out, (count + EXPERTS) * 16)
            sp.sem_inc(waited_sp, 1)

        @block.gpsimd
        def _(pool):
            def gather(s, b, use, read=None):
                if read is not None:
                    pool.wait_ge(turned, read)
                nc.gpsimd.tensor_copy(idx[:, s:s + 1], m.row_ids[:, bass.ds(b, 1)]).then_inc(idx_set[s], 1)
                pool.wait_ge(idx_set[s], use + 1)
                pool.sem_inc(waited_pool, 1)
                pool.indirect_dma_start(rows[:, s, :], None, m.hn_dram,
                                        bass.IndirectOffsetOnAxis(ap=idx[:, s:s + 1], axis=0)).then_inc(rows_in[s], 16)

            for s in range(S):
                gather(s, s, 0)
            with pool.Fori(1, ROUNDS) as i:
                for s in range(S):
                    gather(s, i * S + s, i, read=(i - 1) * S + (s + 1))
            for s in range(REST):
                gather(s, ROUNDS * S + s, ROUNDS, read=(ROUNDS - 1) * S + s + 1)
            over_blocks(pool, lambda j: gather(OVER_SLOT, j + EXPERTS, j + ROUNDS, read=j + EXPERTS))

        @block.tensor
        def _(pe):
            def turn(s, use):
                pe.wait_ge(rows_in[s], (use + 1) * 16)
                for k in range(KT):
                    last = nc.tensor.transpose(ps_x[:, k, 0:CAP], rows[:, s, k * P:(k + 1) * P], m.ident[0:CAP, 0:CAP])
                last.then_inc(turned, 1)

            def gate_up(s, use, b):
                pe.wait_ge(xT_done, b + 1)
                for i, (w, arrived, done) in enumerate(((weights.gate, weights.gate_in, gate_mm),
                                                        (weights.up, weights.up_in, up_mm))):
                    pe.wait_ge(arrived[s], (use + 1) * 16)
                    for f in range(FE):
                        for k in range(KT):
                            last = nc.tensor.matmul(ps_h[:, i, f, 0:CAP], w[s][:, k, f * P:(f + 1) * P],
                                                    xT[:, k, :], start=(k == 0), stop=(k == KT - 1))
                    last.then_inc(done, 1)

            def down(s, use, b, first=False):
                pe.wait_ge(hid_done, b + 1)
                pe.wait_ge(weights.down_in[s], (use + 1) * 16)
                if not first:
                    pe.wait_ge(y_left, b)
                    pe.wait_ge(y_right, b)
                for half in range(2):
                    for f in range(FE):
                        last = nc.tensor.matmul(ps_y[0:CAP, half, :], hidT[:, f, :],
                                                weights.down[s][:, f, half * BANK:(half + 1) * BANK],
                                                start=(f == 0), stop=(f == FE - 1))
                last.then_inc(down_mm, 1)

            def blocks(b, i, first):
                for n in range(S):
                    s, use = (first + n) % S, i + (first + n) // S
                    gate_up(s, use, b + n)
                    turn((s + 1) % S, i + (first + n + 1) // S)
                    down(s, use, b + n)

            turn(0, 0)
            gate_up(0, 0, 0)
            turn(1, 0)
            down(0, 0, 0, first=True)
            with pe.Fori(0, (EXPERTS - 2) // S) as i:
                blocks(i * S + 1, i, 1)
            gate_up(LAST % S, LAST // S, LAST)
            down(LAST % S, LAST // S, LAST)

            def over(j):
                turn(OVER_SLOT, j + ROUNDS)
                gate_up(OVER_SLOT, j + ROUNDS, j + EXPERTS)
                down(OVER_SLOT, j + ROUNDS, j + EXPERTS)

            over_blocks(pe, over)

        @block.scalar
        def _(act):
            def gate(b, first=False):
                act.wait_ge(gate_mm, b + 1)
                if not first:
                    act.wait_ge(hid_done, b)
                nc.scalar.activation(act_out[:], ps_h[:, 0, :, 0:CAP], ACT.Silu).then_inc(act_done, 1)

            def left(b, first=False):
                act.wait_ge(down_mm, b + 1)
                if not first:
                    act.wait_ge(y_out, b * 16)
                nc.scalar.activation(y[:, 0:BANK], ps_y[0:CAP, 0, :], ACT.Copy).then_inc(y_left, 1)

            gate(0, first=True)
            left(0, first=True)
            with act.Fori(1, EXPERTS) as b:
                gate(b)
                left(b)

            def over(j):
                gate(j + EXPERTS)
                left(j + EXPERTS)

            over_blocks(act, over)

        @block.vector
        def _(dve):
            def x_out(b, first=False):
                dve.wait_ge(turned, b + 1)
                if not first:
                    dve.wait_ge(up_mm, b)
                nc.vector.tensor_copy(xT[:], ps_x[:, :, 0:CAP]).then_inc(xT_done, 1)

            def hidden(b, first=False):
                dve.wait_ge(up_mm, b + 1)
                dve.wait_ge(act_done, b + 1)
                if not first:
                    dve.wait_ge(down_mm, b)
                nc.vector.tensor_tensor(hidT[:], act_out[:], ps_h[:, 1, :, 0:CAP], ALU.mult).then_inc(hid_done, 1)

            def right(b, first=False):
                dve.wait_ge(down_mm, b + 1)
                if not first:
                    dve.wait_ge(y_out, b * 16)
                nc.vector.tensor_copy(y[:, BANK:D], ps_y[0:CAP, 1, :]).then_inc(y_right, 1)

            x_out(0, first=True)
            hidden(0, first=True)
            x_out(1)
            right(0, first=True)
            with dve.Fori(1, LAST) as b:
                hidden(b)
                x_out(b + 1)
                right(b)
            hidden(LAST)
            right(LAST)

            def over(j):
                x_out(j + EXPERTS)
                hidden(j + EXPERTS)
                right(j + EXPERTS)

            over_blocks(dve, over)


def combine(nc, m, A):
    with ExitStack() as mem:
        def sb(name, shape, dt=F32):
            return mem.enter_context(nc.sbuf_tensor(name, shape, dt))

        sem = m.sem
        BUF = 6
        y = sb("y_pairs", [P, BUF, 2, D])
        g_row = sb("final_gamma", [P, D])
        squares = sb("final_squares", [P, D])
        sums = sb("final_sums", [P, TT])
        rms = sb("final_rms", [P, TT])
        rstd = sb("final_rstd", [P, TT])
        y_in = [sem(f"y_in{i}") for i in range(BUF)]
        g_in = sem("final_gamma_in")
        summed = sem("combined")
        squared = sem("final_squared")
        rms_done = sem("final_rms_done")
        steps = Steps(sem("combine_steps"))
        block = mem.enter_context(nc.Block())

        @block.sync
        def _(sp):
            sp.dma_start(g_row[:], A["final_g"].to_broadcast([P, D])).then_inc(g_in, 16)

        @block.gpsimd
        def _(pool):
            for t in range(TT):
                if t >= BUF:
                    pool.wait_ge(summed, t - BUF + 1)
                for slot in range(2):
                    pool.indirect_dma_start(y[:, t % BUF, slot, :], None, m.y_dram,
                                            bass.IndirectOffsetOnAxis(ap=m.pair_row[:, slot, t:t + 1], axis=0)) \
                        .then_inc(y_in[t % BUF], 16)

        @block.scalar
        def _(act):
            for t in range(TT):
                act.wait_ge(summed, t + 1)
                if t:
                    act.wait_ge(squared, t)
                nc.scalar.activation(squares[:], m.res[:, t, :], ACT.Square, accum_out=sums[:, t:t + 1]) \
                    .then_inc(squared, 1)
                act.wait_ge(squared, t + 1)
                nc.scalar.activation(rms[:, t:t + 1], sums[:, t:t + 1], ACT.Sqrt, bias=m.eps[:], scale=1.0 / D) \
                    .then_inc(rms_done, 1)

        @block.vector
        def _(dve):
            def normalise(t):
                dve.wait_ge(rms_done, t + 1)
                steps.end(nc.vector.reciprocal(rstd[:, t:t + 1], rms[:, t:t + 1]))
                steps.wait(dve)
                nc.vector.scalar_tensor_tensor(out=m.res[:, t, :], in0=m.res[:, t, :], scalar=rstd[:, t:t + 1],
                                               in1=g_row[:], op0=ALU.mult, op1=ALU.mult)

            dve.wait_ge(g_in, 16)
            for t in range(TT):
                dve.wait_ge(y_in[t % BUF], 32 * (t // BUF + 1))
                for slot in range(2):
                    last = nc.vector.scalar_tensor_tensor(out=m.res[:, t, :], in0=y[:, t % BUF, slot, :],
                                                          scalar=m.pair_w[:, slot, t:t + 1], in1=m.res[:, t, :],
                                                          op0=ALU.mult, op1=ALU.add)
                    if slot == 0:
                        steps.end(last)
                        steps.wait(dve)
                last.then_inc(summed, 1)
                if t:
                    normalise(t - 1)
            normalise(TT - 1)


def mixture(nc, m, A):
    with ExitStack() as mem:
        m.pair_w = mem.enter_context(nc.sbuf_tensor("pair_w", [P, 2, TT], F32))
        m.pair_row = mem.enter_context(nc.sbuf_tensor("pair_row", [P, 2, TT], I32))
        m.over_table = mem.enter_context(nc.sbuf_tensor("over_table", [1, OVER + 1], I32))
        m.row_ids = mem.enter_context(nc.sbuf_tensor("row_ids", [CAP, BLOCKS], I32))
        m.hn_dram = nc.dram_tensor("normed_rows", (SEQ, D), F32).ap()
        with ExitStack() as places:
            router = Router(nc, m, places)
            weights = ExpertWeights(m)
            for s in range(WSLOTS - 1):
                weights.add_place(nc, places)

            def first_experts(sp):
                for s in range(WSLOTS - 1):
                    weights.load(sp, A, s, s)

            with nc.sbuf_tensor("hT2", [P, KT, SEQ], F32) as hT:
                norm_to_T(nc, m, "norm2", hT, gamma_row=A["norm2_g"], rows_out=m.hn_dram,
                          loads_before=lambda sp: router.load(sp, A), loads_after=first_experts,
                          tile_use=lambda pe, t: router.logits(nc, pe, hT, t))
            weights.add_place(nc, places)
            route(nc, m, A, router, weights)
            experts(nc, m, A, weights)
        combine(nc, m, A)


def qkvu_ring(nc, m, mem):
    return SplitRing(nc, m, mem, "qkvu_w", 2, [KT, P], [m.res[:, s, :].rearrange("p (k c) -> p k c", k=KT) for s in range(2)])


def project_second(nc, m, A, hT, ring):
    with ExitStack() as mem:
        sem = m.sem
        S = 2
        PAD = max(WINDOWS)
        LONG = PAD + SEQ
        place = m.res[:].rearrange("p t d -> p (t d)")
        u = place[:, 2 * D:2 * D + 2 * LONG].rearrange("p (n c) -> p n c", n=2)
        sums = place[:, 5 * D:5 * D + 2 * LONG].rearrange("p (n c) -> p n c", n=2)
        w_g = mem.enter_context(nc.sbuf_tensor("pool_group_w", [P, HT, P], F32))
        edge = mem.enter_context(nc.sbuf_tensor("pool_edge", [P, len(WINDOWS), PAD], F32))
        pooled = m.attT
        ps = mem.enter_context(nc.psum_tensor("qkvu_ps", [P, 4, 2, BANK], F32))
        small_in = sem("pool_small_in")
        job_mm = sem("qkvu_job_mm")
        job_out = sem("qkvu_job_out")
        padded = sem("pool_padded")
        window = sem("pool_window")
        pooled_done = sem("pooled_done")
        block = mem.enter_context(nc.Block())
        jobs = [("u", 0), ("u", 1), ("q", 0), ("u", 2), ("g", 0), ("q", 1), ("u", 3), ("g", 1), ("q", 2), ("q", 3),
                ("g", 2), ("k", 0), ("k", 1), ("g", 3), ("k", 2), ("k", 3)]
        J = {job: j for j, job in enumerate(jobs)}
        first_col = {"q": 0, "k": ATT, "u": 3 * ATT}
        tiles = [job for job in jobs if job[0] != "g"]
        ring_n = {job: n for n, job in enumerate(tiles)}
        NW = len(tiles) + KT // 2

        def ring_source(n):
            if n < len(tiles):
                kind, c = tiles[n]
                at = first_col[kind] + c * P
                return A["w_in_2"][0].rearrange("(k p) n -> p k n", p=P)[:, :, at:at + P]
            k = 2 * (n - len(tiles))
            return A["w_in_2"][0, k * P:(k + 2) * P, 2 * ATT:3 * ATT].rearrange("(k p) (b c) -> p k b c", p=P, c=P)

        @block.sync
        def _(sp):
            sp.dma_start(edge[:], A["pool_edge"]).then_inc(small_in, 16)
            sp.dma_start(w_g[:], A["w_pool_group_2"][0].rearrange("g c d -> c g d")).then_inc(small_in, 16)
            for n in range(S, NW):
                s, use = n % S, n // S
                sp.wait_ge(ring.rest_done[s], use)
                if n < len(tiles):
                    sp.dma_start(ring.raw[s], ring_source(n)).then_inc(ring.raw_in[s], 16)
                else:
                    sp.dma_start(ring.raw[s].rearrange("p (k b) c -> p k b c", k=2), ring_source(n)) \
                        .then_inc(ring.raw_in[s], 16)

        @block.tensor
        def _(pe):
            for j, (kind, c) in enumerate(jobs):
                if j >= 4:
                    pe.wait_ge(job_out, j - 3)
                if kind == "g":
                    if c == 0:
                        pe.wait_ge(small_in, 32)
                    pe.wait_ge(pooled_done, c + 1)
                    for half in range(2):
                        last = nc.tensor.matmul(ps[:, j % 4, half, :], w_g[:, c, :],
                                                pooled[:, c, half * BANK:(half + 1) * BANK], start=True, stop=True)
                    last.then_inc(job_mm, 1)
                    continue
                n = ring_n[kind, c]
                ring.arrived(pe, n % S, n // S)
                for half in range(2):
                    cols = slice(half * BANK, (half + 1) * BANK)
                    for k in range(KT):
                        last = product(nc, ps[:, j % 4, half, :], ring.parts(n % S, k),
                                       (hT[0][:, k, cols], hT[1][:, k, cols]), start=(k == 0), stop=(k == KT - 1))
                last.then_inc(ring.used[n % S], 1)
            pe.wait_ge(job_out, len(jobs))
            for kk in range(KT // 2):
                n = len(tiles) + kk
                ring.arrived(pe, n % S, n // S)
                for t in range(TT):
                    here = slice(t * P, (t + 1) * P)
                    for i in range(2):
                        k = 2 * kk + i
                        w = [part[:, n % S, 4 * i:4 * i + 4, :].rearrange("p b c -> p (b c)")
                             for part in (ring.high_part, ring.rest_part)]
                        last = product(nc, ps[:, t // 2, t % 2, :], (hT[0][:, k, here], hT[1][:, k, here]), w,
                                       start=(k == 0), stop=(k == KT - 1))
                last.then_inc(ring.used[n % S], 1)

        def job_done(engine, j):
            kind, c = jobs[j]
            if kind == "g":
                engine.wait_ge(job_mm, c + 1)
            else:
                n = ring_n[kind, c]
                engine.wait_ge(ring.used[n % S], n // S + 1)

        @block.scalar
        def _(act):
            split = S
            for j, (kind, c) in enumerate(jobs):
                job_done(act, j)
                if kind != "g" and split < NW:
                    ring.high(act, split % S, split // S)
                    split += 1
                if j:
                    act.wait_ge(job_out, j)
                out = None
                if kind == "u":
                    act.wait_ge(padded, 1)
                    if c >= 2:
                        act.wait_ge(pooled_done, c - 1)
                    out = u[:, c % 2, PAD:]
                elif kind != "g":
                    out = (m.qT if kind == "q" else m.kT)[:, c, :]
                if out is not None:
                    nc.scalar.activation(out.rearrange("p (h c) -> p h c", h=2), ps[:, j % 4, :, :], ACT.Copy,
                                         scale=HEAD ** -0.5 if kind == "q" else 1.0).then_inc(job_out, 1)
            while split < NW:
                ring.high(act, split % S, split // S)
                split += 1
            n = NW - 1
            act.wait_ge(ring.used[n % S], n // S + 1)
            for t in range(TT):
                last = nc.scalar.activation(m.v[:, t, :], ps[:, t // 2, t % 2, :], ACT.Copy)

        @block.gpsimd
        def _(pool):
            done = Steps(window)
            for g in range(HT):
                pool.wait_ge(job_out, J["u", g] + 1)
                if g:
                    pool.wait_ge(pooled_done, g)
                for i in range(g + 1):
                    src = u[:, g % 2, :] if i == 0 else sums[:, (i - 1) % 2, :]
                    done.end(nc.gpsimd.tensor_tensor(sums[:, i % 2, PAD:], src[:, PAD:], src[:, PAD - 2 ** i:LONG - 2 ** i],
                                                     ALU.add))
                    done.wait(pool)
                if g == 0:
                    pool.wait_ge(small_in, 32)
                done.end(nc.gpsimd.tensor_tensor(sums[:, g % 2, PAD:2 * PAD], sums[:, g % 2, PAD:2 * PAD], edge[:, g, :],
                                                 ALU.mult))
                assert done.n == WINDOW_STEPS[g]

        @block.vector
        def _(dve):
            for a in (u, sums):
                last = nc.vector.memset(a[:, :, 0:PAD], 0.0)
            last.then_inc(padded, 1)
            split, pooled_next = S, 0
            for j, (kind, c) in enumerate(jobs):
                if kind != "g":
                    if split < NW:
                        ring.rest(dve, split % S, split // S)
                        split += 1
                    if pooled_next < HT and J["u", pooled_next] < j:
                        g = pooled_next
                        dve.wait_ge(window, WINDOW_STEPS[g])
                        nc.vector.scalar_tensor_tensor(out=pooled[:, g, :], in0=sums[:, g % 2, PAD:],
                                                       scalar=1.0 / WINDOWS[g], in1=u[:, g % 2, PAD:], op0=ALU.mult,
                                                       op1=ALU.subtract).then_inc(pooled_done, 1)
                        pooled_next += 1
                else:
                    job_done(dve, j)
                    dve.wait_ge(job_out, j)
                    nc.vector.tensor_scalar(m.poolT[:, c, :].rearrange("p (h c) -> p h c", h=2), ps[:, j % 4, :, :],
                                            col(m.params, "pool_scale_2", c), None, ALU.mult).then_inc(job_out, 1)
            while split < NW:
                ring.rest(dve, split % S, split // S)
                split += 1


WINDOW_STEPS = [sum(i + 2 for i in range(g + 1)) for g in range(HT)]


def band_attention(nc, m, A):
    with ExitStack() as mem:
        def sb(name, shape, dt=F32):
            return mem.enter_context(nc.sbuf_tensor(name, shape, dt))

        sem = m.sem
        bias = m.res[:].rearrange("p t d -> p (t d)")[:, 0:HEADS * KEYS].rearrange("p (h k) -> p h k", h=HEADS)
        score = sb("score", [P, 3, KEYS])
        prob = sb("prob", [P, 3, KEYS])
        top = sb("top_score", [P, TT * HEADS])
        ntop = sb("neg_top", [P, TT * HEADS])
        total = sb("total", [P, TT, HEADS])
        inv = sb("inv_total", [P, TT, HEADS])
        probT = sb("probT", [P, 2, KEY_TILES, P])
        att = sb("att", [P, 2, ATT])
        ps_s = mem.enter_context(nc.psum_tensor("score_ps", [P, 2, 2 * BANK], F32))
        ps_p = mem.enter_context(nc.psum_tensor("prob_ps", [P, 2 * BANK], F32))
        ps_o = mem.enter_context(nc.psum_tensor("att_ps", [P, BANK], F32))
        ps_t = mem.enter_context(nc.psum_tensor("attT_ps", [P, BANK], F32))
        bias_in = sem("bias_in")
        masked = sem("bias_masked")
        score_mm = sem("score_mm")
        score_out = sem("score_out")
        ntop_done = sem("ntop_done")
        exp_done = sem("exp_done")
        turned = sem("prob_turned")
        probT_done = sem("probT_done")
        pv_mm = sem("pv_mm")
        inv_done = sem("inv_done")
        att_done = sem("att_done")
        att_turned = sem("att_turned")
        attT_done = sem("attT_done")
        block = mem.enter_context(nc.Block())
        ITEMS = [(i, h) for i in reversed(range(TT)) for h in range(HEADS)]
        N = len(ITEMS)

        def key_tiles(i):
            return min(i + 1, KEY_TILES)

        @block.sync
        def _(sp):
            sp.wait_ge(m.bias_copied, 16)
            for h in range(HEADS):
                rows = bass.AP(tensor=m.bias_rows.tensor, offset=h * P * EXT + P - 1, ap=[[EXT - 1, P], [1, KEYS]])
                sp.dma_start(bias[:, h, :], rows).then_inc(bias_in, 16)

        @block.gpsimd
        def _(pool):
            pool.wait_ge(bias_in, 16 * HEADS)
            nc.gpsimd.memset(bias[0:CHUNK, :, BAND:KEYS], NEG).then_inc(masked, 1)
            nc.gpsimd.memset(bias[CHUNK:P, :, 0:CHUNK], NEG).then_inc(masked, 1)

        @block.tensor
        def _(pe):
            def scores(n):
                i, h = ITEMS[n]
                rows = slice(HEAD * (h % 2), HEAD * (h % 2 + 1))
                width = key_tiles(i) * P
                first_key = (i + 1) * P - width
                if n >= 2:
                    pe.wait_ge(score_out, n - 1)
                for at in range(0, width, BANK):
                    n_keys = min(BANK, width - at)
                    last = nc.tensor.matmul(ps_s[:, n % 2, at:at + n_keys], m.qT[rows, h // 2, i * P:(i + 1) * P],
                                            m.kT[rows, h // 2, first_key + at:first_key + at + n_keys],
                                            start=True, stop=True)
                last.then_inc(score_mm, 1)

            def turn(n):
                i, _ = ITEMS[n]
                pe.wait_ge(exp_done, n + 1)
                if n:
                    pe.wait_ge(probT_done, n)
                for j in range(key_tiles(i)):
                    last = nc.tensor.transpose(ps_p[:, j * P:(j + 1) * P], prob[:, n % 3, j * P:(j + 1) * P], m.ident[:])
                last.then_inc(turned, 1)

            def values(n):
                i, h = ITEMS[n]
                nk = key_tiles(i)
                pe.wait_ge(probT_done, n + 1)
                if h == 0 and n:
                    pe.wait_ge(att_done, n // HEADS)
                for j in range(nk):
                    last = nc.tensor.matmul(ps_o[:, h * HEAD:(h + 1) * HEAD], probT[:, n % 2, j, :],
                                            m.v[:, i + 1 - nk + j, h * HEAD:(h + 1) * HEAD],
                                            start=(j == 0), stop=(j == nk - 1))
                last.then_inc(pv_mm, 1)

            def out(turn_no):
                pe.wait_ge(att_done, turn_no + 1)
                if turn_no:
                    pe.wait_ge(attT_done, turn_no)
                for c in range(HT):
                    last = nc.tensor.transpose(ps_t[:, c * P:(c + 1) * P], att[:, turn_no % 2, c * P:(c + 1) * P], m.ident[:])
                last.then_inc(att_turned, 1)

            scores(0)
            scores(1)
            keep_clock(nc, m, ps_p[:, 0:P], 40)
            for n in range(N):
                if n + 2 < N:
                    scores(n + 2)
                turn(n)
                if n:
                    values(n - 1)
                if n % HEADS == 3 and n > HEADS:
                    out(n // HEADS - 1)
            values(N - 1)
            out(TT - 1)

        @block.scalar
        def _(act):
            def leave(n):
                nk = key_tiles(ITEMS[n][0])
                act.wait_ge(turned, n + 1)
                if n >= 2:
                    act.wait_ge(pv_mm, n - 1)
                nc.scalar.activation(probT[:, n % 2, 0:nk, :].rearrange("p j q -> p (j q)"), ps_p[:, 0:nk * P], ACT.Copy) \
                    .then_inc(probT_done, 1)

            for n, (i, h) in enumerate(ITEMS):
                width = key_tiles(i) * P
                act.wait_ge(ntop_done, n + 1)
                if n >= 3:
                    act.wait_ge(turned, n - 2)
                nc.scalar.activation(prob[:, n % 3, 0:width], score[:, n % 3, 0:width], ACT.Exp,
                                     bias=ntop[:, n:n + 1], accum_out=total[:, n // HEADS, h:h + 1]).then_inc(exp_done, 1)
                if n:
                    leave(n - 1)
            leave(N - 1)

        @block.vector
        def _(dve):
            def head_out(turn_no):
                dve.wait_ge(exp_done, (turn_no + 1) * HEADS)
                nc.vector.reciprocal(inv[:, turn_no, :], total[:, turn_no, :]).then_inc(inv_done, 1)
                dve.wait_ge(inv_done, turn_no + 1)
                dve.wait_ge(pv_mm, (turn_no + 1) * HEADS)
                if turn_no >= 2:
                    dve.wait_ge(att_turned, turn_no - 1)
                nc.vector.tensor_tensor(att[:, turn_no % 2, :].rearrange("p (h d) -> p h d", h=HEADS),
                                        ps_o[:].rearrange("p (h d) -> p h d", h=HEADS),
                                        inv[:, turn_no, :].unsqueeze(2).to_broadcast([P, HEADS, HEAD]), ALU.mult) \
                    .then_inc(att_done, 1)

            def turned_out(turn_no):
                dve.wait_ge(att_turned, turn_no + 1)
                i = TT - 1 - turn_no
                nc.vector.tensor_copy(m.attT[:, :, i * P:(i + 1) * P], ps_t[:].rearrange("p (c q) -> p c q", c=HT)) \
                    .then_inc(attT_done, 1)

            dve.wait_ge(masked, 2)
            for n, (i, h) in enumerate(ITEMS):
                width = key_tiles(i) * P
                dve.wait_ge(score_mm, n + 1)
                if n >= 3:
                    dve.wait_ge(exp_done, n - 2)
                nc.vector.tensor_tensor(score[:, n % 3, 0:width], ps_s[:, n % 2, 0:width],
                                        bias[:, h, KEYS - width:KEYS], ALU.add).then_inc(score_out, 1)
                dve.wait_ge(score_out, n + 1)
                nc.vector.tensor_reduce(top[:, n:n + 1], score[:, n % 3, 0:width], AX_X, ALU.max) \
                    .then_inc(m.top_done, 1)
                dve.wait_ge(m.top_done, n + 1)
                nc.vector.tensor_scalar(ntop[:, n:n + 1], top[:, n:n + 1], -1.0, None, ALU.mult).then_inc(ntop_done, 1)
                if n % HEADS == 2 and n > HEADS:
                    head_out(n // HEADS - 1)
                if n % HEADS == 5 and n > HEADS:
                    turned_out(n // HEADS - 1)
            head_out(TT - 1)
            turned_out(TT - 1)


def gated_mix(nc, m, A, hT):
    with ExitStack() as mem:
        sem = m.sem
        S = 2
        place = [m.res[:, i, :] for i in range(TT)]
        ring = SplitRing(nc, m, mem, "gates_w", S, [KT, P], [place[s].rearrange("p (k c) -> p k c", k=KT) for s in range(S)])
        w_out = mem.enter_context(nc.sbuf_tensor("branches_w", [P, 2, S, HT, P], F32))
        gate = [place[2 + s] for s in range(S)]
        part = [place[4 + s] for s in range(S)]
        ps_g = mem.enter_context(nc.psum_tensor("gates_ps", [P, S, 2, BANK], F32))
        ps_y = mem.enter_context(nc.psum_tensor("branches_ps", [P, S, 2, BANK], F32))
        w_in = [[sem(f"branch_w_in{s}{odd}") for odd in range(2)] for s in range(S)]
        gate_out = [sem(f"gate_out{s}") for s in range(S)]
        branch_mm = [sem(f"branch_mm{s}") for s in range(S)]
        branch_out = [sem(f"branch_out{s}") for s in range(S)]
        mixed = sem("mixed")
        block = mem.enter_context(nc.Block())
        first_gate = 4 * ATT // P
        w2 = A["w_in_2"][0].rearrange("(k p) n -> p k n", p=P)
        outs = [A[n][0].rearrange("(k p) n -> p k n", p=P) for n in ("w_attn_out_2", "w_pool_out_2")]

        @block.sync
        def _(sp):
            def load(s, d, odd, first_gate_load, first_out_load):
                ring.load(sp, s, d, w2[:, :, bass.ds((d + (first_gate + s * KT)) * P, P)], first=first_gate_load)
                if not first_out_load:
                    sp.wait_ge(branch_mm[s], d - 1)
                sp.dma_start(w_out[:, odd, s, :, :], outs[s][:, :, bass.ds(d * P, P)]).then_inc(w_in[s][odd], 16)

            for d in range(2):
                for s in range(S):
                    load(s, d, d, d == 0, True)
            with sp.Fori(1, KT // 2) as i:
                for odd in range(2):
                    for s in range(S):
                        load(s, i * 2 + odd, odd, False, False)

        @block.tensor
        def _(pe):
            def feature_tile(d, odd, use, first=False):
                for s in range(S):
                    ring.arrived(pe, s, d)
                    if not first:
                        pe.wait_ge(gate_out[s], d)
                    for half in range(2):
                        cols = slice(half * BANK, (half + 1) * BANK)
                        for k in range(KT):
                            last = product(nc, ps_g[:, s, half, :], ring.parts(s, k), (hT[0][:, k, cols], hT[1][:, k, cols]),
                                           start=(k == 0), stop=(k == KT - 1))
                    last.then_inc(ring.used[s], 1)
                for s, data in enumerate((m.attT, m.poolT)):
                    pe.wait_ge(w_in[s][odd], (use + 1) * 16)
                    if not first:
                        pe.wait_ge(branch_out[s], d)
                    for half in range(2):
                        for k in range(HT):
                            last = nc.tensor.matmul(ps_y[:, s, half, :], w_out[:, odd, s, k, :],
                                                    data[:, k, half * BANK:(half + 1) * BANK],
                                                    start=(k == 0), stop=(k == HT - 1))
                    last.then_inc(branch_mm[s], 1)

            for d in range(2):
                feature_tile(d, d, 0, first=(d == 0))
            with pe.Fori(1, KT // 2) as i:
                for odd in range(2):
                    feature_tile(i * 2 + odd, odd, i)

        @block.scalar
        def _(act):
            at, _ = COLS["b_gate_2"]

            def sigmoid(d, first=False, last=False):
                for s in range(S):
                    act.wait_ge(ring.used[s], d + 1)
                    if not last:
                        ring.high(act, s, d + 1)
                    if not first:
                        act.wait_ge(branch_out[s], d)
                    nc.scalar.activation(gate[s].rearrange("p (h c) -> p h c", h=2), ps_g[:, s, :, :],
                                         ACT.Sigmoid, bias=m.params[:, bass.ds(d + (at + s * KT), 1)]) \
                        .then_inc(gate_out[s], 1)

            for s in range(S):
                ring.high(act, s, 0, first=True)
            sigmoid(0, first=True)
            with act.Fori(1, KT - 1) as d:
                sigmoid(d)
            sigmoid(KT - 1, last=True)

        @block.vector
        def _(dve):
            def mix(d, first=False, last=False):
                if not last:
                    for s in range(S):
                        ring.rest(dve, s, d + 1)
                for s in range(S):
                    dve.wait_ge(branch_mm[s], d + 1)
                    dve.wait_ge(gate_out[s], d + 1)
                    nc.vector.tensor_tensor(part[s].rearrange("p (h c) -> p h c", h=2),
                                            gate[s].rearrange("p (h c) -> p h c", h=2),
                                            ps_y[:, s, :, :], ALU.mult).then_inc(branch_out[s], 1)
                dve.wait_ge(branch_out[1], d + 1)
                nc.vector.tensor_tensor(m.mixT[:, bass.ds(d, 1), :].rearrange("p o c -> p (o c)"), part[0],
                                        part[1], ALU.add).then_inc(mixed, 1)
                dve.wait_ge(mixed, d + 1)

            for s in range(S):
                ring.rest(dve, s, 0)
            mix(0, first=True)
            with dve.Fori(1, KT - 1) as d:
                mix(d)
            mix(KT - 1, last=True)


class PostNorm:

    def __init__(self, nc, m, mem, name):
        def sb(part, shape):
            return mem.enter_context(nc.sbuf_tensor(f"{name}_{part}", shape, F32))

        self.squares = sb("squares", [P, D])
        self.sums = sb("sums", [P, TT])
        self.rms = sb("rms", [P, TT])
        self.rstd = sb("rstd", [P, TT])
        self.scaled = sb("scaled", [P, 2, D])
        self.gamma = sb("gamma", [P, D])
        self.gamma_in = m.sem(f"{name}_gamma_in")
        self.res_in = m.sem(f"{name}_res_in")
        self.squared = m.sem(f"{name}_squared")
        self.rms_done = m.sem(f"{name}_rms_done")
        self.rstd_done = m.sem(f"{name}_rstd_done")
        self.left_psum = m.sem(f"{name}_left_psum")
        self.added = m.sem(f"{name}_added")

    def scalar_part(self, nc, act, m, t, ps):
        if t:
            act.wait_ge(self.squared, t)
        nc.scalar.activation(self.squares[:].rearrange("p (h c) -> p h c", h=2), ps, ACT.Square,
                             accum_out=self.sums[:, t:t + 1]).then_inc(self.squared, 1)
        act.wait_ge(self.squared, t + 1)
        nc.scalar.activation(self.rms[:, t:t + 1], self.sums[:, t:t + 1], ACT.Sqrt, bias=m.eps[:], scale=1.0 / D) \
            .then_inc(self.rms_done, 1)

    def vector_part(self, nc, dve, m, t, ps):
        if t == 0:
            dve.wait_ge(self.gamma_in, 16)
            dve.wait_ge(self.res_in, 16)
        dve.wait_ge(self.rms_done, t + 1)
        nc.vector.reciprocal(self.rstd[:, t:t + 1], self.rms[:, t:t + 1]).then_inc(self.rstd_done, 1)
        dve.wait_ge(self.rstd_done, t + 1)
        nc.vector.scalar_tensor_tensor(out=self.scaled[:, t % 2, :].rearrange("p (h c) -> p h c", h=2), in0=ps,
                                       scalar=self.rstd[:, t:t + 1],
                                       in1=self.gamma[:].rearrange("p (h c) -> p h c", h=2),
                                       op0=ALU.mult, op1=ALU.mult).then_inc(self.left_psum, 1)
        dve.wait_ge(self.left_psum, t + 1)
        nc.vector.tensor_tensor(m.res[:, t, :], m.res[:, t, :], self.scaled[:, t % 2, :], ALU.add) \
            .then_inc(self.added, 1)


def mix_output(nc, m, A, raw):
    with ExitStack() as mem:
        norm = PostNorm(nc, m, mem, "mix_post")
        ps = mem.enter_context(nc.psum_tensor("w_o_ps", [P, 4, 2, BANK], F32))
        wide = WideProduct(nc, m, mem, "w_o", m.mixT, A["w_o_2"][0], raw, ps)
        block = mem.enter_context(nc.Block())

        @block.sync
        def _(sp):
            wide.load(sp)
            sp.dma_start(norm.gamma[:], A["norm_mix_post_2"].to_broadcast([P, D])).then_inc(norm.gamma_in, 16)
            sp.dma_start(m.res[:], m.res_dram.rearrange("(t p) d -> p t d", p=P)).then_inc(norm.res_in, 16)

        @block.tensor
        def _(pe):
            for t in range(TT):
                wide.tile_product(pe, t, norm.left_psum, t - 3)

        @block.scalar
        def _(act):
            wide.tile_high(act, 0)
            for k in range(KT):
                wide.weight_high(act, k)
            wide.tile_high(act, 1)
            for t in range(TT):
                act.wait_ge(wide.done, t + 1)
                if t + 2 < TT:
                    wide.tile_high(act, t + 2)
                norm.scalar_part(nc, act, m, t, ps[:, t % 4, :, :])

        @block.vector
        def _(dve):
            wide.tile_rest(dve, 0)
            for k in range(KT):
                wide.weight_rest(dve, k)
            wide.tile_rest(dve, 1)
            for t in range(TT):
                if t + 2 < TT:
                    wide.tile_rest(dve, t + 2)
                norm.vector_part(nc, dve, m, t, ps[:, t % 4, :, :])


def ffn_up_ring(nc, m, mem, A):
    ring = SplitRing(nc, m, mem, "w_up_2", 2, [KT, P], [m.res[:, s, :].rearrange("p (k c) -> p k c", k=KT) for s in range(2)])
    weights = A["w_up_2"][0].rearrange("(k p) n -> p k n", p=P)
    return ring, [weights[:, :, s * D_FF:s * D_FF + P] for s in range(2)]


def ffn_up(nc, m, A, hT, prodT, ring):
    with ExitStack() as mem:
        sem = m.sem
        S = 2
        gates = m.res[:, S:2 * S, :]
        ps = mem.enter_context(nc.psum_tensor("up_ps", [P, 2, S, 2, BANK], F32))
        centre = [sem(f"ffn_centre{s}") for s in range(S)]
        near = [sem(f"ffn_near_tap{s}") for s in range(S)]
        far = [sem(f"ffn_far_tap{s}") for s in range(S)]
        gelu = sem("ffn_gelu")
        prod = sem("ffn_prod")
        block = mem.enter_context(nc.Block())
        taps_at, bias_at = COLS["conv_w_2"][0], COLS["conv_b_2"][0]
        weights = A["w_up_2"][0].rearrange("(k p) n -> p k n", p=P)

        def tile_of(f, odd, s):
            return gates[:, odd, :] if s else prodT[:, bass.ds(f, 1), :].rearrange("p o c -> p (o c)")

        @block.sync
        def _(sp):
            with sp.Fori(1, FT) as f:
                for s in range(S):
                    ring.load(sp, s, f, weights[:, :, bass.ds((f + s * FT) * P, P)])

        @block.tensor
        def _(pe):
            def tile(f, odd, first=False):
                for s in range(S):
                    ring.arrived(pe, s, f)
                    if not first:
                        pe.wait_ge(far[s], f - 1)
                    for half in range(2):
                        cols = slice(half * BANK, (half + 1) * BANK)
                        for k in range(KT):
                            last = product(nc, ps[:, odd, s, half, :], ring.parts(s, k),
                                           (hT[0][:, k, cols], hT[1][:, k, cols]), start=(k == 0), stop=(k == KT - 1))
                    last.then_inc(ring.used[s], 1)

            for f in range(2):
                tile(f, f, first=True)
            with pe.Fori(1, FT // 2) as i:
                for odd in range(2):
                    tile(i * 2 + odd, odd)

        @block.scalar
        def _(act):
            def tile(f, odd, first=False, last=False):
                for s in range(S):
                    act.wait_ge(ring.used[s], f + 1)
                    if not last:
                        ring.high(act, s, f + 1)
                    if s and not first:
                        act.wait_ge(prod, f - 1)
                    nc.scalar.activation(tile_of(f, odd, s).rearrange("p (h c) -> p h c", h=2), ps[:, odd, s, :, :],
                                         ACT.Identity, bias=m.params[:, bass.ds(f + (bias_at + s * FT), 1)],
                                         scale=m.params[:, bass.ds(f + (taps_at + (4 + s) * FT), 1)]) \
                        .then_inc(centre[s], 1)
                act.wait_ge(far[1], f + 1)
                nc.scalar.activation(gates[:, odd, :], gates[:, odd, :], ACT.Gelu_apprx_tanh).then_inc(gelu, 1)

            for f in range(2):
                tile(f, f, first=True)
            with act.Fori(1, FT // 2 - 1) as i:
                for odd in range(2):
                    tile(i * 2 + odd, odd)
            tile(FT - 2, 0)
            tile(FT - 1, 1, last=True)

        @block.vector
        def _(dve):
            def tile(f, odd, last=False):
                for s in range(S):
                    if not last:
                        ring.rest(dve, s, f + 1)
                    dve.wait_ge(centre[s], f + 1)
                    raw = ps[:, odd, s, :, :].rearrange("p h c -> p (h c)")
                    for back, done in ((1, near), (2, far)):
                        if back == 2:
                            dve.wait_ge(near[s], f + 1)
                        into = tile_of(f, odd, s)[:, back:SEQ]
                        nc.vector.scalar_tensor_tensor(
                            out=into, in0=raw[:, 0:SEQ - back],
                            scalar=m.params[:, bass.ds(f + (taps_at + (2 * (2 - back) + s) * FT), 1)],
                            in1=into, op0=ALU.mult, op1=ALU.add).then_inc(done[s], 1)
                dve.wait_ge(gelu, f + 1)
                value = tile_of(f, odd, 0)
                nc.vector.tensor_tensor(value, value, gates[:, odd, :], ALU.mult).then_inc(prod, 1)

            with dve.Fori(0, FT // 2 - 1) as i:
                for odd in range(2):
                    tile(i * 2 + odd, odd)
            tile(FT - 2, 0)
            tile(FT - 1, 1, last=True)


def ffn_down(nc, m, A, prodT):
    with ExitStack() as mem:
        sem = m.sem
        S = 3
        QUAD = 4
        N = 2 * FT
        raw = mem.enter_context(nc.sbuf_tensor("w_down_raw", [P, S, D], F32))
        ring = SplitRing(nc, m, mem, "w_down_2", S, [D], [raw[:, s, :] for s in range(S)])
        x_high = mem.enter_context(nc.sbuf_tensor("prod_high", [P, S, QUAD * P], F32R))
        x_rest = mem.enter_context(nc.sbuf_tensor("prod_rest", [P, S, QUAD * P], F32R))
        norm = PostNorm(nc, m, mem, "ffn_post")
        ps = mem.enter_context(nc.psum_tensor("down_ps", [P, QUAD, 2, BANK], F32))
        x_high_done = sem("prod_high_done")
        x_rest_done = sem("prod_rest_done")
        tile_mm = sem("down_tile_mm")
        stored = sem("stored")
        block = mem.enter_context(nc.Block())

        def hidden(n):
            return prodT[:, n % FT, n // FT * QUAD * P:(n // FT + 1) * QUAD * P]

        @block.sync
        def _(sp):
            for n in range(N):
                f = n % FT
                ring.load(sp, n % S, n // S, A["w_down_2"][0, f * P:(f + 1) * P, :], first=(n < S))
                if n == S:
                    sp.dma_start(norm.gamma[:], A["norm_ffn_post_2"].to_broadcast([P, D])).then_inc(norm.gamma_in, 16)
                    sp.dma_start(m.res[:], m.res_dram.rearrange("(t p) d -> p t d", p=P)).then_inc(norm.res_in, 16)
            for t in range(TT):
                sp.wait_ge(norm.added, t + 1)
                sp.dma_start(A["out"][0, t * P:(t + 1) * P, :], m.res[:, t, :]).then_inc(stored, 16)
            sp.wait_ge(stored, 16 * TT)

        @block.tensor
        def _(pe):
            def ready(n):
                ring.arrived(pe, n % S, n // S)
                pe.wait_ge(x_rest_done, n + 1)

            def products(n, q):
                turn, f, s = n // FT, n % FT, n % S
                if turn and f == 0:
                    pe.wait_ge(norm.left_psum, q + 1)
                here = slice(q * P, (q + 1) * P)
                for half in range(2):
                    last = product(nc, ps[:, q, half, :], (x_high[:, s, here], x_rest[:, s, here]),
                                   ring.parts(s, slice(half * BANK, (half + 1) * BANK)),
                                   start=(f == 0), stop=(f == FT - 1))
                if q == QUAD - 1:
                    last.then_inc(ring.used[s], 1)
                elif f == FT - 1:
                    last.then_inc(tile_mm, 1)

            for n in range(N - S):
                ready(n)
                for q in range(QUAD):
                    products(n, q)
            for q in range(QUAD):
                for n in range(N - S, N):
                    if q == 0:
                        ready(n)
                    products(n, q)

        def tile_done(engine, t):
            turn, q = t // QUAD, t % QUAD
            if q < QUAD - 1:
                engine.wait_ge(tile_mm, turn * (QUAD - 1) + q + 1)
            else:
                n = (turn + 1) * FT - 1
                engine.wait_ge(ring.used[n % S], n // S + 1)

        @block.scalar
        def _(act):
            for n in range(N):
                if n >= S:
                    act.wait_ge(ring.used[n % S], n // S)
                nc.scalar.activation(x_high[:, n % S, :], hidden(n), ACT.Copy).then_inc(x_high_done, 1)
                ring.high(act, n % S, n // S, first=(n < S))
                if n == FT + S - 1:
                    for t in range(QUAD):
                        tile_done(act, t)
                        norm.scalar_part(nc, act, m, t, ps[:, t, :, :])
            for t in range(QUAD, TT):
                tile_done(act, t)
                norm.scalar_part(nc, act, m, t, ps[:, t % QUAD, :, :])

        @block.vector
        def _(dve):
            for n in range(N):
                dve.wait_ge(x_high_done, n + 1)
                nc.vector.tensor_tensor(x_rest[:, n % S, :], hidden(n), x_high[:, n % S, :].bitcast(F32), ALU.subtract) \
                    .then_inc(x_rest_done, 1)
                ring.rest(dve, n % S, n // S)
                if n == FT + S - 1:
                    for t in range(QUAD):
                        norm.vector_part(nc, dve, m, t, ps[:, t, :, :])
            for t in range(QUAD, TT):
                norm.vector_part(nc, dve, m, t, ps[:, t % QUAD, :, :])


def second_block(nc, m, A):
    m.res_dram = nc.dram_tensor("residual", (SEQ, D), F32).ap()
    m.bias_rows = nc.dram_tensor("bias_rows", (HEADS, P, EXT), F32).ap()
    m.bias_copied = m.sem("bias_copied")
    with ExitStack() as mem:
        m.mixT = mem.enter_context(nc.sbuf_tensor("mixT2", [P, KT, SEQ], F32))
        with ExitStack() as mem2:
            def sb(name, shape, dt=F32):
                return mem2.enter_context(nc.sbuf_tensor(name, shape, dt))

            m.attT = sb("attT", [P, HT, SEQ])
            m.poolT = sb("poolT", [P, HT, SEQ])
            hT = sb("hT3_high", [P, KT, SEQ], F32R), sb("hT3_rest", [P, KT, SEQ], F32R)
            m.qT = m.mixT[:, 0:HT, :]
            m.kT = m.mixT[:, HT:2 * HT, :]
            with nc.sbuf_tensor("v", [P, TT, ATT], F32) as m.v:
                with ExitStack() as mem3:
                    ring = qkvu_ring(nc, m, mem3)
                    sources = [A["w_in_2"][0].rearrange("(k p) n -> p k n", p=P)[:, :, at:at + P]
                               for at in (3 * ATT, 3 * ATT + P)]

                    def copy_bias(sp):
                        sp.dma_start(m.bias_rows, A["rel_ext"].unsqueeze(1).to_broadcast([HEADS, P, EXT])) \
                            .then_inc(m.bias_copied, 16)

                    norm_to_T(nc, m, "norm3", hT, gamma="norm_mix_pre_2", res_out=m.res_dram, scratch=m.mixT[:, 0:5, :],
                              next_ring=(ring, sources), loads_after=copy_bias)
                    project_second(nc, m, A, hT, ring)
                band_attention(nc, m, A)
            gated_mix(nc, m, A, hT)
        with nc.sbuf_tensor("w_o_raw", [P, 2, D], F32) as raw:
            mix_output(nc, m, A, [raw[:, i, :] for i in range(2)])
    with nc.sbuf_tensor("prodT", [P, FT, SEQ], F32) as prodT:
        with nc.sbuf_tensor("hT4_high", [P, KT, SEQ], F32R) as high, nc.sbuf_tensor("hT4_rest", [P, KT, SEQ], F32R) as rest, \
                ExitStack() as mem:
            ring, sources = ffn_up_ring(nc, m, mem, A)
            norm_to_T(nc, m, "norm4", (high, rest), gamma="norm_ffn_pre_2", res_out=m.res_dram,
                      scratch=prodT[:, 0:5, :], next_ring=(ring, sources))
            ffn_up(nc, m, A, (high, rest), prodT, ring)
        ffn_down(nc, m, A, prodT)


def build_program(nc, A):
    with ExitStack() as ctx:
        m = Shared(nc, ctx)
        with m.section(nc):
            first_mixer(nc, m, A)
        with m.section(nc):
            mixture(nc, m, A)
        with m.section(nc):
            second_block(nc, m, A)


class Shared:

    def __init__(self, nc, ctx):
        def sb(name, shape, dt=F32):
            return ctx.enter_context(nc.sbuf_tensor(name, shape, dt))

        self.sem = nc.alloc_semaphore
        self.params = sb("params", [P, N_COLS])
        self.ident = sb("ident", [P, P])
        self.ones = sb("ones", [P, P])
        self.inv_size = sb("inv_size", [P, HT])
        self.eps = sb("eps", [P, 1])
        self.res = sb("res", [P, TT, D])
        self.eps_set = self.sem("eps_set")
        self.y_dram = nc.dram_tensor("expert_rows", (ROWS, D), F32).ap()
        self.top_done = self.sem("top_done")
        self.x_in = self.sem("x_in")
        self.consts_set = self.sem("consts_set")

    @contextmanager
    def section(self, nc):
        whole, made = self.sem, []

        def sem(name):
            made.append(nc.alloc_semaphore(name))
            return made[-1]

        self.sem = sem
        yield
        self.sem = whole
        nc.clear_and_free_semaphores(made)
        nc.all_engine_barrier()


def _tables():
    j = np.arange(SEQ, dtype=np.float64)
    split = np.concatenate([j[0::2], j[1::2]])
    half = np.arange(HALF, dtype=np.float64) + 0.5
    angle = np.pi / SEQ * np.outer(split, half)
    trig = np.stack([np.cos(angle[:HALF]), np.cos(angle[HALF:]), np.sin(angle[:HALF]), np.sin(angle[HALF:])])
    back = trig.reshape(2, 2, HALF, HALF).transpose(1, 0, 3, 2) / SEQ
    whole = 2 * np.pi / SEQ * np.outer(split, np.arange(HALF, dtype=np.float64))
    scale = 1.0 / np.sqrt(SEQ * HEAD)
    dft = np.stack([np.cos(whole[:HALF]), -np.sin(whole[:HALF]), np.cos(whole[HALF:]), -np.sin(whole[HALF:])]) * scale
    d = np.arange(HEAD, dtype=np.float64)
    small = 2 * np.pi / HEAD * np.outer(d, d)
    pair = np.zeros((P, 2, P))
    for i in range(P // HEAD):
        s = slice(i * HEAD, (i + 1) * HEAD)
        pair[s, 0, s] = np.cos(small)
        pair[s, 1, s] = np.sin(small)
    in_head = (np.arange(D)[:, None] // HEAD == np.arange(D // HEAD)).reshape(KT, P, D // HEAD)
    t = np.linspace(0.0, 1.0, SEQ, dtype=np.float32)
    w = np.float32(2.0 * np.pi / SEQ) * np.arange(SEQ, dtype=np.float32)
    f = np.linspace(1e-4, F_BANDS - 1, F_BANDS, dtype=np.float32)
    fw = (f[:, None] * w[None, :]).astype(np.float32)
    positions = np.concatenate([t[None, :], np.cos(fw), -np.sin(fw)])
    rates = np.abs(np.linspace(np.log(1e-2) / 1.5, np.log(1e-2) / 0.3, D_HYENA))
    decay = np.exp(-t[split.astype(np.int64)][:, None].astype(np.float64) * rates[None, :])
    count = np.minimum(np.arange(max(WINDOWS))[None, :] + 1, np.array(WINDOWS)[:, None])
    edge = np.broadcast_to(np.array(WINDOWS)[:, None] / count, (P, len(WINDOWS), max(WINDOWS)))
    before = np.triu(np.ones((P, P)), 1)
    out = dict(half_tables=trig, back_tables=back, dft_tables=dft, pair_table=pair, head_pick=in_head.transpose(1, 0, 2) / HEAD,
               head_spread=in_head.transpose(2, 0, 1),
               positions=positions, decay=decay, pool_edge=edge, before=before,
               index_rows=np.stack([np.arange(EXPERTS) - 64, np.arange(EXPERTS)])[None],
               count_row=np.arange(CAP)[None, :], token_ids=np.arange(SEQ).reshape(TT, P).T,
               limits=CAP * np.arange(1, FULL_BLOCKS)[None, :])
    return {k: np.ascontiguousarray(v, dtype=np.float32) for k, v in out.items()}


def _laid_out(inputs):
    a = {k: np.asarray(v) for k, v in inputs.items()}
    out = _tables()
    for name in ("x", "w_in", "f_w_in", "f_w_mid", "f_w_out", "w_out", "norm2_g", "w_gate", "w_up", "w_down",
                 "w_in_2", "w_attn_out_2", "w_pool_group_2", "w_pool_out_2", "w_o_2", "norm_mix_post_2",
                 "w_up_2", "w_down_2", "norm_ffn_post_2"):
        out[name] = a[name]
    out["final_g"] = a["final_g"].reshape(1, D)

    def cols(v):
        return v.reshape(-1, P).T

    def twice(v):
        return np.concatenate([v.T, v.T])

    packed = {n: cols(a[n]) for n in COLS if n in a and n not in ("conv_w", "conv_w_2", "f_freq")}
    for n in ("conv_w", "conv_w_2"):
        packed[n] = a[n].reshape(3 * a[n].shape[2] // P, P).T
    packed["f_b"] = twice(np.concatenate([a["f_b_in"], a["f_b_mid"][0]]))
    packed["f_freq"] = twice(a["f_freq"][0])
    out["params"] = np.concatenate([packed[n] for n in COLS], axis=1)
    assert out["params"].shape == (P, N_COLS)
    out["w_router"] = np.concatenate([a["w_group"][0]] + [a["w_router"][0, g] for g in range(GROUPS)], axis=1)
    out["b_router"] = np.concatenate([a["b_group"][0], a["b_router"][0].reshape(-1)])[None, :]
    dist = np.clip(np.arange(EXT)[::-1] - (P - 1), -REL, REL) + REL
    out["rel_ext"] = a["rel_bias_2"][0][:, dist]
    return {k: np.ascontiguousarray(v) for k, v in out.items()}


def kernel(**inputs):
    import concourse.bacc as bacc
    from concourse.bass_utils import run_bass_kernel_spmd

    nc = bacc.Bacc("TRN2", target_bir_lowering=False, num_devices=1)
    arrays, A = {}, {}
    for name, a in _laid_out(inputs).items():
        arrays[f"in_{name}_dram"] = a
        A[name] = nc.dram_tensor(f"in_{name}_dram", a.shape, mybir.dt.from_np(a.dtype), kind="ExternalInput").ap()
    A["out"] = nc.dram_tensor("out_0_dram", (1, SEQ, D), F32, kind="ExternalOutput").ap()
    build_program(nc, A)
    r = run_bass_kernel_spmd(nc, [arrays], core_ids=[0])
    return r.results[0]["out_0_dram"]
```
